# Optimizing a Trainium2 kernel written in Bass

```python
import jax, jax.numpy as jnp
from jax import lax
import numpy as np

D_MODEL = 1024
BATCH = 1
SEQ = 1024
DEPTH = 2
DEC_BATCH = 8
DEC_SEQ = 1
PAST_LEN = 1024
PAGE_SIZE = 128

N_A_LAYERS = DEPTH // 2
N_B_LAYERS = DEPTH - N_A_LAYERS
A_HEADS = 8
A_DK = D_MODEL // A_HEADS
A_DV = D_MODEL // A_HEADS
A_WIDTH = A_HEADS * A_DV
A_CHUNK = 64
B_HEADS = 16
B_DH = D_MODEL // B_HEADS
B_WIDTH = B_HEADS * B_DH
Q_BLOCK = 128
RMS_EPS = 1e-6
FGATE_BIAS_INIT = 3.0

kernel_name = 'yoco_hgrn2_fox_decoder_step'

def rms_norm(x, gain):
    xf = x.astype(jnp.float32)
    xf = xf * lax.rsqrt(jnp.mean(xf * xf, axis=-1, keepdims=True) + RMS_EPS)
    return (xf * gain.astype(jnp.float32)).astype(x.dtype)

def hgrn_lower_bounds(lb_logits):
    p = jax.nn.softmax(lb_logits.astype(jnp.float32), axis=0)
    c = jnp.cumsum(p, axis=0)
    return c - c[:1]

def gated_recurrence(q, k, v, logf, s0, chunk):
    bsz, t, h, _ = q.shape
    n = t // chunk

    def to_chunks(a):
        return a.reshape(bsz, n, chunk, h, a.shape[-1]).transpose(1, 0, 3, 2, 4)

    causal = jnp.tril(jnp.ones((chunk, chunk), dtype=bool))[:, :, None]

    def step(s, inp):
        qc, kc, vc, gc = inp
        cum = jnp.cumsum(gc, axis=2)
        o_inter = jnp.einsum('bhtk,bhkv->bhtv', qc * jnp.exp(cum), s)
        diff = cum[:, :, :, None, :] - cum[:, :, None, :, :]
        decay = jnp.exp(jnp.where(causal, diff, -jnp.inf))
        att = jnp.einsum('bhtk,bhsk,bhtsk->bhts', qc, kc, decay)
        o = o_inter + jnp.einsum('bhts,bhsv->bhtv', att, vc)
        last = cum[:, :, -1:, :]
        s_new = jnp.exp(last[:, :, 0, :])[..., None] * s + jnp.einsum(
            'bhsk,bhsv->bhkv', kc * jnp.exp(last - cum), vc)
        return s_new, o

    s_t, o = lax.scan(step, s0, (to_chunks(q), to_chunks(k), to_chunks(v), to_chunks(logf)))
    return o.transpose(1, 0, 3, 2, 4).reshape(bsz, t, h, -1), s_t

def hgrn_layer(x, s0, norm_g, w_in, g_norm, w_o, lb):
    bsz, t, _ = x.shape
    chunk = A_CHUNK if t % A_CHUNK == 0 else t
    hk = A_HEADS * A_DK
    proj = rms_norm(x, norm_g) @ w_in
    q, fz, i, gate = jnp.split(proj, [hk, 2 * hk, 2 * hk + A_WIDTH], axis=-1)
    heads_k = (bsz, t, A_HEADS, A_DK)
    q = jax.nn.silu(q.astype(jnp.float32)).reshape(heads_k)
    fz = fz.astype(jnp.float32).reshape(heads_k)
    lb = lb.reshape(A_HEADS, A_DK)
    logf = jnp.logaddexp(jnp.log(lb), jnp.log1p(-lb) + jax.nn.log_sigmoid(fz))
    k = (1.0 - lb) * jax.nn.sigmoid(-fz)
    v = i.astype(jnp.float32).reshape(bsz, t, A_HEADS, A_DV)
    o, s_t = gated_recurrence(q, k, v, logf, s0.astype(jnp.float32), chunk)
    o = rms_norm(o, g_norm).reshape(bsz, t, A_WIDTH).astype(x.dtype) * jax.nn.silu(gate)
    return x + o @ w_o, s_t.astype(s0.dtype)

def shared_kv(h, norm_kv, w_kv, k_norm, w_fgate, b_fgate):
    bsz, t, _ = h.shape
    u = rms_norm(h, norm_kv)
    k, v = jnp.split(u @ w_kv, 2, axis=-1)
    k = rms_norm(k.reshape(bsz, t, B_HEADS, B_DH), k_norm)
    v = v.reshape(bsz, t, B_HEADS, B_DH)
    logf = jax.nn.log_sigmoid((u @ w_fgate + b_fgate).astype(jnp.float32))
    return k, v, logf

def forgetting_attention(q, k_all, v_all, c_all):
    bsz, tq = q.shape[:2]
    length = k_all.shape[1]
    q_start = length - tq
    q_block = Q_BLOCK if tq % Q_BLOCK == 0 else tq
    n_blk = tq // q_block
    c_t = jnp.transpose(c_all, (0, 2, 1))
    key_pos = jnp.arange(length)
    scale = B_DH ** -0.5
    qb = q.reshape(bsz, n_blk, q_block, B_HEADS, B_DH).transpose(1, 0, 2, 3, 4)
    starts = q_start + jnp.arange(n_blk) * q_block

    def one_block(args):
        qi, start = args
        s = jnp.einsum('bqhd,bkhd->bhqk', qi, k_all).astype(jnp.float32) * scale
        c_q = lax.dynamic_slice_in_dim(c_t, start, q_block, axis=2)
        q_pos = start + jnp.arange(q_block)
        mask = key_pos[None, :] <= q_pos[:, None]
        logits = jnp.where(mask, s + (c_q[..., :, None] - c_t[..., None, :]), -jnp.inf)
        p = jax.nn.softmax(logits, axis=-1)
        return jnp.einsum('bhqk,bkhd->bqhd', p.astype(v_all.dtype), v_all)

    out = lax.map(one_block, (qb, starts))
    return out.transpose(1, 0, 2, 3, 4).reshape(bsz, tq, B_HEADS, B_DH)

def fox_layer(x, norm_g, w_in, q_norm, w_o, k_all, v_all, c_all):
    bsz, t, _ = x.shape
    q, gate = jnp.split(rms_norm(x, norm_g) @ w_in, 2, axis=-1)
    q = rms_norm(q.reshape(bsz, t, B_HEADS, B_DH), q_norm)
    o = forgetting_attention(q, k_all, v_all, c_all)
    o = o.reshape(bsz, t, B_WIDTH).astype(x.dtype) * jax.nn.silu(gate)
    return x + o @ w_o

def trunk(x, s0, past_k, past_v, past_logf, norm_in, w_in_a, g_norm_a, w_o_a, lbs,
          norm_kv, w_kv, k_norm, w_fgate, b_fgate, w_in_b, q_norm_b, w_o_b):
    h = x
    new_s = []
    for layer in range(DEPTH):
        if layer < N_A_LAYERS:
            h, s = hgrn_layer(h, s0[layer], norm_in[layer], w_in_a[layer], g_norm_a[layer],
                              w_o_a[layer], lbs[layer])
            new_s.append(s)
            if layer == N_A_LAYERS - 1:
                k_new, v_new, lf_new = shared_kv(h, norm_kv, w_kv, k_norm, w_fgate, b_fgate)
                k_new = k_new.astype(past_k.dtype)
                v_new = v_new.astype(past_v.dtype)
                k_all = jnp.concatenate([past_k, k_new], axis=1)
                v_all = jnp.concatenate([past_v, v_new], axis=1)
                c_all = jnp.cumsum(jnp.concatenate(
                    [past_logf.astype(jnp.float32), lf_new], axis=1), axis=1)
                lf_new = lf_new.astype(past_logf.dtype)
        else:
            j = layer - N_A_LAYERS
            h = fox_layer(h, norm_in[layer], w_in_b[j], q_norm_b[j], w_o_b[j], k_all, v_all, c_all)
    return h, jnp.stack(new_s), k_new, v_new, lf_new

def setup_inputs(seed: int = 0) -> dict:
    key = jax.random.key(seed)
    ks = jax.random.split(key, 20)
    f32 = jnp.float32
    n_pages = PAST_LEN // PAGE_SIZE
    n_used = DEC_BATCH * n_pages
    n_pool = n_used + (n_used + 3) // 4
    d_scale = D_MODEL ** -0.5

    def normal(k, shape):
        return jax.random.normal(k, shape, f32)

    def gain(k, shape):
        return 1.0 + 0.02 * normal(k, shape)

    page_table = jax.random.permutation(ks[0], n_pool)[:n_used].reshape(
        DEC_BATCH, n_pages).astype(jnp.int32)
    return {
        'x_prompt': normal(ks[1], (BATCH, SEQ, D_MODEL)),
        'x_sample': normal(ks[2], (DEC_BATCH, DEC_SEQ, D_MODEL)),
        'state_hgrn': 0.3 * normal(ks[3], (N_A_LAYERS, DEC_BATCH, A_HEADS, A_DK, A_DV)),
        'cache_k': normal(ks[4], (n_pool, PAGE_SIZE, B_HEADS, B_DH)),
        'cache_v': normal(ks[5], (n_pool, PAGE_SIZE, B_HEADS, B_DH)),
        'cache_logf': jax.nn.log_sigmoid(FGATE_BIAS_INIT + 0.5 * normal(ks[6], (n_pool, PAGE_SIZE, B_HEADS))),
        'page_table': page_table,
        'norm_in': gain(ks[7], (DEPTH, D_MODEL)),
        'w_in_a': d_scale * normal(ks[8], (N_A_LAYERS, D_MODEL, 2 * A_HEADS * A_DK + 2 * A_WIDTH)),
        'lb_logits': 0.5 * normal(ks[9], (N_A_LAYERS, A_HEADS * A_DK)),
        'g_norm_a': gain(ks[10], (N_A_LAYERS, A_DV)),
        'w_o_a': A_WIDTH ** -0.5 * normal(ks[11], (N_A_LAYERS, A_WIDTH, D_MODEL)),
        'norm_kv': gain(ks[12], (D_MODEL,)),
        'w_kv': d_scale * normal(ks[13], (D_MODEL, 2 * B_WIDTH)),
        'k_norm': gain(ks[14], (B_DH,)),
        'w_fgate': 0.5 * d_scale * normal(ks[15], (D_MODEL, B_HEADS)),
        'b_fgate': FGATE_BIAS_INIT + 0.1 * normal(ks[16], (B_HEADS,)),
        'w_in_b': d_scale * normal(ks[17], (N_B_LAYERS, D_MODEL, 2 * B_WIDTH)),
        'q_norm_b': gain(ks[18], (N_B_LAYERS, B_DH)),
        'w_o_b': B_WIDTH ** -0.5 * normal(ks[19], (N_B_LAYERS, B_WIDTH, D_MODEL)),
    }

def reference(x_prompt, x_sample, state_hgrn, cache_k, cache_v, cache_logf, page_table,
              norm_in, w_in_a, lb_logits, g_norm_a, w_o_a,
              norm_kv, w_kv, k_norm, w_fgate, b_fgate,
              w_in_b, q_norm_b, w_o_b):
    lbs = hgrn_lower_bounds(lb_logits)
    bp = x_prompt.shape[0]
    zero_state = jnp.zeros((N_A_LAYERS, bp, A_HEADS, A_DK, A_DV), state_hgrn.dtype)
    empty_k = jnp.zeros((bp, 0, B_HEADS, B_DH), cache_k.dtype)
    empty_v = jnp.zeros((bp, 0, B_HEADS, B_DH), cache_v.dtype)
    empty_lf = jnp.zeros((bp, 0, B_HEADS), cache_logf.dtype)
    y_prompt, s_prompt, k_prompt, v_prompt, lf_prompt = trunk(
        x_prompt, zero_state, empty_k, empty_v, empty_lf, norm_in, w_in_a, g_norm_a, w_o_a, lbs,
        norm_kv, w_kv, k_norm, w_fgate, b_fgate, w_in_b, q_norm_b, w_o_b)
    db, n_pages = page_table.shape
    past_len = n_pages * PAGE_SIZE
    past_k = cache_k[page_table].reshape(db, past_len, B_HEADS, B_DH)
    past_v = cache_v[page_table].reshape(db, past_len, B_HEADS, B_DH)
    past_lf = cache_logf[page_table].reshape(db, past_len, B_HEADS)
    y_sample, s_sample, k_sample, v_sample, lf_sample = trunk(
        x_sample, state_hgrn, past_k, past_v, past_lf, norm_in, w_in_a, g_norm_a, w_o_a, lbs,
        norm_kv, w_kv, k_norm, w_fgate, b_fgate, w_in_b, q_norm_b, w_o_b)
    return (y_prompt, y_sample, s_prompt, s_sample, k_prompt, k_sample, v_prompt, v_sample, lf_prompt, lf_sample)


_drawn_inputs = setup_inputs


def setup_inputs(seed=0):
    import zlib

    import numpy as np

    out = dict(_drawn_inputs(seed))
    spreads = {}
    factors = {'cache_logf': 29.313,
     'g_norm_a': 4.709,
     'norm_kv': 2.853,
     'k_norm': 2.925,
     'q_norm_b': 8.0}
    for name, (base, spread) in spreads.items():
        noise = np.random.default_rng([zlib.crc32(name.encode()), seed]).standard_normal(out[name].shape)
        drawn = base * np.exp(spread * noise) if base else spread * noise
        out[name] = __import__('jax').numpy.asarray(drawn.astype(out[name].dtype))
    for name, factor in factors.items():
        out[name] = (out[name] * factor).astype(out[name].dtype)
    return out
```

```python
from contextlib import ExitStack

import concourse.bass as bass
from concourse import mybir

F32 = mybir.dt.float32
BF16 = mybir.dt.bfloat16
I32 = mybir.dt.int32
ALU = mybir.AluOpType
ACT = mybir.ActivationFunctionType
AX = mybir.AxisListType

P = 128
EPS = 1e-6


class Steps:

    def __init__(self, eng, sem):
        self.eng, self.sem, self.start, self.base, self.n = eng, sem, 0, 0, 0

    def did(self, ins):
        ins.then_inc(self.sem, 1)
        self.n += 1
        return self.base + self.n

    def need(self, mark):
        self.eng.wait_ge(self.sem, mark)

    def chain(self, ins):
        self.need(self.did(ins))

    def enter(self, i, per):
        self.start = self.start + self.n
        self.base, self.n = self.start + i * per, 0

    def leave(self, per, times):
        assert self.n == per, (self.n, per)
        self.start, self.n = self.start + per * times, 0
        self.base = self.start

    def straight(self):
        self.start = self.start + self.n
        self.base, self.n = self.start, 0


class Marks:

    def __init__(self, sem, *names, ahead=0):
        self.sem, self.names, self.ahead = sem, names, ahead
        self.index = {n: i + 1 for i, n in enumerate(names)}
        assert len(self.index) == len(names)

    def at(self, name, r=0):
        return r * len(self.names) + self.index[name] + self.ahead


D = 1024
T = 1024
S = 8
N = T + S
KT = D // P
TT = T // P
W3 = N // 3
AH = 8
C = 64
NC = T // C
LEVELS = (32, 16, 8, 4, 2, 1)
BH = 16
DH = 64
PAIRS = BH // 2
PAGES = 8
PAGE = 128
RAW = 4 * (DH + 1) + 2 * P
HALF = S // 2
ITEMS = 2 * TT
LOW = -3e38
FOX_STEPS = range(56)


W_COL = (1, 0, 3, 2)
LAST = AH // 2 - 1


def build(nc, io):
    with ExitStack() as ctx:
        def sem(name):
            return ctx.enter_context(nc.semaphore(name))

        WORDS = 53200
        arena = ctx.enter_context(nc.sbuf_tensor("arena", [P, WORDS], F32))
        psum = ctx.enter_context(nc.psum_tensor("psum", [P, 8 * 512], F32))
        bank = [psum[:, 512 * i:512 * (i + 1)] for i in range(8)]
        used = [0]

        def area(words):
            at = used[0]
            used[0] += words
            assert used[0] <= WORDS, used[0]
            return arena[:, at:at + words]

        ident = area(P)
        ones_mean = area(P)
        level_mask = area(len(LEVELS) * C)
        chunk_keep = area(T // 2).bitcast(BF16)
        gain_a = area(KT)
        gain_o = area(1)
        lb_in, one_lb, inv_lb, inv_h = area(AH), area(AH), area(AH), area(1)
        eps = area(1)
        msq, rstd = area(TT + 1), area(TT + 1)
        lb_e, lb_r = area(AH), area(AH)

        x_t = area(KT * N).rearrange("p (k n) -> p k n", n=N)
        w_a_at = used[0]
        w_a = area(2 * KT * 4 * P).rearrange("p (s k y n) -> p s k y n", s=2, y=4, n=P)
        o_t = area(AH * N).rearrange("p (h n) -> p h n", n=N)
        temps = used[0]
        raw_f, raw_q, raw_g = area(N), area(N), area(N)
        t0, t1, t2, t3 = area(N), area(N), area(N), area(N)
        k_h, q_h, sg_h, logf, cum, q_dec = area(N), area(N), area(N), area(N), area(T), area(T)
        k_dec = logf[:, 0:T]
        diffs, facts = area(2 * T), area(2 * T)
        diff = [diffs[:, 0:T], diffs[:, T:2 * T]]
        fact = [facts[:, 0:T], facts[:, T:2 * T]]
        o_sq, o_rs = diffs[:, 0:N], facts[:, 0:N]
        att = area(T)
        v_tok = [area((TT + 1) * P).rearrange("p (t v) -> p t v", v=P) for _ in range(2)]
        k_dec_tok = area(T).rearrange("p (t k) -> p t k", k=P)
        s_all = area(NC * P).rearrange("p (c v) -> p c v", v=P)
        s_smp = area(S * P).rearrange("p (b v) -> p b v", v=P)
        v_diag = area(S * P).rearrange("p (b v) -> p b v", v=P)
        k_smp, o_smp, f_smp, dec = area(P), area(S), area(S), area(NC)
        sq_smp, rs_smp = area(S), area(S)
        x_in = [facts[:, 0:D], facts[:, T:T + D]]
        x_sq = [diffs[:, 0:D], diffs[:, T:T + D]]

        end_a = used[0]

        h_t = x_t
        w_o = arena[:, w_a_at:w_a_at + AH * D].rearrange("p (h n) -> p h n", n=D)
        used[0] = temps
        o_tile = [area(AH * P).rearrange("p (h n) -> p h n", n=P) for _ in range(2)]
        res, h_new, h_sc = [area(D), area(D)], [area(D), area(D)], [area(D), area(D)]
        h_sq = area(D)
        assert used[0] <= temps + 9 * 1024

        used[0] = temps
        raw = area((TT + 1) * RAW).rearrange("p (t c) -> p t c", c=RAW)
        kq_t = area(4 * T).rearrange("p (x n) -> p x n", n=T)
        ssq, rs_kq = area((TT + 1) * 4), area((TT + 1) * 4)
        top, total, r_total = area(16), area(16), area(16)
        expd = [area(HALF * 2 * 9) for _ in range(2)]
        top8, m_all, den, o_two, g_smp = [area(8), area(8)], [area(8), area(8)], area(8), area(8), area(S)
        assert used[0] <= temps + 9 * 1024
        used[0] = temps + 9 * 1024
        w_kv = area(KT * 2 * P).rearrange("p (k y n) -> p k y n", y=2, n=P)
        w_qg = area(KT * 2 * P).rearrange("p (k y n) -> p k y n", y=2, n=P)
        bias = area(S * BH * PAGES).rearrange("p (b h j) -> p b h j", h=BH, j=PAGES)
        gain_kq = area(4 * DH).rearrange("p (x d) -> p x d", d=DH)
        gain_kv, gain_b = area(KT), area(KT)
        lf_tok, c_tok = area((TT + 1) * BH), area(TT * BH)
        causal = area(P)
        pages = area(S * PAGES).bitcast(I32)
        after = used[0]
        v_cur = area((TT + 1) * P).rearrange("p (t v) -> p t v", v=P)
        g_cur = area((TT + 1) * P).rearrange("p (t v) -> p t v", v=P)
        pr_at = used[0]
        prob, prob_t = [area(T), area(T)], [area(T), area(T)]
        kq_sq = arena[:, pr_at:pr_at + (TT + 1) * 4 * DH].rearrange("p (t x d) -> p t x d", x=4, d=DH)
        q_all = area(S * P).rearrange("p (b n) -> p b n", n=P)
        prod = area(PAGES * P)
        og = area(TT * P).rearrange("p (t v) -> p t v", v=P)
        kv_new = area(2 * S * P)
        k_new = kv_new[0:1, 0:S * P].rearrange("p (b n) -> p b n", n=P)
        v_new = kv_new[0:1, S * P:2 * S * P].rearrange("p (b n) -> p b n", n=P)
        lgt = [area(HALF * 2 * 9) for _ in range(2)]
        assert used[0] <= WORDS, used[0]
        k_ring = arena[:, w_a_at:w_a_at + 4 * PAGES * P].rearrange("p (s j n) -> p s j n", s=4, n=P)
        v_ring = arena[:, w_a_at + 4 * PAGES * P:w_a_at + 8 * PAGES * P].rearrange("p (s j n) -> p s j n", s=4, n=P)
        used[0] = after
        w_f = area(KT * BH).rearrange("p (k n) -> p k n", n=BH)
        z16, a16, one16, c16, b_f = area(N), area(N), area(T), area(T), area(1)
        lf_pages = area(S * PAGES * BH)
        later, lf_new = area(P), area(S * BH)
        acc = area(S * BH).rearrange("p (b h) -> p b h", h=BH)
        assert used[0] <= WORDS, used[0]
        h_dram = nc.dram_tensor("h_rows", [N, D], F32).ap()
        q_dram = nc.dram_tensor("q_rows", [PAIRS, S, P], F32).ap()

        consts_in = sem("consts_in")
        built = Marks(sem("built"), "ident0", "ones", "masks0", "keep0", "eps", "vdiag0", "ident", "masks1", "keep", "masks")
        consts_v = sem("consts_v")
        x_loaded = [sem("x_loaded0"), sem("x_loaded1")]
        x_scaled, x_turned, x_ready = sem("x_scaled"), sem("x_turned"), sem("x_ready")
        x_rstd = sem("x_rstd")
        lb_a = sem("lb_a")
        w_a_loaded = [sem("w_a_loaded0"), sem("w_a_loaded1")]
        state_loaded, state_stored, prompt_stored = sem("state_loaded"), sem("state_stored"), sem("prompt_stored")
        s_all_free = sem("s_all_free")
        merge_go, pool_go, sp_go = sem("merge_go"), sem("pool_go"), sem("sp_go")
        raw_set, end_go_v = sem("raw_set"), sem("end_go_v")
        act_steps, dve_steps = sem("act_steps"), sem("dve_steps")
        proj_done = Marks(sem("proj_done"), *range(12))
        lv_done = Marks(sem("lv_done"), "diag0", "diag1", *[f"level{l}" for l in LEVELS], "mean0", "mean1")
        smp_done = Marks(sem("smp_done"), "k_smp", "o_smp", "mean_smp")
        uu_done = Marks(sem("uu_done"), "outer0", "outer1", "turn0", "turn1", "upd0", "upd1", "upd2", "upd3")
        ob_done = Marks(sem("ob_done"), "o0", "o1")
        proj_taken = Marks(sem("proj_taken"), *range(12))
        lv_taken_v, lv_taken_a = sem("lv_taken_v"), sem("lv_taken_a")
        uu_taken_v, uu_taken_a = sem("uu_taken_v"), sem("uu_taken_a")
        acts = Marks(sem("acts"), "ln_f", "ln_q", "ln_g", "k", "decays", "sig_q", "exp_cum", "sig_g", "exp32", "exp16",
                     "exp8", "exp4", "sq_smp", "exp_kd", "exp2", "ln_smp", "exp1", "sq0", "sq1", "dev")
        vecs = Marks(sem("vecs"), "abs_f", "abs_q", "abs_g", "logf", "k_in", "cum", "q_in", "diff32", "g_in", "q", "sg", "diff_kd",
                     "k_smp", "v_diag", "q_dec", "s_smp", "fact32", "diff16", "o_smp", "fact16", "diff8",
                     "fact8", "diff4", "fact4", "diff2", "k_dec", "fact2", "diff1", "fact1",
                     "att_all", "s_all", "o_all", ahead=1)
        w_o_loaded, res_loaded, h_stored = sem("w_o_loaded"), [sem("res_loaded0"), sem("res_loaded1")], [sem("h_stored0"), sem("h_stored1")]
        tile_v = Marks(sem("tile_v"), "o", "new0", "new1", "scaled")
        tile_a = Marks(sem("tile_a"), "rstd", "h_t0", "h_t1")
        y_done, h_turned = sem("y_done"), sem("h_turned")
        keys_in, pages_in, lf_in, lf_new_in = sem("keys_in"), sem("pages_in"), sem("lf_in"), sem("lf_new_in")
        lf_stored = sem("lf_stored")
        keys_p = Marks(sem("keys_p"), "z", "turned", "suffix")
        keys_v = Marks(sem("keys_v"), "w_f", "abs", "lf", "c", "tok", "done")
        keys_a = Marks(sem("keys_a"), "ln")
        masks_b = Marks(sem("masks_b"), "zero", "causal", "later", "raw", "low0", "low1", "causal1", "later1")
        w_kv_loaded, w_qg_loaded = sem("w_kv_loaded"), sem("w_qg_loaded")
        w_kv_scaled, w_qg_scaled = sem("w_kv_scaled"), sem("w_qg_scaled")
        pj_done, pj_taken = sem("pj_done"), sem("pj_taken")
        k_loaded, v_loaded = [sem(f"k_loaded{i}") for i in range(4)], [sem(f"v_loaded{i}") for i in range(4)]
        kv_stored, new_loaded, top_all = sem("kv_stored"), sem("new_loaded"), sem("top_all")
        order_p = [f"kq_t{t}" for t in range(TT)] + ["g_smp", "qk0"]
        order_v = ["ssq", "abs_g", "kq", "g_in"] + [f"kqc{t}" for t in range(0, TT, 2)] + ["g", "g_smp", "mx0"]
        order_a = ["sq", "v_cur", "rs", "ln_g"] + [f"kqc{t}" for t in range(1, TT, 2)] + ["sig_g", "ex0"]
        for w in range(ITEMS):
            order_p += [f"pt{w}_0"] + [f"pt{w}_1"] * (w % TT >= 4) + [f"qk{w + 1}"] * (w + 1 < ITEMS) + [f"pv{w}"]
            order_p += [f"dec{w // TT}"] * (w % TT == TT - 1)
            order_v += [f"od{w // TT - 1}"] * (w == TT)
            order_v += [f"ptc{w}"] + [f"mx{w + 1}"] * (w + 1 < ITEMS) + [f"nm{w}"]
            order_v += [f"pr{w // TT * HALF + w % TT - 1}"] * (1 <= w % TT <= HALF)
            order_v += [f"lg{w // TT}"] * (w % TT == HALF + 1) + [f"df{w // TT}"] * (w % TT == HALF + 2)
            order_a += [f"ptc{w}"] * (w % TT >= 4) + [f"ex{w + 1}"] * (w + 1 < ITEMS)
            order_a += [f"de{w // TT}"] * (w % TT == TT - 1)
        order_p += ["og0", "og1"]
        order_v += ["od1", "ogc0"]
        order_a += ["ogc1"]
        fp, fv, fa = Marks(sem("fox_p"), *order_p), Marks(sem("fox_v"), *order_v), Marks(sem("fox_a"), *order_a)
        w_ob_loaded, resb_loaded, y_stored = sem("w_ob_loaded"), [sem("resb_loaded0"), sem("resb_loaded1")], [sem("y_stored0"), sem("y_stored1")]
        yb_done, yb_v = sem("yb_done"), Marks(sem("yb_v"), "o", "y0", "y1")
        pe_go, end_go = sem("pe_go"), sem("end_go")

        block = ctx.enter_context(nc.Block())

        w_in_a = io["w_in_a"].rearrange("l (k p) (y h n) -> p k y (l h) n", p=P, y=4, n=P)
        x_prompt = io["x_prompt"].rearrange("b (t p) d -> (b t) p d", p=P)
        x_sample = io["x_sample"].rearrange("b s d -> (b s) d")
        state_in = io["state_hgrn"].rearrange("l b h k v -> (l h) k b v")
        state_out = io["state_sample"].rearrange("l b h k v -> (l h) k b v")
        prompt_out = io["state_prompt"].rearrange("l b h k v -> (l b h) k v")

        def cols(t):
            return slice(t * P, t * P + (P if t < TT else S))

        def load_w(sp, i, par):
            for y in range(4):
                sp.dma_start(w_a[:, par, :, y, :], w_in_a[:, :, W_COL[y], 2 * i + par, :]).then_inc(w_a_loaded[par], 16)

        w_kv_d = io["w_kv"].rearrange("(k p) (y h n) -> p k y h n", p=P, y=2, n=P)
        w_qg_d = io["w_in_b"].rearrange("l (k p) (y h n) -> p k y (l h) n", p=P, y=2, n=P)
        k_cache = io["cache_k"].rearrange("g s (x h) d -> g s x (h d)", h=2)
        v_cache = io["cache_v"].rearrange("g s (x h) d -> g s x (h d)", h=2)
        lf_cache = io["cache_logf"]
        n_pool = lf_cache.shape[0]

        def o_cols(p, j):
            if isinstance(p, int):
                return o_t[:, p, 512 * j:512 * j + 512]
            return o_t[:, bass.DynSlice(p, 1), 512 * j:512 * j + 512].rearrange("p a n -> p (a n)")

        def scale_w(dve, w, gain, p, loaded, scaled):
            dve.wait_ge(loaded, 32 * (p + 1))
            dve.tensor_tensor(w, w, gain.unsqueeze(2).unsqueeze(3).broadcast_to([P, KT, 2, P]), ALU.mult).then_inc(scaled, 1)

        def load_wb(sp, dst, src, p, loaded):
            for y in range(2):
                sp.dma_start(dst[:, :, y, :], src[:, :, y, p, :]).then_inc(loaded, 16)

        def page_id(sp, n):
            at = pages[0:1, n:n + 1] if isinstance(n, int) else pages[0:1, bass.DynSlice(n, 1)]
            return sp.value_load(at, min_val=0, max_val=n_pool - 1)

        @block.sync
        def _(sp):
            sp.dma_start(gain_a, io["norm_in"][0].rearrange("(k p) -> p k", p=P), allow_slow_non_contiguous=True).then_inc(consts_in, 16)
            sp.dma_start(gain_o, io["g_norm_a"].rearrange("l p -> p l"), allow_slow_non_contiguous=True).then_inc(consts_in, 16)
            sp.dma_start(lb_in, io["lb_logits"].rearrange("l (h p) -> p (l h)", p=P), allow_slow_non_contiguous=True).then_inc(consts_in, 16)
            for t in range(TT + 1):
                rows = P if t < TT else S
                if t >= 2:
                    sp.wait_ge(x_turned, 2 * (t - 1))
                sp.dma_start(x_in[t % 2][0:rows], x_prompt[t] if t < TT else x_sample).then_inc(x_loaded[t % 2], 16)
                if t < 2:
                    load_w(sp, 0, t)

            def body(i):
                for par in range(2):
                    sp.wait_ge(proj_done.sem, proj_done.at(11, 2 * i + par))
                    load_w(sp, i + 1, par)

            with sp.Fori(0, LAST) as i:
                body(i)

            sp.wait_ge(proj_done.sem, proj_done.at(11, AH - 1))
            sp.dma_start(w_o, io["w_o_a"][0].rearrange("(h p) n -> p h n", p=P)).then_inc(w_o_loaded, 16)
            sp.wait_ge(vecs.sem, vecs.at("o_all", AH - 1))
            sp.dma_start(pages[0:1, :], io["page_table"].rearrange("(o b) j -> o (b j)", o=1)).then_inc(pages_in, 16)

            def res_in(i, par):
                t = 2 * i + par
                sp.wait_ge(tile_v.sem, tile_v.at("new1", t) - 2 * len(tile_v.names)) if not (isinstance(t, int) and t < 2) else None
                sp.sem_inc(sp_go, 1)
                src = x_sample if isinstance(t, int) and t == TT else x_prompt[t]
                sp.dma_start(res[par][0:src.shape[0]], src).then_inc(res_loaded[par], 16)

            res_in(0, 0)
            res_in(0, 1)
            load_wb(sp, w_kv, w_kv_d, 0, w_kv_loaded)
            load_wb(sp, w_qg, w_qg_d, 0, w_qg_loaded)
            with nc.allow_non_contiguous_dma(reason="small constants"):
                sp.dma_start(gain_kv, io["norm_kv"].rearrange("(k p) -> p k", p=P)).then_inc(keys_in, 16)
                sp.dma_start(gain_b, io["norm_in"][1].rearrange("(k p) -> p k", p=P)).then_inc(keys_in, 16)
                sp.dma_start(b_f[0:BH], io["b_fgate"].rearrange("(h o) -> h o", o=1)).then_inc(keys_in, 16)
            for x, g in enumerate((io["k_norm"], io["k_norm"], io["q_norm_b"][0], io["q_norm_b"][0])):
                sp.dma_start(gain_kq[:, x, :], g.partition_broadcast(P)).then_inc(keys_in, 16)
            sp.dma_start(w_f, io["w_fgate"].rearrange("(k p) n -> p k n", p=P)).then_inc(keys_in, 16)
            with sp.Fori(1, TT // 2) as i:
                res_in(i, 0)
                res_in(i, 1)
            res_in(TT // 2, 0)
            sp.wait_ge(pages_in, 16)
            with sp.Fori(0, S * PAGES) as n:
                page = page_id(sp, n)
                sp.dma_start(lf_pages[:, bass.DynSlice(n * BH, BH)], lf_cache[page]).then_inc(lf_in, 16)

            def k_in(p, g):
                for b in range(HALF):
                    for j in range(PAGES):
                        page = page_id(sp, (HALF * g + b) * PAGES + j)
                        sp.dma_start(k_ring[:, b, j, :], k_cache[page, :, p, :]).then_inc(k_loaded[b], 16)

            def v_in(p, g):
                for b in range(HALF):
                    for j in range(PAGES):
                        page = page_id(sp, (HALF * g + b) * PAGES + j)
                        sp.dma_start(v_ring[:, b, j, :], v_cache[page, :, p, :]).then_inc(v_loaded[b], 16)

            sp.wait_ge(y_done, 2 * (TT + 1))
            sp.sem_inc(sp_go, 1)
            k_in(0, 0)
            v_in(0, 0)
            sp.wait_ge(pj_done, TT + 1)
            load_wb(sp, w_kv, w_kv_d, 1, w_kv_loaded)
            sp.wait_ge(pj_done, 2 * (TT + 1))
            load_wb(sp, w_qg, w_qg_d, 1, w_qg_loaded)

            def pair(p, nxt, nxt2):
                sp.wait_ge(fv.sem, fv.at(f"pr{HALF - 1}", p))
                sp.sem_inc(sp_go, 1)
                k_in(p, 1)
                sp.wait_ge(fp.sem, fp.at("dec0", p))
                sp.sem_inc(sp_go, 1)
                v_in(p, 1)
                if nxt2:
                    sp.wait_ge(pj_done, 18 * (p + 1) + TT + 1)
                    sp.sem_inc(sp_go, 1)
                    load_wb(sp, w_kv, w_kv_d, p + 2, w_kv_loaded)
                if nxt:
                    sp.wait_ge(fv.sem, fv.at(f"pr{S - 1}", p))
                    sp.sem_inc(sp_go, 1)
                    k_in(p + 1, 0)
                    sp.wait_ge(fp.sem, fp.at("dec1", p))
                    sp.sem_inc(sp_go, 1)
                    v_in(p + 1, 0)
                if nxt2:
                    sp.wait_ge(pj_done, 18 * (p + 2))
                    sp.sem_inc(sp_go, 1)
                    load_wb(sp, w_qg, w_qg_d, p + 2, w_qg_loaded)

            with sp.Fori(0, PAIRS - 2) as p:
                pair(p, True, True)
            pair(PAIRS - 2, True, False)
            pair(PAIRS - 1, False, False)

            sp.wait_ge(fp.sem, fp.at("dec1", PAIRS - 1))
            sp.dma_start(w_o, io["w_o_b"][0].rearrange("(h p) n -> p h n", p=P)).then_inc(w_ob_loaded, 16)
            sp.wait_ge(fv.sem, fv.at("ogc0", PAIRS - 1))
            sp.wait_ge(h_stored[0], 16 * (TT // 2 + 1))
            sp.wait_ge(h_stored[1], 16 * TT // 2)

            def resb_in(i, par):
                t = 2 * i + par
                rows = S if isinstance(t, int) and t == TT else P
                if not (isinstance(t, int) and t < 2):
                    sp.wait_ge(y_stored[par], 16 * i)
                sp.sem_inc(sp_go, 1)
                sp.dma_start(res[par][0:rows], h_dram[bass.DynSlice(t * P, rows)] if not isinstance(t, int) else
                             h_dram[t * P:t * P + rows]).then_inc(resb_loaded[par], 16)
            resb_in(0, 0)
            resb_in(0, 1)
            with sp.Fori(1, TT // 2) as i:
                resb_in(i, 0)
                resb_in(i, 1)
            resb_in(TT // 2, 0)

        k_out = io["k_prompt"].rearrange("b (t p) (g x) d -> p (b t) g x d", p=P, x=2)
        v_out = io["v_prompt"].rearrange("b (t p) (g x) d -> p (b t) g (x d)", p=P, x=2)
        ks_out = io["k_sample"].rearrange("b s (g x) d -> (b s) g x d", x=2)
        vs_out = io["v_sample"].rearrange("b s (g x) d -> (b s) g (x d)", x=2)
        y_rows = io["y_prompt"].rearrange("b (t p) d -> (b t) p d", p=P)

        @block.gpsimd
        def _(pool):
            pool.memset(ident, 0.0).then_inc(built.sem, 1)
            pool.memset(ones_mean, 1.0 / P).then_inc(built.sem, 1)
            pool.memset(level_mask, 1.0).then_inc(built.sem, 1)
            pool.memset(chunk_keep, 1.0).then_inc(built.sem, 1)
            pool.memset(eps, EPS).then_inc(built.sem, 1)
            pool.memset(v_diag, 0.0).then_inc(built.sem, 1)
            pool.wait_ge(built.sem, built.at("vdiag0"))
            pool.affine_select(out=ident, in_=ident, compare_op=ALU.not_equal, fill=1.0, base=0,
                               pattern=[[-1, P]], channel_multiplier=1).then_inc(built.sem, 1)
            for l, w in enumerate(LEVELS):
                m = level_mask[:, l * C:(l + 1) * C].rearrange("p (b w) -> p b w", w=w)
                last = pool.affine_select(out=m, in_=m, compare_op=ALU.is_ge, fill=0.0, base=0,
                                          pattern=[[-2 * w, C // w], [0, w]], channel_multiplier=1)
            last.then_inc(built.sem, 1)
            keep = chunk_keep.rearrange("p (c s) -> p c s", s=C)
            pool.affine_select(out=keep, in_=keep, compare_op=ALU.not_equal, fill=0.0, base=0,
                               pattern=[[0, NC], [1, C]], channel_multiplier=0).then_inc(built.sem, 1)
            pool.wait_ge(built.sem, built.at("masks1"))
            for l, w in enumerate(LEVELS):
                m = level_mask[:, l * C:(l + 1) * C].rearrange("p (b w) -> p b w", w=w)
                last = pool.affine_select(out=m, in_=m, compare_op=ALU.is_ge, fill=0.0, base=w - 1,
                                          pattern=[[2 * w, C // w], [0, w]], channel_multiplier=-1)
            last.then_inc(built.sem, 1)

            pool.sem_inc(s_all_free, 1)

            def head(h):
                pool.dma_start(s_smp, state_in[h]).then_inc(state_loaded, 16)
                pool.wait_ge(vecs.sem, vecs.at("s_smp", h))
                pool.sem_inc(pool_go, 1)
                pool.dma_start(state_out[h], s_smp).then_inc(state_stored, 16)
                pool.wait_ge(vecs.sem, vecs.at("s_all", h))
                pool.sem_inc(pool_go, 1)
                pool.dma_start(prompt_out[h], s_all[:, NC - 1, :]).then_inc(prompt_stored, 16)
                pool.wait_ge(smp_done.sem, smp_done.at("o_smp", h))
                pool.wait_ge(state_stored, 16 * (h + 1))
                pool.wait_ge(prompt_stored, 16 * (h + 1))
                pool.sem_inc(s_all_free, 1)
            with pool.Fori(0, AH) as h:
                head(h)
            pool.wait_ge(prompt_stored, 16 * AH)
            pool.wait_ge(vecs.sem, vecs.at("o_all", AH - 1))
            pool.memset(one16, 1.0).then_inc(masks_b.sem, 1)
            pool.memset(causal, 0.0).then_inc(masks_b.sem, 1)
            pool.memset(later, 1.0).then_inc(masks_b.sem, 1)
            pool.wait_ge(masks_b.sem, masks_b.at("later"))
            pool.sem_inc(masks_b.sem, 1)
            pool.memset(lgt[0], LOW).then_inc(masks_b.sem, 1)
            pool.memset(lgt[1], LOW).then_inc(masks_b.sem, 1)
            pool.affine_select(out=causal, in_=causal, compare_op=ALU.is_ge, fill=LOW, base=0,
                               pattern=[[-1, P]], channel_multiplier=1).then_inc(masks_b.sem, 1)
            pool.affine_select(out=later, in_=later, compare_op=ALU.is_gt, fill=0.0, base=0,
                               pattern=[[-1, P]], channel_multiplier=1).then_inc(masks_b.sem, 1)

            def h_out(i, par):
                t = 2 * i + par
                rows = S if isinstance(t, int) and t == TT else P
                pool.wait_ge(tile_v.sem, tile_v.at("new1", t))
                pool.sem_inc(pool_go, 1)
                pool.dma_start(h_dram[t * P:t * P + rows] if isinstance(t, int) else h_dram[bass.DynSlice(t * P, rows)],
                               h_new[par][0:rows]).then_inc(h_stored[par], 16)
            with pool.Fori(0, TT // 2) as i:
                h_out(i, 0)
                h_out(i, 1)
            h_out(TT // 2, 0)
            pool.wait_ge(h_stored[0], 16 * (TT // 2 + 1))
            pool.wait_ge(h_stored[1], 16 * TT // 2)
            pool.wait_ge(tile_a.sem, tile_a.at("h_t1", TT))
            pool.memset(raw, 0.0).then_inc(raw_set, 1)
            pool.wait_ge(raw_set, 1)
            pool.memset(raw[:, :, 0:4 * (DH + 1)].rearrange("p t (x d) -> p t x d", x=4)[:, :, 2:4, DH:DH + 1], 1.0).then_inc(raw_set, 1)

            pool.wait_ge(keys_v.sem, keys_v.at("tok"))
            lf = lf_tok.rearrange("p (t h) -> p t h", h=BH)
            pool.dma_start(io["logf_prompt"].rearrange("b (t p) h -> p (b t) h", p=P), lf[:, 0:TT, :]).then_inc(lf_stored, 16)
            pool.dma_start(io["logf_sample"].rearrange("b s h -> (b s) h"), lf[0:S, TT, :]).then_inc(lf_stored, 16)
            pool.wait_ge(lf_stored, 32)
            pool.dma_start(lf_new, io["logf_sample"].rearrange("b s h -> (b s h)").partition_broadcast(P)).then_inc(lf_new_in, 16)
            pool.wait_ge(lf_new_in, 16)

            def pair(p):
                pool.wait_ge(fv.sem, fv.at("kq", p))
                pool.wait_ge(fa.sem, fa.at("v_cur", p))
                pool.sem_inc(pool_go, 1)
                kk = raw[:, :, 0:2 * (DH + 1)].rearrange("p t (x d) -> p t x d", x=2)[:, :, :, 0:DH]
                qq = raw[:, :, 2 * (DH + 1):4 * (DH + 1)].rearrange("p t (x d) -> p t x d", x=2)[:, :, :, 0:DH]
                for x in range(2):
                    pool.dma_start(k_out[:, :, p, x, :], kk[:, 0:TT, x, :]).then_inc(kv_stored, 16)
                pool.dma_start(v_out[:, :, p, :], v_cur[:, 0:TT, :]).then_inc(kv_stored, 16)
                pool.dma_start(ks_out[:, p, :, :], kk[0:S, TT]).then_inc(kv_stored, 16)
                pool.dma_start(vs_out[:, p, :], v_cur[0:S, TT, :]).then_inc(kv_stored, 16)
                pool.dma_start(q_dram[p].rearrange("b (x d) -> b x d", x=2), qq[0:S, TT]).then_inc(kv_stored, 16)
                pool.wait_ge(kv_stored, 96 * (p + 1))
                pool.sem_inc(pool_go, 1)
                if not isinstance(p, int) or p:
                    pool.wait_ge(fv.sem, fv.at("lg1", p - 1))
                    pool.wait_ge(fp.sem, fp.at("dec1", p - 1))
                    pool.sem_inc(pool_go, 1)
                pool.dma_start(q_all, q_dram[p].rearrange("b n -> (b n)").partition_broadcast(P)).then_inc(new_loaded, 16)
                pool.dma_start(k_new, ks_out[:, p].rearrange("b x d -> b (x d)").unsqueeze(0)).then_inc(new_loaded, 16)
                pool.dma_start(v_new, vs_out[:, p, :].unsqueeze(0)).then_inc(new_loaded, 16)
                for g in range(2):
                    pool.wait_ge(fv.sem, fv.at(f"lg{g}", p))
                    pool.sem_inc(pool_go, 1)
                    pool.partition_all_reduce(m_all[g], top8[g], P, bass.bass_isa.ReduceOp.max).then_inc(top_all, 1)

            pair(0)
            with pool.Fori(1, PAIRS) as p:
                pair(p)

            def y_out(i, par):
                t = 2 * i + par
                last = isinstance(t, int) and t == TT
                rows = S if last else P
                pool.wait_ge(yb_v.sem, yb_v.at("y1", t))
                pool.sem_inc(pool_go, 1)
                dst = io["y_sample"].rearrange("b s d -> (b s) d") if last else y_rows[t]
                pool.dma_start(dst, res[par][0:rows]).then_inc(y_stored[par], 16)
            with pool.Fori(0, TT // 2) as i:
                y_out(i, 0)
                y_out(i, 1)
            y_out(TT // 2, 0)
            pool.wait_ge(y_stored[0], 16 * (TT // 2 + 1))
            pool.wait_ge(y_stored[1], 16 * TT // 2)
            pool.wait_ge(kv_stored, 96 * PAIRS)
            pool.wait_ge(state_stored, 16 * AH)

        @block.scalar
        def _(act):
            me = Steps(act, act_steps)
            act.preload_act_table_set("natural_log_exp_and_others")
            act.sem_inc(lv_taken_a, 2)
            act.wait_ge(consts_v, 1)
            act.activation(lb_e, lb_e, ACT.Exp).then_inc(lb_a, 1)
            act.wait_ge(built.sem, built.at("eps"))
            for t in range(TT + 1):
                rows = P if t < TT else S
                act.wait_ge(x_loaded[t % 2], 16 * (t // 2 + 1))
                me.chain(act.activation(x_sq[t % 2][0:rows], x_in[t % 2][0:rows], ACT.Square, accum_out=msq[0:rows, t:t + 1]))
                me.chain(act.activation(rstd[0:rows, t:t + 1], msq[0:rows, t:t + 1], ACT.Ln, bias=eps[0:rows], scale=1.0 / D))
                act.activation(rstd[0:rows, t:t + 1], rstd[0:rows, t:t + 1], ACT.Exp, scale=-0.5).then_inc(x_rstd, 1)

            def evac(i, par, g):
                h = 2 * i + par
                act.wait_ge(proj_done.sem, proj_done.at(g, h))
                src = bank[g % 2]
                if g < 9:
                    if g % 3 == 0 and not (isinstance(h, int) and h == 0):
                        act.wait_ge(vecs.sem, vecs.at(("k_in", "q", "sg")[g // 3], h - 1))
                    dst = (raw_f, raw_q, raw_g)[g // 3][:, g % 3 * W3:(g % 3 + 1) * W3]
                    ins = act.copy(dst, src[:, 0:W3])
                elif g < 11:
                    ins = act.copy(v_tok[par][:, 4 * (g - 9):4 * (g - 8), :], src[:, :])
                else:
                    ins = act.copy(v_tok[par][0:S, TT, :], src[0:S, 0:P])
                ins.then_inc(proj_taken.sem, 1)

            def head(i, par, nxt):
                h = 2 * i + par

                def v(name):
                    act.wait_ge(vecs.sem, vecs.at(name, h))

                def e(g):
                    if nxt:
                        evac(i + par, 1 - par, g)

                def level(w):
                    d = diff[LEVELS.index(w) % 2]
                    v(f"diff{w}")
                    act.activation(d, d, ACT.Exp).then_inc(acts.sem, 1)

                v("abs_f")
                me.chain(act.activation(t0, t0, ACT.Exp, scale=-1.0))
                act.activation(t0, t0, ACT.Ln, bias=inv_h, scale=inv_h).then_inc(acts.sem, 1)
                v("abs_q")
                me.chain(act.activation(t3, t3, ACT.Exp, scale=-1.0))
                act.activation(t3, t3, ACT.Ln, bias=1.0).then_inc(acts.sem, 1)
                v("abs_g")
                me.chain(act.activation(sg_h, sg_h, ACT.Exp, scale=-1.0))
                act.activation(sg_h, sg_h, ACT.Ln, bias=1.0).then_inc(acts.sem, 1)
                v("k_in")
                act.activation(k_h, t1, ACT.Exp, scale=-1.0).then_inc(acts.sem, 1)
                e(0)
                act.activation(f_smp, logf[:, T:N], ACT.Exp)
                v("cum")
                act.activation(dec, cum[:, C - 1::C], ACT.Exp).then_inc(acts.sem, 1)
                v("q_in")
                act.activation(t3, t3, ACT.Exp).then_inc(acts.sem, 1)
                act.activation(q_dec, cum, ACT.Exp).then_inc(acts.sem, 1)
                v("g_in")
                act.activation(sg_h, sg_h, ACT.Exp).then_inc(acts.sem, 1)
                e(1)
                level(32)
                e(2)
                level(16)
                e(3)
                level(8)
                e(4)
                level(4)
                v("o_smp")
                act.activation(sq_smp, o_smp, ACT.Square).then_inc(acts.sem, 1)
                e(5)
                v("diff_kd")
                act.activation(t1[:, 0:T], t1[:, 0:T], ACT.Exp).then_inc(acts.sem, 1)
                level(2)
                act.wait_ge(smp_done.sem, smp_done.at("mean_smp", h))
                act.activation(rs_smp, bank[6][:, 16:16 + S], ACT.Ln, bias=eps).then_inc(acts.sem, 1)
                e(6)
                level(1)
                for j in range(2):
                    act.wait_ge(uu_done.sem, uu_done.at(f"turn{j}", h))
                    act.copy(k_dec_tok[:, 4 * j:4 * j + 4, :], bank[4 + j][:, :]).then_inc(uu_taken_a, 1)
                e(7)
                e(8)
                for j in range(2):
                    act.wait_ge(ob_done.sem, ob_done.at(f"o{j}", h))
                    act.activation(o_sq[:, 512 * j:512 * j + 512], bank[6 + j][:, :], ACT.Square).then_inc(acts.sem, 1)
                e(9)
                e(10)
                for j in range(2):
                    act.wait_ge(lv_done.sem, lv_done.at(f"mean{j}", h))
                    act.activation(o_rs[:, 512 * j:512 * j + 512], bank[2 + j][:, :], ACT.Ln, bias=eps).then_inc(lv_taken_a, 1)
                    if j == 0:
                        e(11)
                act.wait_ge(lv_taken_a, 2 * h + 4)
                act.activation(o_rs[:, 0:T], o_rs[:, 0:T], ACT.Exp, scale=-0.5)
                act.activation(rs_smp, rs_smp, ACT.Exp, scale=-0.5).then_inc(acts.sem, 1)

            for g in range(12):
                evac(0, 0, g)
            PER = 2 * 3
            with act.Fori(0, LAST) as i:
                me.enter(i, PER)
                head(i, 0, True)
                head(i, 1, True)
                me.leave(PER, LAST)
            head(LAST, 0, True)
            head(LAST, 1, False)

            me.straight()

            def tile(i, par):
                t = 2 * i + par
                rows = S if isinstance(t, int) and t == TT else P
                act.wait_ge(tile_v.sem, tile_v.at("new1", t))
                me.chain(act.activation(h_sq[0:rows], h_new[par][0:rows], ACT.Square, accum_out=msq[0:rows, par:par + 1]))
                me.chain(act.activation(rstd[0:rows, par:par + 1], msq[0:rows, par:par + 1], ACT.Ln, bias=eps[0:rows], scale=1.0 / D))
                act.activation(rstd[0:rows, par:par + 1], rstd[0:rows, par:par + 1], ACT.Exp, scale=-0.5).then_inc(tile_a.sem, 1)
                for j in range(2):
                    act.wait_ge(h_turned, 2 * t + j + 1)
                    dst = h_t[:, 4 * j:4 * j + 4, t * P:t * P + rows] if isinstance(t, int) else h_t[:, 4 * j:4 * j + 4, bass.DynSlice(t * P, rows)]
                    act.sem_inc(end_go, 1)
                    act.copy(dst, bank[4 + 2 * par + j].rearrange("p (k n) -> p k n", n=P)[:, :, 0:rows]).then_inc(tile_a.sem, 1)
            with act.Fori(0, TT // 2) as i:
                me.enter(i, 4)
                tile(i, 0)
                tile(i, 1)
                me.leave(4, TT // 2)
            tile(TT // 2, 0)

            act.wait_ge(keys_v.sem, keys_v.at("abs"))
            me.chain(act.activation(a16[0:BH], a16[0:BH], ACT.Exp, scale=-1.0))
            act.activation(a16[0:BH], a16[0:BH], ACT.Ln, bias=1.0).then_inc(keys_a.sem, 1)

            act.wait_ge(raw_set, 2)

            def evac_b(p, c):
                t, rows = c % 9, P if c % 9 < TT else S
                act.wait_ge(pj_done, 18 * p + c + 1)
                if c == 0 and not (isinstance(p, int) and p == 0):
                    act.wait_ge(fv.sem, fv.at("g", p - 1))
                    act.wait_ge(fp.sem, fp.at(f"kq_t{TT - 1}", p - 1))
                    act.wait_ge(kv_stored, 96 * p)
                y = c // 9
                kq = raw[0:rows, t, y * 2 * (DH + 1):(y + 1) * 2 * (DH + 1)].rearrange("p (x d) -> p x d", x=2)[:, :, 0:DH]
                act.copy(kq, bank[c % 2][0:rows, 0:P].rearrange("p (x d) -> p x d", x=2))
                act.copy(raw[0:rows, t, 4 * (DH + 1) + y * P:4 * (DH + 1) + (y + 1) * P], bank[c % 2][0:rows, P:2 * P]).then_inc(pj_taken, 1)

            for c in range(18):
                evac_b(0, c)

            def pair(p, nxt):
                def v(name):
                    act.wait_ge(fv.sem, fv.at(name, p))

                act.wait_ge(pj_taken, 18 * (p + 1))
                kq4 = raw[:, :, 0:4 * (DH + 1)].rearrange("p t (x d) -> p t x d", x=4)[:, :, :, 0:DH]
                act.activation(kq_sq, kq4, ACT.Square).then_inc(fa.sem, 1)
                act.copy(v_cur, raw[:, :, 4 * (DH + 1):4 * (DH + 1) + P]).then_inc(fa.sem, 1)
                v("ssq")
                me.chain(act.activation(rs_kq, ssq, ACT.Ln, bias=eps, scale=1.0 / DH))
                act.activation(rs_kq, rs_kq, ACT.Exp, scale=-0.5).then_inc(fa.sem, 1)
                v("abs_g")
                me.chain(act.activation(g_cur, g_cur, ACT.Exp, scale=-1.0))
                act.activation(g_cur, g_cur, ACT.Ln, bias=1.0).then_inc(fa.sem, 1)
                for t in range(1, TT, 2):
                    act.wait_ge(fp.sem, fp.at(f"kq_t{t}", p))
                    act.copy(kq_t[0:DH + 1, :, cols(t)], bank[2 + t % 4][0:DH + 1, :].rearrange("p (x n) -> p x n", x=4)).then_inc(fa.sem, 1)
                v("g_in")
                act.activation(g_cur, g_cur, ACT.Exp).then_inc(fa.sem, 1)

                def exp(w):
                    x, i = w % 2, w % TT
                    v(f"mx{w}")
                    if w >= 2:
                        act.wait_ge(fp.sem, fp.at(f"pt{w - 2}_{int((w - 2) % TT >= 4)}", p))
                    me.did(act.activation(prob[x][:, 0:(i + 1) * P], psum[:, (2 + 2 * x) * 512:(2 + 2 * x) * 512 + (i + 1) * P],
                                   ACT.Exp, bias=top[:, w:w + 1], accum_out=total[:, w:w + 1]))
                    me.need(me.base + me.n)
                    act.sem_inc(fa.sem, 1)

                exp(0)
                for w in range(ITEMS):
                    x, i = w % 2, w % TT
                    if i >= 4:
                        act.wait_ge(fp.sem, fp.at(f"pt{w}_1", p))
                        act.copy(prob_t[x][:, 512:(i + 1) * P], bank[7][:, 0:(i + 1) * P - 512]).then_inc(fa.sem, 1)
                    if w + 1 < ITEMS:
                        exp(w + 1)
                    if nxt:
                        evac_b(p + 1, w)
                    if w % TT == TT - 1:
                        g = w // TT
                        v(f"df{g}")
                        act.activation(expd[g], expd[g], ACT.Exp).then_inc(fa.sem, 1)
                if nxt:
                    evac_b(p + 1, 16)
                    evac_b(p + 1, 17)
                act.wait_ge(fp.sem, fp.at("og1", p))
                act.sem_inc(end_go, 1)
                act.copy(o_cols(p, 1), bank[3]).then_inc(fa.sem, 1)

            PER = 2 + ITEMS
            me.straight()
            with act.Fori(0, PAIRS - 1) as p:
                me.enter(p, PER)
                pair(p, True)
                me.leave(PER, PAIRS - 1)
            pair(PAIRS - 1, False)

        @block.vector
        def _(dve):
            me = Steps(dve, dve_steps)
            dve.sem_inc(vecs.sem, vecs.ahead)
            dve.sem_inc(uu_taken_v, 6)
            dve.wait_ge(consts_in, 48)
            dve.tensor_tensor(lb_e, lb_in, lb_in, ALU.subtract).then_inc(consts_v, 1)
            dve.wait_ge(lb_a, 1)
            me.chain(dve.reciprocal(lb_r, lb_e))
            me.chain(dve.tensor_tensor(lb_r, lb_e, lb_r, ALU.mult))
            me.chain(dve.tensor_tensor(lb_r, lb_r, lb_r, ALU.subtract))
            me.chain(dve.tensor_scalar(one_lb, lb_r, -1.0, 1.0, ALU.mult, ALU.add))
            me.chain(dve.reciprocal(inv_lb, one_lb))
            dve.wait_ge(built.sem, built.at("masks"))

            def x_out(t):
                rows = P if t < TT else S
                for j in range(2):
                    dve.wait_ge(x_turned, 2 * t + j + 1)
                    src = bank[2 + 2 * (t % 2) + j][:, :].rearrange("p (k n) -> p k n", n=P)[:, :, 0:rows]
                    dve.tensor_tensor(x_t[:, 4 * j:4 * j + 4, cols(t)], src,
                                      gain_a[:, 4 * j:4 * j + 4].unsqueeze(2).broadcast_to([P, 4, rows]),
                                      ALU.mult).then_inc(x_ready, 1)

            for t in range(TT + 1):
                rows = P if t < TT else S
                dve.wait_ge(x_rstd, t + 1)
                dve.tensor_scalar(x_in[t % 2][0:rows], x_in[t % 2][0:rows], rstd[0:rows, t:t + 1], None,
                                  ALU.mult).then_inc(x_scaled, 1)
                if t:
                    x_out(t - 1)
            x_out(TT)
            def head(i, par):
                h = 2 * i + par
                me.straight() if isinstance(i, int) else None

                def a(name):
                    dve.wait_ge(acts.sem, acts.at(name, h))

                def split(w):
                    c = cum.rearrange("p (b w) -> p b w", w=2 * w)
                    d = diff[LEVELS.index(w) % 2].rearrange("p (b w) -> p b w", w=2 * w)
                    mid = c[:, :, w - 1:w].broadcast_to([P, T // (2 * w), w])
                    dve.tensor_tensor(d[:, :, w:2 * w], c[:, :, w:2 * w], mid, ALU.subtract)
                    dve.tensor_tensor(d[:, :, 0:w], mid, c[:, :, 0:w], ALU.subtract).then_inc(vecs.sem, 1)

                def factors(w):
                    a(f"exp{w}")
                    d = diff[LEVELS.index(w) % 2].rearrange("p (b w) -> p b w", w=2 * w)
                    f = fact[LEVELS.index(w) % 2].rearrange("p (b w) -> p b w", w=2 * w)
                    q = q_h[:, 0:T].rearrange("p (b w) -> p b w", w=2 * w)
                    k = k_h[:, 0:T].rearrange("p (b w) -> p b w", w=2 * w)
                    dve.tensor_tensor(f[:, :, w:2 * w], d[:, :, w:2 * w], q[:, :, w:2 * w], ALU.mult)
                    dve.tensor_tensor(f[:, :, 0:w], d[:, :, 0:w], k[:, :, 0:w], ALU.mult).then_inc(vecs.sem, 1)

                def merge(w):
                    l = LEVELS.index(w)
                    dve.wait_ge(lv_done.sem, lv_done.at(f"level{w}", h))
                    dve.wait_ge(lv_taken_v, 8 * h + 2 + l)
                    dve.sem_inc(merge_go, 1)
                    out = att.rearrange("p (t b w) -> p t b w", t=TT, w=2 * w)[:, :, :, w:2 * w]
                    mask = level_mask[:, l * C:(l + 1) * C].bitcast(I32).rearrange("p (b w) -> p b w", w=w)
                    dve.copy_predicated(out, mask.unsqueeze(1).broadcast_to([P, TT, C // w, w]),
                                        bank[2 + l % 2][:, :].rearrange("p (t b w) -> p t b w", t=TT, w=w))\
                       .then_inc(lv_taken_v, 1)

                dve.tensor_copy(inv_h, col(inv_lb, h))
                for raw, out, g in ((raw_f, t0, 2), (raw_q, t3, 5), (raw_g, sg_h, 8)):
                    dve.wait_ge(proj_taken.sem, proj_taken.at(g, h))
                    if g == 8:
                        dve.wait_ge(vecs.sem, vecs.at("o_all", h - 1))
                    dve.tensor_scalar(out.bitcast(I32), raw.bitcast(I32), 0x7FFFFFFF, None, ALU.bitwise_and).then_inc(vecs.sem, 1)
                a("ln_f")
                dve.scalar_tensor_tensor(out=logf, in0=raw_f, scalar=0.0, in1=t0, op0=ALU.min,
                                         op1=ALU.subtract).then_inc(vecs.sem, 1)
                dve.scalar_tensor_tensor(out=t1, in0=raw_f, scalar=0.0, in1=t0, op0=ALU.max,
                                         op1=ALU.add).then_inc(vecs.sem, 1)
                dve.wait_ge(vecs.sem, vecs.at("logf", h))
                dve.tensor_tensor_scan(cum, chunk_keep, logf[:, 0:T], 0.0, ALU.mult, ALU.add)\
                   .then_inc(vecs.sem, 1)
                a("ln_q")
                dve.scalar_tensor_tensor(out=t3, in0=raw_q, scalar=0.0, in1=t3, op0=ALU.min,
                                         op1=ALU.subtract).then_inc(vecs.sem, 1)
                dve.wait_ge(vecs.sem, vecs.at("cum", h))
                split(32)
                a("ln_g")
                dve.scalar_tensor_tensor(out=sg_h, in0=raw_g, scalar=0.0, in1=sg_h, op0=ALU.min,
                                         op1=ALU.subtract).then_inc(vecs.sem, 1)
                a("sig_q")
                dve.tensor_tensor(q_h, raw_q, t3, ALU.mult).then_inc(vecs.sem, 1)
                a("sig_g")
                dve.scalar_tensor_tensor(out=sg_h, in0=raw_g, scalar=gain_o, in1=sg_h, op0=ALU.mult,
                                         op1=ALU.mult).then_inc(vecs.sem, 1)
                c3 = cum.rearrange("p (c s) -> p c s", s=C)
                dve.tensor_tensor(t1[:, 0:T].rearrange("p (c s) -> p c s", s=C),
                                  c3[:, :, C - 1:C].broadcast_to([P, NC, C]), c3, ALU.subtract)\
                   .then_inc(vecs.sem, 1)
                dve.wait_ge(smp_done.sem, smp_done.at("k_smp", h))
                dve.tensor_copy(k_smp[0:S, :], bank[6][0:S, P:2 * P]).then_inc(vecs.sem, 1)
                dve.wait_ge(proj_taken.sem, proj_taken.at(11, h))
                dve.tensor_tensor(v_diag[0:S], v_tok[par][0:S, TT:TT + 1, :].broadcast_to([S, S, P]),
                                  ident[0:S, 0:S].unsqueeze(2).broadcast_to([S, S, P]), ALU.mult)\
                   .then_inc(vecs.sem, 1)
                a("exp_cum")
                dve.wait_ge(vecs.sem, vecs.at("q", h))
                dve.tensor_tensor(q_dec, q_dec, q_h[:, 0:T], ALU.mult).then_inc(vecs.sem, 1)
                dve.wait_ge(state_loaded, 16 * (h + 1))
                me.chain(dve.tensor_tensor(s_smp, s_smp, f_smp.unsqueeze(2).broadcast_to([P, S, P]), ALU.mult))
                for j in range(2):
                    dve.wait_ge(uu_done.sem, uu_done.at(f"outer{j}", h))
                    dve.tensor_tensor(s_smp[:, 4 * j:4 * j + 4, :], s_smp[:, 4 * j:4 * j + 4, :],
                                      bank[4 + j][:, :].rearrange("p (b v) -> p b v", v=P), ALU.add)\
                       .then_inc(uu_taken_v, 1)
                dve.wait_ge(uu_taken_v, 6 * h + 8)
                dve.sem_inc(vecs.sem, 1)
                factors(32)
                split(16)
                dve.wait_ge(smp_done.sem, smp_done.at("o_smp", h))
                dve.tensor_copy(o_smp, bank[6][:, 0:S]).then_inc(vecs.sem, 1)
                for j in range(2):
                    dve.wait_ge(lv_done.sem, lv_done.at(f"diag{j}", h))
                    dve.tensor_tensor(att[:, 512 * j:512 * j + 512].rearrange("p (t q) -> p t q", q=P),
                                      bank[2 + j][:, :].rearrange("p (t q) -> p t q", q=P),
                                      ident.unsqueeze(1).broadcast_to([P, 4, P]), ALU.mult).then_inc(lv_taken_v, 1)
                factors(16)
                split(8)
                merge(32)
                factors(8)
                split(4)
                merge(16)
                factors(4)
                split(2)
                merge(8)
                a("exp_kd")
                dve.tensor_tensor(k_dec, k_h[:, 0:T], t1[:, 0:T], ALU.mult).then_inc(vecs.sem, 1)
                factors(2)
                split(1)
                merge(4)
                factors(1)
                merge(2)
                merge(1)
                dve.wait_ge(lv_taken_v, 8 * h + 8)
                dve.sem_inc(vecs.sem, 1)
                dve.wait_ge(s_all_free, h + 1)
                for c in range(NC):
                    half, new = c // 8, bank[4 + c % 2][:, c % 8 // 2 * P:(c % 8 // 2 + 1) * P]
                    if c % 8 == 0:
                        dve.wait_ge(uu_done.sem, uu_done.at(f"upd{2 * half + 1}", h))
                    if c == 0:
                        ins = dve.tensor_copy(s_all[:, 0, :], new)
                    else:
                        ins = dve.scalar_tensor_tensor(out=s_all[:, c, :], in0=s_all[:, c - 1, :],
                                                       scalar=dec[:, c:c + 1], in1=new, op0=ALU.mult, op1=ALU.add)
                    if c % 8 >= 6:
                        ins.then_inc(uu_taken_v, 1)
                        dve.wait_ge(uu_taken_v, 6 * h + 8 + 2 * half + c % 8 - 5)
                    else:
                        me.chain(ins)
                dve.sem_inc(vecs.sem, 1)
                a("dev")
                for j in range(2):
                    me.did(dve.tensor_tensor(o_rs[:, 512 * j:512 * j + 512], bank[6 + j][:, :],
                                             o_rs[:, 512 * j:512 * j + 512], ALU.mult))
                me.chain(dve.tensor_tensor(o_rs[:, T:N], o_smp, rs_smp, ALU.mult))
                dve.tensor_tensor(o_t[:, h, :], o_rs, sg_h, ALU.mult).then_inc(vecs.sem, 1)

            def col(a, h):
                return a[:, h:h + 1] if isinstance(h, int) else a[:, bass.DynSlice(h, 1)]

            PER = 2 * 16
            with dve.Fori(0, LAST) as i:
                me.enter(i, PER)
                head(i, 0)
                head(i, 1)
                me.leave(PER, LAST)
            head(LAST, 0)
            head(LAST, 1)

            dve.wait_ge(vecs.sem, vecs.at("o_all", AH - 1))

            def tile(i, par):
                t = 2 * i + par
                static = isinstance(t, int)
                rows = S if static and t == TT else P
                if not (static and t < 2):
                    dve.wait_ge(y_done, 2 * (t - 1))
                dve.sem_inc(end_go_v, 1)
                dve.tensor_copy(o_tile[par][:, :, 0:rows], o_t[:, :, cols(t)] if static else o_t[:, :, bass.DynSlice(t * P, P)])\
                   .then_inc(tile_v.sem, 1)
                dve.wait_ge(res_loaded[par], 16 * (i + 1))
                if not (static and t < 2):
                    dve.wait_ge(h_stored[par], 16 * i)
                for j in range(2):
                    dve.wait_ge(y_done, 2 * t + j + 1)
                    dve.tensor_tensor(h_new[par][0:rows, 512 * j:512 * j + 512], res[par][0:rows, 512 * j:512 * j + 512],
                                      bank[2 * par + j][0:rows], ALU.add).then_inc(tile_v.sem, 1)
                dve.wait_ge(tile_a.sem, tile_a.at("rstd", t))
                if not (static and t < 2):
                    dve.wait_ge(h_turned, 2 * (t - 1))
                dve.tensor_scalar(h_sc[par][0:rows], h_new[par][0:rows], rstd[0:rows, par:par + 1], None, ALU.mult)\
                   .then_inc(tile_v.sem, 1)
            tile(0, 0)
            tile(0, 1)
            with dve.Fori(1, TT // 2) as i:
                tile(i, 0)
                tile(i, 1)
            tile(TT // 2, 0)

            dve.wait_ge(keys_in, 16 * 8)
            dve.wait_ge(masks_b.sem, masks_b.at("later1"))
            dve.tensor_tensor(w_f, w_f, gain_kv.unsqueeze(2).broadcast_to([P, KT, BH]), ALU.mult).then_inc(keys_v.sem, 1)
            me.chain(dve.tensor_scalar(gain_kq[:, 2:4, :], gain_kq[:, 2:4, :], DH ** -0.5, None, ALU.mult))
            scale_w(dve, w_kv, gain_kv, 0, w_kv_loaded, w_kv_scaled)
            scale_w(dve, w_qg, gain_b, 0, w_qg_loaded, w_qg_scaled)
            dve.wait_ge(keys_p.sem, keys_p.at("z"))
            z = z16[0:BH]
            for n in range(3):
                me.did(dve.tensor_scalar(z[:, n * W3:(n + 1) * W3], bank[n][0:BH, 0:W3], b_f[0:BH], None, ALU.add))
            me.need(me.base + me.n)
            dve.tensor_scalar(a16[0:BH].bitcast(I32), z.bitcast(I32), 0x7FFFFFFF, None, ALU.bitwise_and).then_inc(keys_v.sem, 1)
            dve.wait_ge(keys_a.sem, 1)
            dve.scalar_tensor_tensor(out=z, in0=z, scalar=0.0, in1=a16[0:BH], op0=ALU.min, op1=ALU.subtract).then_inc(keys_v.sem, 1)
            dve.wait_ge(keys_v.sem, keys_v.at("lf"))
            dve.tensor_tensor_scan(c16[0:BH], one16[0:BH], z[:, 0:T], 0.0, ALU.mult, ALU.add).then_inc(keys_v.sem, 1)
            dve.wait_ge(keys_p.sem, keys_p.at("turned"))
            me.did(dve.tensor_scalar(c_tok, bank[4][:, 0:TT * BH], -1.0, None, ALU.mult))
            me.did(dve.tensor_copy(lf_tok[0:S, TT * BH:(TT + 1) * BH], bank[3][0:S, TT * BH:(TT + 1) * BH]))
            dve.tensor_copy(lf_tok[:, 0:TT * BH], bank[3][:, 0:TT * BH]).then_inc(keys_v.sem, 1)
            dve.wait_ge(keys_p.sem, keys_p.at("suffix"))
            dve.wait_ge(lf_new_in, 16)
            me.chain(dve.tensor_copy(acc, lf_new.rearrange("p (b h) -> p b h", h=BH)))
            within = psum[:, 0:1024].rearrange("p (b j h) -> p b j h", j=PAGES, h=BH)
            whole = psum[:, 2560:3584].rearrange("p (b j h) -> p b j h", j=PAGES, h=BH)
            for j in reversed(range(PAGES)):
                me.did(dve.tensor_tensor(bias[:, :, :, j], acc, within[:, :, j, :], ALU.add))
                me.chain(dve.scalar_tensor_tensor(out=acc, in0=whole[:, :, j, :], scalar=float(P), in1=acc, op0=ALU.mult, op1=ALU.add))
            dve.sem_inc(keys_v.sem, 1)

            def pair(p, nxt, nxt2):
                static = isinstance(p, int)

                def a(name):
                    dve.wait_ge(fa.sem, fa.at(name, p))

                def pe(name, q=None):
                    dve.wait_ge(fp.sem, fp.at(name, p if q is None else q))

                a("sq")
                dve.tensor_reduce(ssq, kq_sq, AX.X, ALU.add).then_inc(fv.sem, 1)
                g_raw = raw[:, :, 4 * (DH + 1) + P:RAW]
                dve.tensor_scalar(g_cur.bitcast(I32), g_raw.bitcast(I32), 0x7FFFFFFF, None, ALU.bitwise_and).then_inc(fv.sem, 1)
                kq5 = raw[:, :, 0:4 * (DH + 1)].rearrange("p t (x d) -> p t x d", x=4)
                c2 = c_tok.rearrange("p (t h) -> p t h", h=BH)
                me.did(dve.tensor_copy(kq5[:, 0:TT, 0:2, DH], c2[:, :, 2 * p:2 * p + 2] if static else c2[:, :, bass.DynSlice(2 * p, 2)]))
                a("rs")
                kq4 = kq5[:, :, :, 0:DH]
                me.chain(dve.tensor_tensor(kq4, kq4, rs_kq.rearrange("p (t x) -> p t x", x=4).unsqueeze(3).broadcast_to([P, TT + 1, 4, DH]), ALU.mult))
                dve.tensor_tensor(kq4, kq4, gain_kq.unsqueeze(1).broadcast_to([P, TT + 1, 4, DH]), ALU.mult).then_inc(fv.sem, 1)
                a("ln_g")
                dve.scalar_tensor_tensor(out=g_cur, in0=g_raw, scalar=0.0, in1=g_cur, op0=ALU.min, op1=ALU.subtract).then_inc(fv.sem, 1)
                for t in range(0, TT, 2):
                    pe(f"kq_t{t}")
                    dve.tensor_copy(kq_t[0:DH + 1, :, cols(t)], bank[2 + t % 4][0:DH + 1, :].rearrange("p (x n) -> p x n", x=4)).then_inc(fv.sem, 1)
                a("sig_g")
                dve.tensor_tensor(g_cur, g_cur, g_raw, ALU.mult).then_inc(fv.sem, 1)
                pe("g_smp")
                dve.tensor_copy(g_smp, bank[7][:, 0:S]).then_inc(fv.sem, 1)

                def masked_max(w):
                    x, i = w % 2, w % TT
                    pe(f"qk{w}")
                    diag = psum[:, (2 + 2 * x) * 512 + i * P:(2 + 2 * x) * 512 + (i + 1) * P]
                    me.chain(dve.tensor_tensor(diag, diag, causal, ALU.add))
                    dve.tensor_reduce(top[:, w:w + 1], psum[:, (2 + 2 * x) * 512:(2 + 2 * x) * 512 + (i + 1) * P], AX.X,
                                      ALU.max, negate=True).then_inc(fv.sem, 1)

                def smp_out(g):
                    pe(f"dec{g}")
                    me.chain(dve.tensor_reduce(den, bank[7][:, 16:16 + 72].rearrange("p (n j) -> p n j", j=9), AX.X, ALU.add))
                    me.chain(dve.reciprocal(den, den))
                    me.chain(dve.scalar_tensor_tensor(out=o_two, in0=bank[7][:, P:P + 8], scalar=1.0 / P, in1=den, op0=ALU.mult, op1=ALU.mult))
                    o2 = o_two.rearrange("p (b x) -> p b x", x=2)
                    for x in range(2):
                        rows = slice(x * DH, (x + 1) * DH)
                        lo = T + HALF * g
                        dst = o_t[rows, p, lo:lo + HALF] if static else o_t[rows, bass.DynSlice(p, 1), lo:lo + HALF].rearrange("p a n -> p (a n)")
                        ins = dve.tensor_tensor(dst, o2[rows, :, x], g_smp[rows, HALF * g:HALF * g + HALF], ALU.mult)
                        if x == 0:
                            me.did(ins)
                    ins.then_inc(fv.sem, 1)

                masked_max(0)
                for w in range(ITEMS):
                    x, i, g = w % 2, w % TT, w // TT
                    if w == TT:
                        smp_out(0)
                    pe(f"pt{w}_0")
                    width = min(i + 1, 4) * P
                    dve.tensor_copy(prob_t[x][:, 0:width], bank[6][:, 0:width]).then_inc(fv.sem, 1)
                    if w + 1 < ITEMS:
                        masked_max(w + 1)
                    pe(f"pv{w}")
                    me.chain(dve.reciprocal(r_total[:, w:w + 1], total[:, w:w + 1]))
                    head_cols = slice(g * DH, (g + 1) * DH)
                    dve.scalar_tensor_tensor(out=og[:, i, head_cols], in0=bank[2 + 2 * x][:, 0:DH], scalar=r_total[:, w:w + 1],
                                             in1=g_cur[:, i, head_cols], op0=ALU.mult, op1=ALU.mult).then_inc(fv.sem, 1)
                    lg = lgt[g].rearrange("p (b x j) -> p b x j", x=2, j=9)
                    if 1 <= i <= HALF:
                        b = i - 1
                        n = HALF * g + b
                        if w == 1:
                            dve.wait_ge(new_loaded, 48 * (p + 1))
                        dve.wait_ge(k_loaded[b], 128 * (2 * p + g + 1))
                        if w > 1:
                            me.need(me_last[0])
                        k = k_ring[:, b]
                        dve.tensor_tensor(prod.rearrange("p (j n) -> p j n", n=P), k, q_all[:, n:n + 1, :].broadcast_to([P, PAGES, P]), ALU.mult).then_inc(fv.sem, 1)
                        dve.wait_ge(fv.sem, fv.at(f"pr{n}", p))
                        me_last[0] = me.did(dve.tensor_reduce(lg[:, b, :, 0:PAGES].rearrange("p x j -> p j x"),
                                                 prod.rearrange("p (j x d) -> p j x d", x=2, d=DH), AX.X, ALU.add))
                    if i == HALF + 1:
                        me.need(me_last[0])
                        lo = slice(HALF * g, HALF * (g + 1))
                        me.did(dve.tensor_tensor(lg[:, :, :, 0:PAGES], lg[:, :, :, 0:PAGES],
                                                 bias[:, lo, 2 * p:2 * p + 2, :] if static else bias[:, lo, bass.DynSlice(2 * p, 2), :], ALU.add))
                        new = prod[0:1, 0:HALF * P]
                        me.chain(dve.tensor_tensor(new.rearrange("p (b n) -> p b n", n=P), k_new[:, lo, :], q_all[0:1, lo, :], ALU.mult))
                        me.chain(dve.tensor_reduce(lg[0:1, :, :, PAGES], new.rearrange("p (b x d) -> p b x d", x=2, d=DH), AX.X, ALU.add))
                        dve.tensor_reduce(top8[g], lg, AX.X, ALU.max).then_inc(fv.sem, 1)
                    if i == HALF + 2:
                        dve.wait_ge(top_all, 2 * p + g + 1)
                        if not (static and p == 0):
                            pe(f"dec{g}", p - 1)
                        dve.tensor_tensor(expd[g].rearrange("p (n j) -> p n j", j=9), lgt[g].rearrange("p (n j) -> p n j", j=9),
                                          m_all[g].unsqueeze(2).broadcast_to([P, 8, 9]), ALU.subtract).then_inc(fv.sem, 1)
                    if w == 5 and nxt:
                        scale_w(dve, w_qg, gain_b, p + 1, w_qg_loaded, w_qg_scaled)
                    if w == 13 and nxt2:
                        scale_w(dve, w_kv, gain_kv, p + 2, w_kv_loaded, w_kv_scaled)
                smp_out(1)
                pe("og0")
                dve.sem_inc(end_go_v, 1)
                dve.tensor_copy(o_cols(p, 0), bank[2]).then_inc(fv.sem, 1)

            me_last = [0]
            me.straight()
            scale_w(dve, w_kv, gain_kv, 1, w_kv_loaded, w_kv_scaled)
            pair(0, True, True)
            me.straight()
            PER = len(FOX_STEPS)
            with dve.Fori(1, PAIRS - 2) as p:
                me.enter(p - 1, PER)
                pair(p, True, True)
                me.leave(PER, PAIRS - 3)
            pair(PAIRS - 2, True, False)
            me.straight()
            pair(PAIRS - 1, False, False)
            me.straight()

            dve.wait_ge(fa.sem, fa.at("ogc1", PAIRS - 1))
            dve.wait_ge(fv.sem, fv.at("ogc0", PAIRS - 1))

            def tile_b(i, par):
                t = 2 * i + par
                static = isinstance(t, int)
                rows = S if static and t == TT else P
                if not (static and t < 2):
                    dve.wait_ge(yb_done, 2 * (t - 1))
                dve.sem_inc(end_go_v, 1)
                dve.tensor_copy(o_tile[par][:, :, 0:rows], o_t[:, :, cols(t)] if static else o_t[:, :, bass.DynSlice(t * P, P)])\
                   .then_inc(yb_v.sem, 1)
                dve.wait_ge(resb_loaded[par], 16 * (i + 1))
                for j in range(2):
                    dve.wait_ge(yb_done, 2 * t + j + 1)
                    dve.tensor_tensor(res[par][0:rows, 512 * j:512 * j + 512], res[par][0:rows, 512 * j:512 * j + 512],
                                      bank[2 * par + j][0:rows], ALU.add).then_inc(yb_v.sem, 1)
            tile_b(0, 0)
            tile_b(0, 1)
            with dve.Fori(1, TT // 2) as i:
                tile_b(i, 0)
                tile_b(i, 1)
            tile_b(TT // 2, 0)

        @block.tensor
        def _(pe):
            pe.wait_ge(built.sem, built.at("masks"))
            for t in range(TT + 1):
                rows = P if t < TT else S
                pe.wait_ge(x_scaled, t + 1)
                if t >= 2:
                    pe.wait_ge(x_ready, 2 * (t - 1))
                for k in range(KT):
                    ins = pe.transpose(bank[2 + 2 * (t % 2) + k // 4][:, k % 4 * P:k % 4 * P + rows],
                                       x_in[t % 2][0:rows, k * P:(k + 1) * P], ident[0:rows, 0:rows])
                    if k % 4 == 3:
                        ins.then_inc(x_turned, 1)
            pe.wait_ge(x_ready, 2 * (TT + 1))

            def proj(i, par, g):
                h = 2 * i + par
                first = isinstance(h, int) and h == 0
                if g == 0:
                    pe.wait_ge(w_a_loaded[par], 64 * (i + 1))
                if not (first and g < 2):
                    pe.wait_ge(proj_taken.sem, 12 * h + g - 1)
                dst = bank[g % 2]
                if g < 9:
                    for k in range(KT):
                        ins = pe.matmul(dst[:, 0:W3], w_a[:, par, k, g // 3, :], x_t[:, k, g % 3 * W3:(g % 3 + 1) * W3],
                                        start=(k == 0), stop=(k == KT - 1))
                else:
                    for t in range(4 * (g - 9), 4 * (g - 8)) if g < 11 else (TT,):
                        rows = P if t < TT else S
                        for k in range(KT):
                            ins = pe.matmul(dst[0:rows, t % 4 * P:(t % 4 + 1) * P], x_t[:, k, cols(t)],
                                            w_a[:, par, k, 3, :], start=(k == 0), stop=(k == KT - 1))
                ins.then_inc(proj_done.sem, 1)

            def head(i, par, nxt):
                h = 2 * i + par

                def v(name, hh=None):
                    pe.wait_ge(vecs.sem, vecs.at(name, h if hh is None else hh))

                def group(g):
                    if nxt:
                        proj(i + par, 1 - par, g)

                def level(w):
                    l = LEVELS.index(w)
                    v(f"fact{w}")
                    pe.wait_ge(lv_taken_v, 8 * h + l + 1)
                    f = fact[l % 2]
                    for t in range(TT):
                        q = f[:, t * P:(t + 1) * P].rearrange("p (b w) -> p b w", w=2 * w)[:, :, w:2 * w]
                        ins = pe.matmul(bank[2 + l % 2][:, t * C:(t + 1) * C], f[:, t * P:(t + 1) * P], q,
                                        start=True, stop=True)
                    ins.then_inc(lv_done.sem, 1)

                group(0)
                pe.wait_ge(acts.sem, acts.at("k", h))
                v("o_all", h - 1)
                pe.transpose(bank[6][0:S, P:2 * P], k_h[:, T:N], ident).then_inc(smp_done.sem, 1)
                v("v_diag")
                for j in range(2):
                    pe.wait_ge(uu_taken_v, 6 * h + 5 + j)
                    pe.matmul(bank[4 + j][:, :], k_smp[0:S, :], v_diag[0:S, 4 * j:4 * j + 4, :],
                              start=True, stop=True).then_inc(uu_done.sem, 1)
                group(1)
                v("q")
                for j in range(2):
                    pe.wait_ge(lv_taken_a, 2 * h + 1 + j)
                    for t in range(4 * j, 4 * j + 4):
                        ins = pe.matmul(bank[2 + j][:, t % 4 * P:(t % 4 + 1) * P], k_h[:, cols(t)], q_h[:, cols(t)],
                                        start=True, stop=True)
                    ins.then_inc(lv_done.sem, 1)
                v("s_smp")
                for b in range(S):
                    ins = pe.matmul(bank[6][:, b:b + 1], s_smp[:, b, :], q_h[:, T + b:T + b + 1],
                                    start=True, stop=True)
                ins.then_inc(smp_done.sem, 1)
                group(2)
                level(32)
                group(3)
                level(16)
                group(4)
                level(8)
                group(5)
                pe.wait_ge(acts.sem, acts.at("sq_smp", h))
                pe.matmul(bank[6][:, 16:16 + S], ones_mean, sq_smp, start=True, stop=True)\
                  .then_inc(smp_done.sem, 1)
                level(4)
                group(6)
                level(2)
                for j in range(2):
                    pe.wait_ge(uu_taken_v, 6 * h + 7 + j)
                    for t in range(4 * j, 4 * j + 4):
                        ins = pe.transpose(bank[4 + j][:, t % 4 * P:(t % 4 + 1) * P], k_dec[:, cols(t)], ident)
                    ins.then_inc(uu_done.sem, 1)
                group(7)
                level(1)
                for j in range(4):
                    if j < 2:
                        pe.wait_ge(uu_taken_a, 2 * h + 1 + j)
                        if j == 0:
                            pe.wait_ge(uu_taken_a, 2 * h + 2)
                    else:
                        pe.wait_ge(uu_taken_v, 6 * h + 7 + j)
                    for n in range(4):
                        c = 8 * (j // 2) + 2 * n + j % 2
                        rows = slice(c % 2 * C, (c % 2 + 1) * C)
                        ins = pe.matmul(bank[4 + j % 2][:, n * P:(n + 1) * P], k_dec_tok[rows, c // 2, :],
                                        v_tok[par][rows, c // 2, :], start=True, stop=True)
                    ins.then_inc(uu_done.sem, 1)
                group(8)
                v("s_all")
                pe.wait_ge(acts.sem, acts.at("ln_smp", h))
                for t in range(TT):
                    dst = bank[6 + t // 4][:, t % 4 * P:(t % 4 + 1) * P]
                    pe.matmul(dst, v_tok[par][:, t, :], att[:, cols(t)], start=True, stop=False, skip_group_check=True)
                    for c in (2 * t, 2 * t + 1):
                        if c:
                            ins = pe.matmul(dst[:, c % 2 * C:(c % 2 + 1) * C], s_all[:, c - 1, :],
                                            q_dec[:, c * C:(c + 1) * C], start=False, stop=(c % 2 == 1),
                                            skip_group_check=True)
                    if t % 4 == 3:
                        ins.then_inc(ob_done.sem, 1)
                group(9)
                group(10)
                for j in range(2):
                    pe.wait_ge(acts.sem, acts.at(f"sq{j}", h))
                    pe.wait_ge(lv_taken_v, 8 * h + 7 + j)
                    pe.matmul(bank[2 + j][:, :], ones_mean, o_sq[:, 512 * j:512 * j + 512], start=True,
                              stop=True).then_inc(lv_done.sem, 1)
                group(11)

            for g in range(12):
                proj(0, 0, g)
            with pe.Fori(0, LAST) as i:
                head(i, 0, True)
                head(i, 1, True)
            head(LAST, 0, True)
            head(LAST, 1, False)

            pe.wait_ge(w_o_loaded, 16)
            pe.wait_ge(vecs.sem, vecs.at("o_all", AH - 1))

            def y_tile(i, par, marks, done):
                t = 2 * i + par
                static = isinstance(t, int)
                rows = S if static and t == TT else P
                pe.wait_ge(marks.sem, marks.at("o", t))
                for j in range(2):
                    for h in range(AH):
                        ins = pe.matmul(bank[2 * par + j][0:rows, :], o_tile[par][:, h, 0:rows], w_o[:, h, 512 * j:512 * j + 512],
                                        start=(h == 0), stop=(h == AH - 1))
                    ins.then_inc(done, 1)

            def turn(i, par):
                t = 2 * i + par
                static = isinstance(t, int)
                rows = S if static and t == TT else P
                pe.wait_ge(tile_v.sem, tile_v.at("scaled", t))
                if not (static and t < 2):
                    pe.wait_ge(tile_a.sem, tile_a.at("h_t1", t) - 2 * len(tile_a.names))
                for k in range(KT):
                    ins = pe.transpose(bank[4 + 2 * par + k // 4][:, k % 4 * P:k % 4 * P + rows],
                                       h_sc[par][0:rows, k * P:(k + 1) * P], ident[0:rows, 0:rows])
                    if k % 4 == 3:
                        ins.then_inc(h_turned, 1)

            y_tile(0, 0, tile_v, y_done)
            y_tile(0, 1, tile_v, y_done)
            turn(0, 0)
            with pe.Fori(1, TT // 2) as i:
                y_tile(i, 0, tile_v, y_done)
                turn(i - 1, 1)
                y_tile(i, 1, tile_v, y_done)
                turn(i, 0)
            y_tile(TT // 2, 0, tile_v, y_done)
            turn(TT // 2 - 1, 1)
            turn(TT // 2, 0)

            pe.wait_ge(tile_a.sem, tile_a.at("h_t1", TT))
            pe.wait_ge(keys_v.sem, keys_v.at("w_f"))
            for n in range(3):
                for k in range(KT):
                    ins = pe.matmul(bank[n][0:BH, 0:W3], w_f[:, k, :], h_t[:, k, n * W3:(n + 1) * W3],
                                    start=(k == 0), stop=(k == KT - 1))
            ins.then_inc(keys_p.sem, 1)
            pe.wait_ge(keys_v.sem, keys_v.at("c"))
            for t in range(TT + 1):
                rows = P if t < TT else S
                ins = pe.transpose(bank[3][0:rows, t * BH:(t + 1) * BH], z16[0:BH, cols(t)], ident[0:BH, 0:BH])
                if t < TT:
                    ins = pe.transpose(bank[4][:, t * BH:(t + 1) * BH], c16[0:BH, cols(t)], ident[0:BH, 0:BH])
            ins.then_inc(keys_p.sem, 1)
            pe.wait_ge(lf_in, 16 * S * PAGES)
            pe.wait_ge(masks_b.sem, masks_b.at("later1"))
            for j in range(2):
                pe.matmul(bank[j], later, lf_pages[:, 512 * j:512 * j + 512], start=True, stop=True)
                ins = pe.matmul(bank[5 + j], ones_mean, lf_pages[:, 512 * j:512 * j + 512], start=True, stop=True)
            ins.then_inc(keys_p.sem, 1)
            pe.wait_ge(keys_v.sem, keys_v.at("done"))

            def half(p, c):
                t, rows = c % 9, P if c % 9 < TT else S
                if c % 9 == 0:
                    pe.wait_ge((w_kv_scaled, w_qg_scaled)[c // 9], p + 1)
                if not (isinstance(p, int) and p == 0 and c < 2):
                    pe.wait_ge(pj_taken, 18 * p + c - 1)
                w = (w_kv, w_qg)[c // 9]
                for k in range(KT):
                    ins = pe.matmul(bank[c % 2][0:rows, 0:2 * P], h_t[:, k, cols(t)], w[:, k, :, :],
                                    start=(k == 0), stop=(k == KT - 1))
                ins.then_inc(pj_done, 1)

            for c in range(18):
                half(0, c)

            def pair(p, nxt):
                static = isinstance(p, int)

                def v(name, q=None):
                    pe.wait_ge(fv.sem, fv.at(name, p if q is None else q))

                def a(name):
                    pe.wait_ge(fa.sem, fa.at(name, p))

                v("kq")
                if not (static and p == 0):
                    pe.wait_ge(fv.sem, fv.at("ogc0", p - 1))
                    pe.wait_ge(fa.sem, fa.at("ogc1", p - 1))
                for t in range(TT):
                    if t >= 4:
                        (v if t % 2 == 0 else a)(f"kqc{t - 4}")
                    for x in range(4):
                        ins = pe.transpose(bank[2 + t % 4][0:DH + 1, x * P:(x + 1) * P], raw[:, t, x * (DH + 1):(x + 1) * (DH + 1)], ident)
                    ins.then_inc(fp.sem, 1)
                v("g")
                pe.sem_inc(pe_go, 1)
                pe.transpose(bank[7][:, 0:S], g_cur[0:S, TT, :], ident[0:S, 0:S]).then_inc(fp.sem, 1)
                v(f"kqc{TT - 2}")
                a(f"kqc{TT - 1}")

                def logits(w):
                    hd, i, x = w // TT, w % TT, w % 2
                    if w >= 2:
                        v(f"nm{w - 2}")
                    for j in range(0, i + 1, 4):
                        n = min(4, i + 1 - j)
                        ins = pe.matmul(bank[2 + 2 * x + j // 4][:, 0:n * P], kq_t[0:DH + 1, 2 + hd, cols(i)],
                                        kq_t[0:DH + 1, hd, j * P:(j + n) * P], start=True, stop=True)
                    ins.then_inc(fp.sem, 1)

                def decode(g):
                    a(f"de{g}")
                    pe.wait_ge(fa.sem, fa.at(f"ptc{8 * g + 7}", p))
                    e = expd[g].rearrange("p (b x j) -> p b x j", x=2, j=9)
                    pe.matmul(bank[7][:, 16:16 + 72], ones_mean, expd[g], start=True, stop=True, skip_group_check=True)
                    for b in range(HALF):
                        pe.wait_ge(v_loaded[b], 128 * (2 * p + g + 1))
                        dst = bank[7][:, P + 2 * b:P + 2 * b + 2]
                        for j in range(PAGES):
                            pe.matmul(dst, v_ring[:, b, j, :], e[:, b, :, j], start=(j == 0), stop=False, skip_group_check=True)
                        ins = pe.matmul(dst, v_new[:, HALF * g + b, :], e[0:1, b, :, PAGES], start=False, stop=True, skip_group_check=True)
                    ins.then_inc(fp.sem, 1)

                logits(0)
                for w in range(ITEMS):
                    hd, i, x = w // TT, w % TT, w % 2
                    a(f"ex{w}")
                    for j in range(0, i + 1, 4):
                        if j == 0:
                            v(f"ptc{w - 1}" if w else "g_smp")
                        else:
                            last = {4: "g_smp", 12: "od0"}.get(w)
                            v(last) if last else a(f"ptc{w - 1}")
                        for n in range(j, min(j + 4, i + 1)):
                            ins = pe.transpose(bank[6 + j // 4][:, n % 4 * P:(n % 4 + 1) * P], prob[x][:, n * P:(n + 1) * P], ident)
                        ins.then_inc(fp.sem, 1)
                    if w + 1 < ITEMS:
                        logits(w + 1)
                    if nxt:
                        half(p + 1, w)
                    v(f"ptc{w}")
                    if i >= 4:
                        a(f"ptc{w}")
                    for n in range(i + 1):
                        ins = pe.matmul(bank[2 + 2 * x][:, 0:DH], prob_t[x][:, n * P:(n + 1) * P],
                                        v_cur[:, n, hd * DH:(hd + 1) * DH], start=(n == 0), stop=(n == i))
                    ins.then_inc(fp.sem, 1)
                    if i == TT - 1:
                        decode(w // TT)
                if nxt:
                    half(p + 1, 16)
                    half(p + 1, 17)
                v(f"nm{ITEMS - 1}")
                for j in range(2):
                    for t in range(4 * j, 4 * j + 4):
                        ins = pe.transpose(bank[2 + j][:, t % 4 * P:(t % 4 + 1) * P], og[:, t, :], ident)
                    ins.then_inc(fp.sem, 1)

            pair(0, True)
            with pe.Fori(1, PAIRS - 1) as p:
                pair(p, True)
            pair(PAIRS - 1, False)

            pe.wait_ge(w_ob_loaded, 16)
            pe.wait_ge(fv.sem, fv.at("ogc0", PAIRS - 1))
            pe.wait_ge(fa.sem, fa.at("ogc1", PAIRS - 1))

            def yb_free(t):
                pe.wait_ge(yb_v.sem, yb_v.at("y1", t) - 2 * len(yb_v.names))
            y_tile(0, 0, yb_v, yb_done)
            y_tile(0, 1, yb_v, yb_done)
            with pe.Fori(1, TT // 2) as i:
                yb_free(2 * i)
                y_tile(i, 0, yb_v, yb_done)
                yb_free(2 * i + 1)
                y_tile(i, 1, yb_v, yb_done)
            yb_free(TT)
            y_tile(TT // 2, 0, yb_v, yb_done)


_OUTS = [("y_prompt", (1, T, D)), ("y_sample", (S, 1, D)), ("state_prompt", (1, 1, AH, P, P)),
         ("state_sample", (1, S, AH, P, P)), ("k_prompt", (1, T, BH, DH)), ("k_sample", (S, 1, BH, DH)),
         ("v_prompt", (1, T, BH, DH)), ("v_sample", (S, 1, BH, DH)), ("logf_prompt", (1, T, BH)),
         ("logf_sample", (S, 1, BH))]


def kernel(**inputs):
    import numpy as np
    import concourse.bacc as bacc
    from concourse.bass_utils import run_bass_kernel_spmd

    nc = bacc.Bacc("TRN2", target_bir_lowering=False, num_devices=1)
    arrays, io = {}, {}
    for name, a in inputs.items():
        a = np.ascontiguousarray(a)
        arrays[f"in_{name}"] = a
        io[name] = nc.dram_tensor(f"in_{name}", a.shape, mybir.dt.from_np(a.dtype), kind="ExternalInput").ap()
    for name, shape in _OUTS:
        io[name] = nc.dram_tensor(f"out_{name}", shape, F32, kind="ExternalOutput").ap()
    build(nc, io)
    r = run_bass_kernel_spmd(nc, [arrays], core_ids=[0])
    return tuple(r.results[0][f"out_{name}"] for name, _ in _OUTS)
```

```python
from contextlib import ExitStack

import concourse.bass as bass
from concourse import mybir

F32 = mybir.dt.float32
BF16 = mybir.dt.bfloat16
I32 = mybir.dt.int32
ALU = mybir.AluOpType
ACT = mybir.ActivationFunctionType
AX = mybir.AxisListType

P = 128
EPS = 1e-6


class Steps:

    def __init__(self, eng, sem):
        self.eng, self.sem, self.start, self.base, self.n = eng, sem, 0, 0, 0

    def did(self, ins):
        ins.then_inc(self.sem, 1)
        self.n += 1
        return self.base + self.n

    def need(self, mark):
        self.eng.wait_ge(self.sem, mark)

    def chain(self, ins):
        self.need(self.did(ins))

    def enter(self, i, per):
        self.start = self.start + self.n
        self.base, self.n = self.start + i * per, 0

    def leave(self, per, times):
        assert self.n == per, (self.n, per)
        self.start, self.n = self.start + per * times, 0
        self.base = self.start

    def straight(self):
        self.start = self.start + self.n
        self.base, self.n = self.start, 0


class Marks:

    def __init__(self, sem, *names, ahead=0):
        self.sem, self.names, self.ahead = sem, names, ahead
        self.index = {n: i + 1 for i, n in enumerate(names)}
        assert len(self.index) == len(names)

    def at(self, name, r=0):
        return r * len(self.names) + self.index[name] + self.ahead


D = 1024
T = 1024
S = 8
N = T + S
KT = D // P
TT = T // P
W3 = N // 3
AH = 8
C = 64
NC = T // C
LEVELS = (32, 16, 8, 4, 2, 1)
BH = 16
DH = 64
PAIRS = BH // 2
PAGES = 8
PAGE = 128
RAW = 4 * (DH + 1) + 2 * P
HALF = S // 2
ITEMS = 2 * TT
LOW = -3e38
FILL = (2, 2, 1, 1, 1, 1, 1, 1, 2, 2, 1, 1, 1, 1)
SLOTS = 28


W_COL = (1, 0, 3, 2)
LAST = AH // 2 - 1


def build(nc, io):
    with ExitStack() as ctx:
        def sem(name):
            return ctx.enter_context(nc.semaphore(name))

        WORDS = 53200
        arena = ctx.enter_context(nc.sbuf_tensor("arena", [P, WORDS], F32))
        psum = ctx.enter_context(nc.psum_tensor("psum", [P, 8 * 512], F32))
        bank = [psum[:, 512 * i:512 * (i + 1)] for i in range(8)]
        used = [0]

        def area(words):
            at = used[0]
            used[0] += words
            assert used[0] <= WORDS, used[0]
            return arena[:, at:at + words]

        ident = area(P)
        ones_mean = area(P)
        spare_at = used[0]
        level_mask = area(len(LEVELS) * C)
        chunk_keep = area(T // 2).bitcast(BF16)
        gain_a = area(KT)
        gain_o = area(1)
        lb_in, one_lb, inv_lb, inv_h = area(AH), area(AH), area(AH), area(1)
        eps = area(1)
        msq, rstd = area(TT + 1), area(TT + 1)
        lb_e, lb_r = area(AH), area(AH)

        x_t = area(KT * N).rearrange("p (k n) -> p k n", n=N)
        w_a_at = used[0]
        w_a = area(2 * KT * 4 * P).rearrange("p (s k y n) -> p s k y n", s=2, y=4, n=P)
        o_t = area(AH * N).rearrange("p (h n) -> p h n", n=N)
        temps = used[0]
        raw_f, raw_q, raw_g = area(N), area(N), area(N)
        t0, t1, t2, t3 = area(N), area(N), area(N), area(N)
        k_h, q_h, sg_h, logf, cum, q_dec = area(N), area(N), area(N), area(N), area(T), area(T)
        k_dec = logf[:, 0:T]
        diffs, facts = area(2 * T), area(2 * T)
        diff = [diffs[:, 0:T], diffs[:, T:2 * T]]
        fact = [facts[:, 0:T], facts[:, T:2 * T]]
        o_sq, o_rs = diffs[:, 0:N], facts[:, 0:N]
        att = area(T)
        v_tok = [area((TT + 1) * P).rearrange("p (t v) -> p t v", v=P) for _ in range(2)]
        k_dec_tok = area(T).rearrange("p (t k) -> p t k", k=P)
        s_all = area(NC * P).rearrange("p (c v) -> p c v", v=P)
        s_smp = area(S * P).rearrange("p (b v) -> p b v", v=P)
        v_diag = area(S * P).rearrange("p (b v) -> p b v", v=P)
        k_smp, o_smp, f_smp, dec = area(P), area(S), area(S), area(NC)
        sq_smp, rs_smp = area(S), area(S)
        x_in = [facts[:, 0:D], facts[:, T:T + D]]
        x_sq = [diffs[:, 0:D], diffs[:, T:T + D]]

        end_a = used[0]

        h_t = x_t
        w_o = arena[:, w_a_at:w_a_at + AH * D].rearrange("p (h n) -> p h n", n=D)
        used[0] = temps
        o_tile = [area(AH * P).rearrange("p (h n) -> p h n", n=P) for _ in range(2)]
        res, h_new, h_sc = [area(D), area(D)], [area(D), area(D)], [area(D), area(D)]
        h_sq = area(D)
        assert used[0] <= temps + 9 * 1024

        used[0] = temps
        raw = area((TT + 1) * RAW).rearrange("p (t c) -> p t c", c=RAW)
        kq_t = area(4 * T).rearrange("p (x n) -> p x n", n=T)
        ssq, rs_kq = area((TT + 1) * 4), area((TT + 1) * 4)
        top, total, r_total = area(16), area(16), area(16)
        expd = [area(HALF * 2 * 9) for _ in range(2)]
        top8, m_all, den, o_two, g_smp = [area(8), area(8)], [area(8), area(8)], area(8), area(8), area(S)
        assert used[0] <= temps + 9 * 1024
        used[0] = temps + 9 * 1024
        w_kv = area(KT * 2 * P).rearrange("p (k y n) -> p k y n", y=2, n=P)
        w_qg = area(KT * 2 * P).rearrange("p (k y n) -> p k y n", y=2, n=P)
        bias = area(S * BH * PAGES).rearrange("p (b h j) -> p b h j", h=BH, j=PAGES)
        gain_kv, gain_b = area(KT), area(KT)
        pages = area(S * PAGES).bitcast(I32)
        after = used[0]
        v_cur = area((TT + 1) * P).rearrange("p (t v) -> p t v", v=P)
        g_cur = area((TT + 1) * P).rearrange("p (t v) -> p t v", v=P)
        prob, prob_t = [area(T), area(T)], [area(T), area(T)]
        q_all = area(S * P).rearrange("p (b n) -> p b n", n=P)
        prod = area(PAGES * P)
        og = area(TT * P).rearrange("p (t v) -> p t v", v=P)
        kv_new = area(2 * S * P)
        k_new = kv_new[0:1, 0:S * P].rearrange("p (b n) -> p b n", n=P)
        v_new = kv_new[0:1, S * P:2 * S * P].rearrange("p (b n) -> p b n", n=P)
        g_next = area((TT + 1) * P).rearrange("p (t v) -> p t v", v=P)
        trash = area(DH)
        assert used[0] <= WORDS, used[0]
        used[0] = spare_at
        gain_kq = area(4 * DH).rearrange("p (x d) -> p x d", d=DH)
        lf_tok, c_tok = area((TT + 1) * BH), area(TT * BH)
        causal = area(P)
        lgt = [area(HALF * 2 * 9) for _ in range(2)]
        assert used[0] <= spare_at + len(LEVELS) * C + T // 2
        k_ring = arena[:, w_a_at:w_a_at + 4 * PAGES * P].rearrange("p (s j n) -> p s j n", s=4, n=P)
        v_ring = arena[:, w_a_at + 4 * PAGES * P:w_a_at + 8 * PAGES * P].rearrange("p (s j n) -> p s j n", s=4, n=P)
        used[0] = after
        w_f = area(KT * BH).rearrange("p (k n) -> p k n", n=BH)
        z16, a16, one16, c16, b_f = area(N), area(N), area(T), area(T), area(1)
        lf_pages = area(S * PAGES * BH)
        later, lf_new = area(P), area(S * BH)
        acc = area(S * BH).rearrange("p (b h) -> p b h", h=BH)
        assert used[0] <= WORDS, used[0]
        h_dram = nc.dram_tensor("h_rows", [N, D], F32).ap()
        q_dram = nc.dram_tensor("q_rows", [PAIRS, S, P], F32).ap()

        consts_in = sem("consts_in")
        built = Marks(sem("built"), "ident0", "ones", "masks0", "keep0", "eps", "vdiag0", "ident", "masks1", "keep", "masks")
        consts_v = sem("consts_v")
        x_loaded = [sem("x_loaded0"), sem("x_loaded1")]
        x_scaled, x_turned, x_ready = sem("x_scaled"), sem("x_turned"), sem("x_ready")
        x_rstd = sem("x_rstd")
        lb_a = sem("lb_a")
        w_a_loaded = [sem("w_a_loaded0"), sem("w_a_loaded1")]
        state_loaded, state_stored, prompt_stored = sem("state_loaded"), sem("state_stored"), sem("prompt_stored")
        s_all_free = sem("s_all_free")
        merge_go, pool_go, sp_go = sem("merge_go"), sem("pool_go"), sem("sp_go")
        raw_set, end_go_v = sem("raw_set"), sem("end_go_v")
        act_steps, dve_steps = sem("act_steps"), sem("dve_steps")
        proj_done = Marks(sem("proj_done"), *range(12))
        lv_done = Marks(sem("lv_done"), "diag0", "diag1", *[f"level{l}" for l in LEVELS], "mean0", "mean1")
        smp_done = Marks(sem("smp_done"), "k_smp", "o_smp", "mean_smp")
        uu_done = Marks(sem("uu_done"), "outer0", "outer1", "turn0", "turn1", "upd0", "upd1", "upd2", "upd3")
        ob_done = Marks(sem("ob_done"), "o0", "o1")
        proj_taken = Marks(sem("proj_taken"), *range(12))
        lv_taken_v, lv_taken_a = sem("lv_taken_v"), sem("lv_taken_a")
        uu_taken_v, uu_taken_a = sem("uu_taken_v"), sem("uu_taken_a")
        acts = Marks(sem("acts"), "ln_f", "ln_q", "ln_g", "k", "sig_q", "exp32", "decays", "exp_cum", "sig_g", "exp16",
                     "exp8", "exp4", "sq_smp", "exp_kd", "exp2", "ln_smp", "exp1", "sq0", "sq1", "dev")
        vecs = Marks(sem("vecs"), "abs_f", "abs_q", "abs_g", "logf", "k_in", "cum", "q_in", "diff32", "g_in", "q",
                     "fact32", "diff16", "sg", "diff_kd", "k_smp", "fact16", "diff8", "v_diag", "q_dec", "s_smp",
                     "fact8", "diff4", "o_smp", "fact4", "diff2", "k_dec", "fact2", "diff1", "fact1",
                     "att_all", "s_all", "o_all", ahead=1)
        w_o_loaded, res_loaded, h_stored = sem("w_o_loaded"), [sem("res_loaded0"), sem("res_loaded1")], [sem("h_stored0"), sem("h_stored1")]
        o_set, tile_v = sem("o_set"), Marks(sem("tile_v"), "new0", "new1", "scaled")
        tile_a = Marks(sem("tile_a"), "rstd", "h_t0", "h_t1")
        y_done, h_turned = sem("y_done"), sem("h_turned")
        keys_in, pages_in, lf_in, lf_new_in = sem("keys_in"), sem("pages_in"), sem("lf_in"), sem("lf_new_in")
        lf_stored = sem("lf_stored")
        keys_p = Marks(sem("keys_p"), "z", "turned", "suffix")
        keys_v = Marks(sem("keys_v"), "w_f", "abs", "lf", "c", "tok", "done")
        keys_a = Marks(sem("keys_a"), "ln")
        masks_b = Marks(sem("masks_b"), "zero", "causal", "later", "raw", "low0", "low1", "causal1", "later1")
        w_kv_loaded, w_qg_loaded = sem("w_kv_loaded"), sem("w_qg_loaded")
        w_kv_scaled, w_qg_scaled = sem("w_kv_scaled"), sem("w_qg_scaled")
        pj_done, pj_taken = sem("pj_done"), sem("pj_taken")
        k_loaded, v_loaded = [sem(f"k_loaded{i}") for i in range(4)], [sem(f"v_loaded{i}") for i in range(4)]
        kv_stored, q_stored, new_loaded, v_new_loaded, top_all = sem("kv_stored"), sem("q_stored"), sem("new_loaded"), sem("v_new_loaded"), sem("top_all")
        order_p, order_v, order_a = [], [], []
        for w in range(ITEMS):
            order_p += ["g_smp"] * (w == 1)
            order_v += ["g_smp"] * (w == 1)
            order_p += [f"pt{w}_0"] + [f"pt{w}_1"] * (w % TT >= 4) + [f"qk{w + 1}"] * (w + 1 < ITEMS) + [f"pv{w}"]
            order_v += [f"ptc{w}"] + [f"mx{w + 1}"] * (w + 1 < ITEMS) + [f"nm{w}"]
            order_v += [f"pr{w // TT * HALF + w % TT - 1}"] * (1 <= w % TT <= HALF)
            order_v += [f"lg{w // TT}"] * (w % TT == HALF + 1) + [f"df{w // TT}"] * (w % TT == TT - 1)
            order_a += [f"ptc{w}"] * (w % TT >= 4) + [f"ex{w + 1}"] * (w + 1 < ITEMS)
        fp = Marks(sem("fox_p"), *order_p, "qk_next", ahead=1)
        fv = Marks(sem("fox_v"), *order_v, "mx_next", ahead=1)
        fa = Marks(sem("fox_a"), *order_a, "ex_next", ahead=1)
        prep_v = Marks(sem("prep_v"), "k", "abs_g", "q", "g_in", "g")
        prep_a = Marks(sem("prep_a"), "rs_k", "rs_q", "ln_g", "sig_g", "v_cur")
        dec_ready, dec_done, od_done = sem("dec_ready"), sem("dec_done"), sem("od_done")
        w_ob_loaded, resb_loaded, y_stored = sem("w_ob_loaded"), [sem("resb_loaded0"), sem("resb_loaded1")], [sem("y_stored0"), sem("y_stored1")]
        yb_done, ob_set, yb_v = sem("yb_done"), sem("ob_set"), Marks(sem("yb_v"), "y0", "y1")
        pe_go, end_go = sem("pe_go"), sem("end_go")

        block = ctx.enter_context(nc.Block())

        w_in_a = io["w_in_a"].rearrange("l (k p) (y h n) -> p k y (l h) n", p=P, y=4, n=P)
        x_prompt = io["x_prompt"].rearrange("b (t p) d -> (b t) p d", p=P)
        x_sample = io["x_sample"].rearrange("b s d -> (b s) d")
        state_in = io["state_hgrn"].rearrange("l b h k v -> (l h) k b v")
        state_out = io["state_sample"].rearrange("l b h k v -> (l h) k b v")
        prompt_out = io["state_prompt"].rearrange("l b h k v -> (l b h) k v")

        def cols(t):
            return slice(t * P, t * P + (P if t < TT else S))

        def load_w(sp, i, par):
            for y in range(4):
                sp.dma_start(w_a[:, par, :, y, :], w_in_a[:, :, W_COL[y], 2 * i + par, :]).then_inc(w_a_loaded[par], 16)

        w_kv_d = io["w_kv"].rearrange("(k p) (y h n) -> p k y h n", p=P, y=2, n=P)
        w_qg_d = io["w_in_b"].rearrange("l (k p) (y h n) -> p k y (l h) n", p=P, y=2, n=P)
        k_cache = io["cache_k"].rearrange("g s (x h) d -> g s x (h d)", h=2)
        v_cache = io["cache_v"].rearrange("g s (x h) d -> g s x (h d)", h=2)
        lf_cache = io["cache_logf"]
        n_pool = lf_cache.shape[0]

        def o_cols(p, j):
            if isinstance(p, int):
                return o_t[:, p, 512 * j:512 * j + 512]
            return o_t[:, bass.DynSlice(p, 1), 512 * j:512 * j + 512].rearrange("p a n -> p (a n)")

        def scale_w(dve, w, gain, p, loaded, scaled):
            dve.wait_ge(loaded, 32 * (p + 1))
            dve.tensor_tensor(w, w, gain.unsqueeze(2).unsqueeze(3).broadcast_to([P, KT, 2, P]), ALU.mult).then_inc(scaled, 1)

        def load_wb(sp, dst, src, p, loaded):
            for y in range(2):
                sp.dma_start(dst[:, :, y, :], src[:, :, y, p, :]).then_inc(loaded, 16)

        OUT_TAKEN = SLOTS * PAIRS + 2

        def page_id(sp, n):
            at = pages[0:1, n:n + 1] if isinstance(n, int) else pages[0:1, bass.DynSlice(n, 1)]
            return sp.value_load(at, min_val=0, max_val=n_pool - 1)

        @block.sync
        def _(sp):
            sp.dma_start(gain_a, io["norm_in"][0].rearrange("(k p) -> p k", p=P), allow_slow_non_contiguous=True).then_inc(consts_in, 16)
            sp.dma_start(gain_o, io["g_norm_a"].rearrange("l p -> p l"), allow_slow_non_contiguous=True).then_inc(consts_in, 16)
            sp.dma_start(lb_in, io["lb_logits"].rearrange("l (h p) -> p (l h)", p=P), allow_slow_non_contiguous=True).then_inc(consts_in, 16)
            for t in range(TT + 1):
                rows = P if t < TT else S
                if t >= 2:
                    sp.wait_ge(x_turned, 2 * (t - 1))
                sp.dma_start(x_in[t % 2][0:rows], x_prompt[t] if t < TT else x_sample).then_inc(x_loaded[t % 2], 16)
                if t < 2:
                    load_w(sp, 0, t)

            def body(i):
                for par in range(2):
                    sp.wait_ge(proj_done.sem, proj_done.at(11, 2 * i + par))
                    load_w(sp, i + 1, par)

            with sp.Fori(0, LAST) as i:
                body(i)

            sp.wait_ge(proj_done.sem, proj_done.at(11, AH - 1))
            sp.dma_start(w_o, io["w_o_a"][0].rearrange("(h p) n -> p h n", p=P)).then_inc(w_o_loaded, 16)
            sp.wait_ge(vecs.sem, vecs.at("o_all", AH - 1))
            sp.dma_start(pages[0:1, :], io["page_table"].rearrange("(o b) j -> o (b j)", o=1)).then_inc(pages_in, 16)

            LF_STEP = S * PAGES // (TT // 2 - 1)

            def res_in(i, par):
                t = 2 * i + par
                sp.wait_ge(tile_v.sem, tile_v.at("new1", t) - 2 * len(tile_v.names)) if not (isinstance(t, int) and t < 2) else None
                sp.sem_inc(sp_go, 1)
                src = x_sample if isinstance(t, int) and t == TT else x_prompt[t]
                sp.dma_start(res[par][0:src.shape[0]], src).then_inc(res_loaded[par], 16)

            res_in(0, 0)
            res_in(0, 1)
            load_wb(sp, w_kv, w_kv_d, 0, w_kv_loaded)
            load_wb(sp, w_qg, w_qg_d, 0, w_qg_loaded)
            with nc.allow_non_contiguous_dma(reason="small constants"):
                sp.dma_start(gain_kv, io["norm_kv"].rearrange("(k p) -> p k", p=P)).then_inc(keys_in, 16)
                sp.dma_start(gain_b, io["norm_in"][1].rearrange("(k p) -> p k", p=P)).then_inc(keys_in, 16)
                sp.dma_start(b_f[0:BH], io["b_fgate"].rearrange("(h o) -> h o", o=1)).then_inc(keys_in, 16)
            for x, g in enumerate((io["k_norm"], io["k_norm"], io["q_norm_b"][0], io["q_norm_b"][0])):
                sp.dma_start(gain_kq[:, x, :], g.partition_broadcast(P)).then_inc(keys_in, 16)
            sp.dma_start(w_f, io["w_fgate"].rearrange("(k p) n -> p k n", p=P)).then_inc(keys_in, 16)
            sp.wait_ge(pages_in, 16)
            with sp.Fori(1, TT // 2) as i:
                res_in(i, 0)
                res_in(i, 1)
                for n in range(LF_STEP):
                    at = (i - 1) * LF_STEP + n
                    page = page_id(sp, at)
                    sp.dma_start(lf_pages[:, bass.DynSlice(at * BH, BH)], lf_cache[page]).then_inc(lf_in, 16)
            res_in(TT // 2, 0)
            for at in range(LF_STEP * (TT // 2 - 1), S * PAGES):
                page = page_id(sp, at)
                sp.dma_start(lf_pages[:, at * BH:(at + 1) * BH], lf_cache[page]).then_inc(lf_in, 16)

            def k_in(p, g):
                for b in range(HALF):
                    for j in range(PAGES):
                        page = page_id(sp, (HALF * g + b) * PAGES + j)
                        sp.dma_start(k_ring[:, b, j, :], k_cache[page, :, p, :]).then_inc(k_loaded[b], 16)

            def v_in(p, g):
                for b in range(HALF):
                    for j in range(PAGES):
                        page = page_id(sp, (HALF * g + b) * PAGES + j)
                        sp.dma_start(v_ring[:, b, j, :], v_cache[page, :, p, :]).then_inc(v_loaded[b], 16)

            sp.wait_ge(y_done, 2 * (TT + 1))
            sp.sem_inc(sp_go, 1)
            k_in(0, 0)
            v_in(0, 0)
            sp.wait_ge(pj_done, TT + 1)
            load_wb(sp, w_kv, w_kv_d, 1, w_kv_loaded)
            sp.wait_ge(pj_done, 2 * (TT + 1))
            load_wb(sp, w_qg, w_qg_d, 1, w_qg_loaded)

            def pair(p, nxt, nxt2):
                sp.wait_ge(fv.sem, fv.at(f"pr{HALF - 1}", p))
                sp.sem_inc(sp_go, 1)
                k_in(p, 1)
                if nxt2:
                    sp.wait_ge(pj_done, SLOTS * (p + 1) + TT + 1)
                    sp.sem_inc(sp_go, 1)
                    load_wb(sp, w_kv, w_kv_d, p + 2, w_kv_loaded)
                sp.wait_ge(dec_done, 2 * p + 1)
                sp.sem_inc(sp_go, 1)
                v_in(p, 1)
                if nxt:
                    sp.wait_ge(fv.sem, fv.at(f"pr{S - 1}", p))
                    sp.sem_inc(sp_go, 1)
                    k_in(p + 1, 0)
                if nxt2:
                    sp.wait_ge(pj_done, SLOTS * (p + 1) + 18)
                    sp.sem_inc(sp_go, 1)
                    load_wb(sp, w_qg, w_qg_d, p + 2, w_qg_loaded)
                if nxt:
                    sp.wait_ge(dec_done, 2 * p + 2)
                    sp.sem_inc(sp_go, 1)
                    v_in(p + 1, 0)

            with sp.Fori(0, PAIRS - 2) as p:
                pair(p, True, True)
            pair(PAIRS - 2, True, False)
            pair(PAIRS - 1, False, False)

            sp.wait_ge(dec_done, 2 * PAIRS)
            sp.dma_start(w_o, io["w_o_b"][0].rearrange("(h p) n -> p h n", p=P)).then_inc(w_ob_loaded, 16)
            sp.wait_ge(pj_taken, OUT_TAKEN)
            sp.wait_ge(h_stored[0], 16 * (TT // 2 + 1))
            sp.wait_ge(h_stored[1], 16 * TT // 2)

            def resb_in(i, par):
                t = 2 * i + par
                rows = S if isinstance(t, int) and t == TT else P
                if not (isinstance(t, int) and t < 2):
                    sp.wait_ge(y_stored[par], 16 * i)
                sp.sem_inc(sp_go, 1)
                sp.dma_start(res[par][0:rows], h_dram[bass.DynSlice(t * P, rows)] if not isinstance(t, int) else
                             h_dram[t * P:t * P + rows]).then_inc(resb_loaded[par], 16)
            resb_in(0, 0)
            resb_in(0, 1)
            with sp.Fori(1, TT // 2) as i:
                resb_in(i, 0)
                resb_in(i, 1)
            resb_in(TT // 2, 0)

        k_out = io["k_prompt"].rearrange("b (t p) (g x) d -> p (b t) g x d", p=P, x=2)
        v_out = io["v_prompt"].rearrange("b (t p) (g x) d -> p (b t) g (x d)", p=P, x=2)
        ks_out = io["k_sample"].rearrange("b s (g x) d -> (b s) g x d", x=2)
        vs_out = io["v_sample"].rearrange("b s (g x) d -> (b s) g (x d)", x=2)
        y_rows = io["y_prompt"].rearrange("b (t p) d -> (b t) p d", p=P)

        @block.gpsimd
        def _(pool):
            pool.memset(ident, 0.0).then_inc(built.sem, 1)
            pool.memset(ones_mean, 1.0 / P).then_inc(built.sem, 1)
            pool.memset(level_mask, 1.0).then_inc(built.sem, 1)
            pool.memset(chunk_keep, 1.0).then_inc(built.sem, 1)
            pool.memset(eps, EPS).then_inc(built.sem, 1)
            pool.memset(v_diag, 0.0).then_inc(built.sem, 1)
            pool.wait_ge(built.sem, built.at("vdiag0"))
            pool.affine_select(out=ident, in_=ident, compare_op=ALU.not_equal, fill=1.0, base=0,
                               pattern=[[-1, P]], channel_multiplier=1).then_inc(built.sem, 1)
            for l, w in enumerate(LEVELS):
                m = level_mask[:, l * C:(l + 1) * C].rearrange("p (b w) -> p b w", w=w)
                last = pool.affine_select(out=m, in_=m, compare_op=ALU.is_ge, fill=0.0, base=0,
                                          pattern=[[-2 * w, C // w], [0, w]], channel_multiplier=1)
            last.then_inc(built.sem, 1)
            keep = chunk_keep.rearrange("p (c s) -> p c s", s=C)
            pool.affine_select(out=keep, in_=keep, compare_op=ALU.not_equal, fill=0.0, base=0,
                               pattern=[[0, NC], [1, C]], channel_multiplier=0).then_inc(built.sem, 1)
            pool.wait_ge(built.sem, built.at("masks1"))
            for l, w in enumerate(LEVELS):
                m = level_mask[:, l * C:(l + 1) * C].rearrange("p (b w) -> p b w", w=w)
                last = pool.affine_select(out=m, in_=m, compare_op=ALU.is_ge, fill=0.0, base=w - 1,
                                          pattern=[[2 * w, C // w], [0, w]], channel_multiplier=-1)
            last.then_inc(built.sem, 1)

            pool.sem_inc(s_all_free, 1)

            def head(h):
                pool.dma_start(s_smp, state_in[h]).then_inc(state_loaded, 16)
                pool.wait_ge(vecs.sem, vecs.at("s_smp", h))
                pool.sem_inc(pool_go, 1)
                pool.dma_start(state_out[h], s_smp).then_inc(state_stored, 16)
                pool.wait_ge(vecs.sem, vecs.at("s_all", h))
                pool.sem_inc(pool_go, 1)
                pool.dma_start(prompt_out[h], s_all[:, NC - 1, :]).then_inc(prompt_stored, 16)
                pool.wait_ge(smp_done.sem, smp_done.at("o_smp", h))
                pool.wait_ge(state_stored, 16 * (h + 1))
                pool.wait_ge(prompt_stored, 16 * (h + 1))
                pool.sem_inc(s_all_free, 1)
            with pool.Fori(0, AH) as h:
                head(h)
            pool.wait_ge(prompt_stored, 16 * AH)
            pool.wait_ge(vecs.sem, vecs.at("o_all", AH - 1))
            pool.memset(one16, 1.0).then_inc(masks_b.sem, 1)
            pool.memset(causal, 0.0).then_inc(masks_b.sem, 1)
            pool.memset(later, 1.0).then_inc(masks_b.sem, 1)
            pool.wait_ge(masks_b.sem, masks_b.at("later"))
            pool.sem_inc(masks_b.sem, 1)
            pool.memset(lgt[0], LOW).then_inc(masks_b.sem, 1)
            pool.memset(lgt[1], LOW).then_inc(masks_b.sem, 1)
            pool.affine_select(out=causal, in_=causal, compare_op=ALU.is_ge, fill=LOW, base=0,
                               pattern=[[-1, P]], channel_multiplier=1).then_inc(masks_b.sem, 1)
            pool.affine_select(out=later, in_=later, compare_op=ALU.is_gt, fill=0.0, base=0,
                               pattern=[[-1, P]], channel_multiplier=1).then_inc(masks_b.sem, 1)

            def h_out(i, par):
                t = 2 * i + par
                rows = S if isinstance(t, int) and t == TT else P
                pool.wait_ge(tile_v.sem, tile_v.at("new1", t))
                pool.sem_inc(pool_go, 1)
                pool.dma_start(h_dram[t * P:t * P + rows] if isinstance(t, int) else h_dram[bass.DynSlice(t * P, rows)],
                               h_new[par][0:rows]).then_inc(h_stored[par], 16)
            with pool.Fori(0, TT // 2) as i:
                h_out(i, 0)
                h_out(i, 1)
            h_out(TT // 2, 0)
            pool.wait_ge(h_stored[0], 16 * (TT // 2 + 1))
            pool.wait_ge(h_stored[1], 16 * TT // 2)
            pool.wait_ge(tile_a.sem, tile_a.at("h_t1", TT))
            pool.memset(raw, 0.0).then_inc(raw_set, 1)
            pool.memset(ssq, 0.0).then_inc(raw_set, 1)
            pool.wait_ge(raw_set, 2)
            pool.memset(raw[:, :, 0:4 * (DH + 1)].rearrange("p t (x d) -> p t x d", x=4)[:, :, 2:4, DH:DH + 1], 1.0).then_inc(raw_set, 1)

            pool.wait_ge(keys_v.sem, keys_v.at("tok"))
            lf = lf_tok.rearrange("p (t h) -> p t h", h=BH)
            pool.dma_start(io["logf_prompt"].rearrange("b (t p) h -> p (b t) h", p=P), lf[:, 0:TT, :]).then_inc(lf_stored, 16)
            pool.dma_start(io["logf_sample"].rearrange("b s h -> (b s) h"), lf[0:S, TT, :]).then_inc(lf_stored, 16)
            pool.wait_ge(lf_stored, 32)
            pool.dma_start(lf_new, io["logf_sample"].rearrange("b s h -> (b s h)").partition_broadcast(P)).then_inc(lf_new_in, 16)
            pool.wait_ge(lf_new_in, 16)

            def pair(p):
                if not isinstance(p, int) or p:
                    pool.wait_ge(fv.sem, fv.at("lg0", p - 1))
                    pool.sem_inc(pool_go, 1)
                    pool.partition_all_reduce(m_all[0], top8[0], P, bass.bass_isa.ReduceOp.max).then_inc(top_all, 1)
                pool.wait_ge(prep_v.sem, prep_v.at("k", p))
                pool.sem_inc(pool_go, 1)
                kk = raw[:, :, 0:2 * (DH + 1)].rearrange("p t (x d) -> p t x d", x=2)[:, :, :, 0:DH]
                qq = raw[:, :, 2 * (DH + 1):4 * (DH + 1)].rearrange("p t (x d) -> p t x d", x=2)[:, :, :, 0:DH]
                vv = raw[:, :, 4 * (DH + 1):4 * (DH + 1) + P]
                for x in range(2):
                    pool.dma_start(k_out[:, :, p, x, :], kk[:, 0:TT, x, :]).then_inc(kv_stored, 16)
                pool.dma_start(v_out[:, :, p, :], vv[:, 0:TT, :]).then_inc(kv_stored, 16)
                pool.dma_start(ks_out[:, p, :, :], kk[0:S, TT]).then_inc(kv_stored, 16)
                pool.dma_start(vs_out[:, p, :], vv[0:S, TT, :]).then_inc(kv_stored, 16)
                if not isinstance(p, int) or p:
                    pool.wait_ge(fv.sem, fv.at("lg1", p - 1))
                    pool.sem_inc(pool_go, 1)
                    pool.partition_all_reduce(m_all[1], top8[1], P, bass.bass_isa.ReduceOp.max).then_inc(top_all, 1)
                pool.wait_ge(kv_stored, 80 * (p + 1))
                pool.sem_inc(pool_go, 1)
                pool.dma_start(k_new, ks_out[:, p].rearrange("b x d -> b (x d)").unsqueeze(0)).then_inc(new_loaded, 16)
                pool.wait_ge(prep_v.sem, prep_v.at("q", p))
                pool.sem_inc(pool_go, 1)
                pool.dma_start(q_dram[p].rearrange("b (x d) -> b x d", x=2), qq[0:S, TT]).then_inc(q_stored, 16)
                pool.wait_ge(q_stored, 16 * (p + 1))
                pool.sem_inc(pool_go, 1)
                pool.dma_start(q_all, q_dram[p].rearrange("b n -> (b n)").partition_broadcast(P)).then_inc(new_loaded, 16)
                if not isinstance(p, int) or p:
                    pool.wait_ge(dec_done, 2 * p)
                    pool.sem_inc(pool_go, 1)
                pool.dma_start(v_new, vs_out[:, p, :].unsqueeze(0)).then_inc(v_new_loaded, 16)

            pair(0)
            with pool.Fori(1, PAIRS) as p:
                pair(p)
            for g in range(2):
                pool.wait_ge(fv.sem, fv.at(f"lg{g}", PAIRS - 1))
                pool.partition_all_reduce(m_all[g], top8[g], P, bass.bass_isa.ReduceOp.max).then_inc(top_all, 1)

            def y_out(i, par):
                t = 2 * i + par
                last = isinstance(t, int) and t == TT
                rows = S if last else P
                pool.wait_ge(yb_v.sem, yb_v.at("y1", t))
                pool.sem_inc(pool_go, 1)
                dst = io["y_sample"].rearrange("b s d -> (b s) d") if last else y_rows[t]
                pool.dma_start(dst, res[par][0:rows]).then_inc(y_stored[par], 16)
            with pool.Fori(0, TT // 2) as i:
                y_out(i, 0)
                y_out(i, 1)
            y_out(TT // 2, 0)
            pool.wait_ge(y_stored[0], 16 * (TT // 2 + 1))
            pool.wait_ge(y_stored[1], 16 * TT // 2)
            pool.wait_ge(kv_stored, 80 * PAIRS)
            pool.wait_ge(q_stored, 16 * PAIRS)
            pool.wait_ge(state_stored, 16 * AH)

        @block.scalar
        def _(act):
            me = Steps(act, act_steps)
            act.preload_act_table_set("natural_log_exp_and_others")
            act.sem_inc(lv_taken_a, 2)
            act.wait_ge(consts_v, 1)
            act.activation(lb_e, lb_e, ACT.Exp).then_inc(lb_a, 1)
            act.wait_ge(built.sem, built.at("eps"))
            for t in range(TT + 1):
                rows = P if t < TT else S
                act.wait_ge(x_loaded[t % 2], 16 * (t // 2 + 1))
                me.chain(act.activation(x_sq[t % 2][0:rows], x_in[t % 2][0:rows], ACT.Square, accum_out=msq[0:rows, t:t + 1]))
                me.chain(act.activation(rstd[0:rows, t:t + 1], msq[0:rows, t:t + 1], ACT.Ln, bias=eps[0:rows], scale=1.0 / D))
                act.activation(rstd[0:rows, t:t + 1], rstd[0:rows, t:t + 1], ACT.Exp, scale=-0.5).then_inc(x_rstd, 1)

            def evac(i, par, g):
                h = 2 * i + par
                act.wait_ge(proj_done.sem, proj_done.at(g, h))
                src = bank[g % 2]
                if g < 9:
                    if g % 3 == 0 and not (isinstance(h, int) and h == 0):
                        act.wait_ge(vecs.sem, vecs.at(("k_in", "q", "sg")[g // 3], h - 1))
                    dst = (raw_f, raw_q, raw_g)[g // 3][:, g % 3 * W3:(g % 3 + 1) * W3]
                    ins = act.copy(dst, src[:, 0:W3])
                elif g < 11:
                    ins = act.copy(v_tok[par][:, 4 * (g - 9):4 * (g - 8), :], src[:, :])
                else:
                    ins = act.copy(v_tok[par][0:S, TT, :], src[0:S, 0:P])
                ins.then_inc(proj_taken.sem, 1)

            def head(i, par, nxt):
                h = 2 * i + par

                def v(name):
                    act.wait_ge(vecs.sem, vecs.at(name, h))

                def e(g):
                    if nxt:
                        evac(i + par, 1 - par, g)

                def level(w):
                    d = diff[LEVELS.index(w) % 2]
                    v(f"diff{w}")
                    act.activation(d, d, ACT.Exp).then_inc(acts.sem, 1)

                v("abs_f")
                me.chain(act.activation(t0, t0, ACT.Exp, scale=-1.0))
                act.activation(t0, t0, ACT.Ln, bias=inv_h, scale=inv_h).then_inc(acts.sem, 1)
                v("abs_q")
                me.chain(act.activation(t3, t3, ACT.Exp, scale=-1.0))
                act.activation(t3, t3, ACT.Ln, bias=1.0).then_inc(acts.sem, 1)
                v("abs_g")
                me.chain(act.activation(sg_h, sg_h, ACT.Exp, scale=-1.0))
                act.activation(sg_h, sg_h, ACT.Ln, bias=1.0).then_inc(acts.sem, 1)
                v("k_in")
                act.activation(k_h, t1, ACT.Exp, scale=-1.0).then_inc(acts.sem, 1)
                v("q_in")
                act.activation(t3, t3, ACT.Exp).then_inc(acts.sem, 1)
                level(32)
                evac(i, par, 9)
                act.activation(f_smp, logf[:, T:N], ACT.Exp)
                act.activation(dec, cum[:, C - 1::C], ACT.Exp).then_inc(acts.sem, 1)
                act.activation(q_dec, cum, ACT.Exp).then_inc(acts.sem, 1)
                v("g_in")
                act.activation(sg_h, sg_h, ACT.Exp).then_inc(acts.sem, 1)
                level(16)
                evac(i, par, 10)
                level(8)
                evac(i, par, 11)
                e(0)
                level(4)
                e(1)
                v("o_smp")
                act.activation(sq_smp, o_smp, ACT.Square).then_inc(acts.sem, 1)
                v("diff_kd")
                act.activation(t1[:, 0:T], t1[:, 0:T], ACT.Exp).then_inc(acts.sem, 1)
                level(2)
                e(2)
                act.wait_ge(smp_done.sem, smp_done.at("mean_smp", h))
                act.activation(rs_smp, bank[6][:, 16:16 + S], ACT.Ln, bias=eps).then_inc(acts.sem, 1)
                level(1)
                e(3)
                e(4)
                for j in range(2):
                    act.wait_ge(uu_done.sem, uu_done.at(f"turn{j}", h))
                    act.copy(k_dec_tok[:, 4 * j:4 * j + 4, :], bank[4 + j][:, :]).then_inc(uu_taken_a, 1)
                e(5)
                e(6)
                e(7)
                for j in range(2):
                    act.wait_ge(ob_done.sem, ob_done.at(f"o{j}", h))
                    act.activation(o_sq[:, 512 * j:512 * j + 512], bank[6 + j][:, :], ACT.Square).then_inc(acts.sem, 1)
                e(8)
                for j in range(2):
                    act.wait_ge(lv_done.sem, lv_done.at(f"mean{j}", h))
                    act.activation(o_rs[:, 512 * j:512 * j + 512], bank[2 + j][:, :], ACT.Ln, bias=eps).then_inc(lv_taken_a, 1)
                act.wait_ge(lv_taken_a, 2 * h + 4)
                act.activation(o_rs[:, 0:T], o_rs[:, 0:T], ACT.Exp, scale=-0.5)
                act.activation(rs_smp, rs_smp, ACT.Exp, scale=-0.5).then_inc(acts.sem, 1)

            for g in range(9):
                evac(0, 0, g)
            PER = 2 * 3
            with act.Fori(0, LAST) as i:
                me.enter(i, PER)
                head(i, 0, True)
                head(i, 1, True)
                me.leave(PER, LAST)
            head(LAST, 0, True)
            head(LAST, 1, False)

            me.straight()

            def tile(i, par):
                t = 2 * i + par
                rows = S if isinstance(t, int) and t == TT else P
                act.wait_ge(tile_v.sem, tile_v.at("new1", t))
                me.chain(act.activation(h_sq[0:rows], h_new[par][0:rows], ACT.Square, accum_out=msq[0:rows, par:par + 1]))
                me.chain(act.activation(rstd[0:rows, par:par + 1], msq[0:rows, par:par + 1], ACT.Ln, bias=eps[0:rows], scale=1.0 / D))
                act.activation(rstd[0:rows, par:par + 1], rstd[0:rows, par:par + 1], ACT.Exp, scale=-0.5).then_inc(tile_a.sem, 1)
                for j in range(2):
                    act.wait_ge(h_turned, 2 * t + j + 1)
                    dst = h_t[:, 4 * j:4 * j + 4, t * P:t * P + rows] if isinstance(t, int) else h_t[:, 4 * j:4 * j + 4, bass.DynSlice(t * P, rows)]
                    act.sem_inc(end_go, 1)
                    act.copy(dst, bank[4 + 2 * par + j].rearrange("p (k n) -> p k n", n=P)[:, :, 0:rows]).then_inc(tile_a.sem, 1)
            with act.Fori(0, TT // 2) as i:
                me.enter(i, 4)
                tile(i, 0)
                tile(i, 1)
                me.leave(4, TT // 2)
            tile(TT // 2, 0)

            act.wait_ge(keys_v.sem, keys_v.at("abs"))
            me.chain(act.activation(a16[0:BH], a16[0:BH], ACT.Exp, scale=-1.0))
            act.activation(a16[0:BH], a16[0:BH], ACT.Ln, bias=1.0).then_inc(keys_a.sem, 1)

            act.wait_ge(raw_set, 3)
            me.straight()
            kq_half = ((0, 0), (0, 1), (1, 0), (1, 1), (2, 0), (2, 1), (3, 0), (3, 1))

            def slot(p, c, marks=None):
                first = isinstance(p, int) and p == 0
                if c == 0 and not first:
                    act.wait_ge(prep_v.sem, prep_v.at("g", p - 1))
                    act.wait_ge(prep_a.sem, prep_a.at("v_cur", p - 1))
                    act.wait_ge(kv_stored, 80 * p)
                    act.wait_ge(q_stored, 16 * p)
                if c < 18:
                    t, rows, y = c % 9, P if c % 9 < TT else S, c // 9
                    act.wait_ge(pj_done, SLOTS * p + c + 1)
                    kq = raw[0:rows, t, y * 2 * (DH + 1):(y + 1) * 2 * (DH + 1)].rearrange("p (x d) -> p x d", x=2)[:, :, 0:DH]
                    act.copy(kq, bank[c % 2][0:rows, 0:P].rearrange("p (x d) -> p x d", x=2))
                    for x in range(2):
                        me.chain(act.activation(trash[0:rows], bank[c % 2][0:rows, x * DH:(x + 1) * DH], ACT.Square,
                                                accum_out=ssq[0:rows, 2 * ((TT + 1) * y + t) + x:2 * ((TT + 1) * y + t) + x + 1]))
                    act.copy(raw[0:rows, t, 4 * (DH + 1) + y * P:4 * (DH + 1) + (y + 1) * P], bank[c % 2][0:rows, P:2 * P]).then_inc(pj_taken, 1)
                    if t == TT:
                        part = slice(y * 2 * (TT + 1), (y + 1) * 2 * (TT + 1))
                        me.chain(act.activation(rs_kq[:, part], ssq[:, part], ACT.Ln, bias=eps, scale=1.0 / DH))
                        act.activation(rs_kq[:, part], rs_kq[:, part], ACT.Exp, scale=-0.5).then_inc(prep_a.sem, 1)
                else:
                    x, j = divmod(c - 18, 2)
                    x = (0, 1, 2, 3)[x]
                    if j == 0 and not first:
                        act.wait_ge(fp.sem, fp.at(f"qk{TT - 1 if x in (0, 2) else ITEMS - 1}", p - 1))
                    act.wait_ge(pj_done, SLOTS * p + c + 1)
                    act.copy(kq_t[0:DH + 1, x, 512 * j:512 * j + 512], bank[c % 2][0:DH + 1, :]).then_inc(pj_taken, 1)

            def gate_ln(q):
                act.wait_ge(prep_v.sem, prep_v.at("abs_g", q))
                me.chain(act.activation(g_next, g_next, ACT.Exp, scale=-1.0))
                act.activation(g_next, g_next, ACT.Ln, bias=1.0).then_inc(prep_a.sem, 1)

            def gate_sig(q):
                act.wait_ge(prep_v.sem, prep_v.at("g_in", q))
                act.activation(g_next, g_next, ACT.Exp).then_inc(prep_a.sem, 1)

            def v_copy(q):
                act.copy(v_cur, raw[:, :, 4 * (DH + 1):4 * (DH + 1) + P]).then_inc(prep_a.sem, 1)

            def exp(w, p, name, logits):
                x, i = w % 2, w % TT
                act.wait_ge(fv.sem, logits)
                if w >= 2:
                    act.wait_ge(fp.sem, fp.at(f"pt{w - 2}_{int((w - 2) % TT >= 4)}", p))
                me.did(act.activation(prob[x][:, 0:(i + 1) * P], psum[:, (2 + 2 * x) * 512:(2 + 2 * x) * 512 + (i + 1) * P],
                               ACT.Exp, bias=top[:, w:w + 1], accum_out=total[:, w:w + 1]))
                me.need(me.base + me.n)
                act.sem_inc(fa.sem, 1)

            for c in range(18):
                slot(0, c)
            slot(0, 18)
            slot(0, 19)
            slot(0, 20)
            slot(0, 21)
            gate_ln(0)
            gate_sig(0)
            v_copy(0)
            for c in range(22, 26):
                slot(0, c)
            act.wait_ge(pj_taken, 26)
            act.sem_inc(pj_taken, 2)
            exp(0, 0, "ex_next", fv.at("mx_next", -1))

            def pair(p, nxt):
                done = 0
                for w in range(ITEMS):
                    x, i = w % 2, w % TT
                    if i >= 4:
                        act.wait_ge(fp.sem, fp.at(f"pt{w}_1", p))
                        act.copy(prob_t[x][:, 512:(i + 1) * P], bank[7][:, 0:(i + 1) * P - 512]).then_inc(fa.sem, 1)
                    if w + 1 < ITEMS:
                        exp(w + 1, p, f"ex{w + 1}", fv.at(f"mx{w + 1}", p))
                    if nxt:
                        for _ in range(FILL[w] if w < len(FILL) else 0):
                            slot(p + 1, done)
                            done += 1
                        if w == ITEMS - 2:
                            slot(p + 1, 18)
                            slot(p + 1, 19)
                            gate_ln(p + 1)
                        if w == ITEMS - 1:
                            slot(p + 1, 20)
                            slot(p + 1, 21)
                    if i == TT - 1:
                        g = w // TT
                        act.wait_ge(fv.sem, fv.at(f"df{g}", p))
                        act.activation(expd[g], expd[g], ACT.Exp).then_inc(dec_ready, 1)
                if nxt:
                    gate_sig(p + 1)
                    slot(p + 1, 22)
                    slot(p + 1, 23)
                    act.wait_ge(fp.sem, fp.at(f"pv{ITEMS - 1}", p))
                    act.sem_inc(end_go, 1)
                    v_copy(p + 1)
                    exp(0, p + 1, "ex_next", fv.at("mx_next", p))
                    slot(p + 1, 24)
                    slot(p + 1, 25)
                for j in range(2):
                    act.wait_ge(pj_done, SLOTS * (p + 1) + 26 * nxt + j + 1)
                    act.sem_inc(end_go, 1)
                    act.copy(o_cols(p, j), bank[j]).then_inc(pj_taken, 1)

            PER = 39 + ITEMS
            me.straight()
            with act.Fori(0, PAIRS - 1) as p:
                me.enter(p, PER)
                pair(p, True)
                me.leave(PER, PAIRS - 1)
            pair(PAIRS - 1, False)

        @block.vector
        def _(dve):
            me = Steps(dve, dve_steps)
            dve.sem_inc(vecs.sem, vecs.ahead)
            dve.sem_inc(uu_taken_v, 6)
            dve.wait_ge(consts_in, 48)
            dve.tensor_tensor(lb_e, lb_in, lb_in, ALU.subtract).then_inc(consts_v, 1)
            dve.wait_ge(lb_a, 1)
            me.chain(dve.reciprocal(lb_r, lb_e))
            me.chain(dve.tensor_tensor(lb_r, lb_e, lb_r, ALU.mult))
            me.chain(dve.tensor_tensor(lb_r, lb_r, lb_r, ALU.subtract))
            me.chain(dve.tensor_scalar(one_lb, lb_r, -1.0, 1.0, ALU.mult, ALU.add))
            me.chain(dve.reciprocal(inv_lb, one_lb))
            dve.wait_ge(built.sem, built.at("masks"))

            def x_out(t):
                rows = P if t < TT else S
                for j in range(2):
                    dve.wait_ge(x_turned, 2 * t + j + 1)
                    src = bank[2 + 2 * (t % 2) + j][:, :].rearrange("p (k n) -> p k n", n=P)[:, :, 0:rows]
                    dve.tensor_tensor(x_t[:, 4 * j:4 * j + 4, cols(t)], src,
                                      gain_a[:, 4 * j:4 * j + 4].unsqueeze(2).broadcast_to([P, 4, rows]),
                                      ALU.mult).then_inc(x_ready, 1)

            for t in range(TT + 1):
                rows = P if t < TT else S
                dve.wait_ge(x_rstd, t + 1)
                dve.tensor_scalar(x_in[t % 2][0:rows], x_in[t % 2][0:rows], rstd[0:rows, t:t + 1], None,
                                  ALU.mult).then_inc(x_scaled, 1)
                if t:
                    x_out(t - 1)
            x_out(TT)
            def head(i, par):
                h = 2 * i + par
                me.straight() if isinstance(i, int) else None

                def a(name):
                    dve.wait_ge(acts.sem, acts.at(name, h))

                def split(w):
                    c = cum.rearrange("p (b w) -> p b w", w=2 * w)
                    d = diff[LEVELS.index(w) % 2].rearrange("p (b w) -> p b w", w=2 * w)
                    mid = c[:, :, w - 1:w].broadcast_to([P, T // (2 * w), w])
                    dve.tensor_tensor(d[:, :, w:2 * w], c[:, :, w:2 * w], mid, ALU.subtract)
                    dve.tensor_tensor(d[:, :, 0:w], mid, c[:, :, 0:w], ALU.subtract).then_inc(vecs.sem, 1)

                def factors(w):
                    a(f"exp{w}")
                    if w == LEVELS[0]:
                        dve.wait_ge(vecs.sem, vecs.at("q", h))
                    d = diff[LEVELS.index(w) % 2].rearrange("p (b w) -> p b w", w=2 * w)
                    f = fact[LEVELS.index(w) % 2].rearrange("p (b w) -> p b w", w=2 * w)
                    q = q_h[:, 0:T].rearrange("p (b w) -> p b w", w=2 * w)
                    k = k_h[:, 0:T].rearrange("p (b w) -> p b w", w=2 * w)
                    dve.tensor_tensor(f[:, :, w:2 * w], d[:, :, w:2 * w], q[:, :, w:2 * w], ALU.mult)
                    dve.tensor_tensor(f[:, :, 0:w], d[:, :, 0:w], k[:, :, 0:w], ALU.mult).then_inc(vecs.sem, 1)

                def merge(w):
                    l = LEVELS.index(w)
                    dve.wait_ge(lv_done.sem, lv_done.at(f"level{w}", h))
                    dve.wait_ge(lv_taken_v, 8 * h + 2 + l)
                    dve.sem_inc(merge_go, 1)
                    out = att.rearrange("p (t b w) -> p t b w", t=TT, w=2 * w)[:, :, :, w:2 * w]
                    mask = level_mask[:, l * C:(l + 1) * C].bitcast(I32).rearrange("p (b w) -> p b w", w=w)
                    dve.copy_predicated(out, mask.unsqueeze(1).broadcast_to([P, TT, C // w, w]),
                                        bank[2 + l % 2][:, :].rearrange("p (t b w) -> p t b w", t=TT, w=w))\
                       .then_inc(lv_taken_v, 1)

                dve.tensor_copy(inv_h, col(inv_lb, h))
                for raw, out, g in ((raw_f, t0, 2), (raw_q, t3, 5), (raw_g, sg_h, 8)):
                    dve.wait_ge(proj_taken.sem, proj_taken.at(g, h))
                    if g == 8:
                        dve.wait_ge(vecs.sem, vecs.at("o_all", h - 1))
                    dve.tensor_scalar(out.bitcast(I32), raw.bitcast(I32), 0x7FFFFFFF, None, ALU.bitwise_and).then_inc(vecs.sem, 1)
                a("ln_f")
                dve.scalar_tensor_tensor(out=logf, in0=raw_f, scalar=0.0, in1=t0, op0=ALU.min,
                                         op1=ALU.subtract).then_inc(vecs.sem, 1)
                dve.scalar_tensor_tensor(out=t1, in0=raw_f, scalar=0.0, in1=t0, op0=ALU.max,
                                         op1=ALU.add).then_inc(vecs.sem, 1)
                dve.wait_ge(vecs.sem, vecs.at("logf", h))
                dve.tensor_tensor_scan(cum, chunk_keep, logf[:, 0:T], 0.0, ALU.mult, ALU.add)\
                   .then_inc(vecs.sem, 1)
                a("ln_q")
                dve.scalar_tensor_tensor(out=t3, in0=raw_q, scalar=0.0, in1=t3, op0=ALU.min,
                                         op1=ALU.subtract).then_inc(vecs.sem, 1)
                dve.wait_ge(vecs.sem, vecs.at("cum", h))
                split(32)
                a("ln_g")
                dve.scalar_tensor_tensor(out=sg_h, in0=raw_g, scalar=0.0, in1=sg_h, op0=ALU.min,
                                         op1=ALU.subtract).then_inc(vecs.sem, 1)
                a("sig_q")
                dve.tensor_tensor(q_h, raw_q, t3, ALU.mult).then_inc(vecs.sem, 1)
                factors(32)
                split(16)
                a("sig_g")
                dve.scalar_tensor_tensor(out=sg_h, in0=raw_g, scalar=gain_o, in1=sg_h, op0=ALU.mult,
                                         op1=ALU.mult).then_inc(vecs.sem, 1)
                c3 = cum.rearrange("p (c s) -> p c s", s=C)
                dve.tensor_tensor(t1[:, 0:T].rearrange("p (c s) -> p c s", s=C),
                                  c3[:, :, C - 1:C].broadcast_to([P, NC, C]), c3, ALU.subtract)\
                   .then_inc(vecs.sem, 1)
                dve.wait_ge(smp_done.sem, smp_done.at("k_smp", h))
                dve.tensor_copy(k_smp[0:S, :], bank[6][0:S, P:2 * P]).then_inc(vecs.sem, 1)
                for j in range(2):
                    dve.wait_ge(lv_done.sem, lv_done.at(f"diag{j}", h))
                    dve.tensor_tensor(att[:, 512 * j:512 * j + 512].rearrange("p (t q) -> p t q", q=P),
                                      bank[2 + j][:, :].rearrange("p (t q) -> p t q", q=P),
                                      ident.unsqueeze(1).broadcast_to([P, 4, P]), ALU.mult).then_inc(lv_taken_v, 1)
                factors(16)
                split(8)
                merge(32)
                dve.wait_ge(proj_taken.sem, proj_taken.at(11, h))
                dve.tensor_tensor(v_diag[0:S], v_tok[par][0:S, TT:TT + 1, :].broadcast_to([S, S, P]),
                                  ident[0:S, 0:S].unsqueeze(2).broadcast_to([S, S, P]), ALU.mult)\
                   .then_inc(vecs.sem, 1)
                dve.tensor_tensor(q_dec, q_dec, q_h[:, 0:T], ALU.mult).then_inc(vecs.sem, 1)
                dve.wait_ge(state_loaded, 16 * (h + 1))
                me.chain(dve.tensor_tensor(s_smp, s_smp, f_smp.unsqueeze(2).broadcast_to([P, S, P]), ALU.mult))
                for j in range(2):
                    dve.wait_ge(uu_done.sem, uu_done.at(f"outer{j}", h))
                    dve.tensor_tensor(s_smp[:, 4 * j:4 * j + 4, :], s_smp[:, 4 * j:4 * j + 4, :],
                                      bank[4 + j][:, :].rearrange("p (b v) -> p b v", v=P), ALU.add)\
                       .then_inc(uu_taken_v, 1)
                dve.wait_ge(uu_taken_v, 6 * h + 8)
                dve.sem_inc(vecs.sem, 1)
                factors(8)
                split(4)
                merge(16)
                dve.wait_ge(smp_done.sem, smp_done.at("o_smp", h))
                dve.tensor_copy(o_smp, bank[6][:, 0:S]).then_inc(vecs.sem, 1)
                factors(4)
                split(2)
                merge(8)
                a("exp_kd")
                dve.tensor_tensor(k_dec, k_h[:, 0:T], t1[:, 0:T], ALU.mult).then_inc(vecs.sem, 1)
                factors(2)
                split(1)
                merge(4)
                factors(1)
                merge(2)
                merge(1)
                dve.wait_ge(lv_taken_v, 8 * h + 8)
                dve.sem_inc(vecs.sem, 1)
                dve.wait_ge(s_all_free, h + 1)
                for c in range(NC):
                    half, new = c // 8, bank[4 + c % 2][:, c % 8 // 2 * P:(c % 8 // 2 + 1) * P]
                    if c % 8 == 0:
                        dve.wait_ge(uu_done.sem, uu_done.at(f"upd{2 * half + 1}", h))
                    if c == 0:
                        ins = dve.tensor_copy(s_all[:, 0, :], new)
                    else:
                        ins = dve.scalar_tensor_tensor(out=s_all[:, c, :], in0=s_all[:, c - 1, :],
                                                       scalar=dec[:, c:c + 1], in1=new, op0=ALU.mult, op1=ALU.add)
                    if c % 8 >= 6:
                        ins.then_inc(uu_taken_v, 1)
                        dve.wait_ge(uu_taken_v, 6 * h + 8 + 2 * half + c % 8 - 5)
                    else:
                        me.chain(ins)
                dve.sem_inc(vecs.sem, 1)
                a("dev")
                for j in range(2):
                    me.did(dve.tensor_tensor(o_rs[:, 512 * j:512 * j + 512], bank[6 + j][:, :],
                                             o_rs[:, 512 * j:512 * j + 512], ALU.mult))
                me.chain(dve.tensor_tensor(o_rs[:, T:N], o_smp, rs_smp, ALU.mult))
                dve.tensor_tensor(o_t[:, h, :], o_rs, sg_h, ALU.mult).then_inc(vecs.sem, 1)

            def col(a, h):
                return a[:, h:h + 1] if isinstance(h, int) else a[:, bass.DynSlice(h, 1)]

            PER = 2 * 16
            with dve.Fori(0, LAST) as i:
                me.enter(i, PER)
                head(i, 0)
                head(i, 1)
                me.leave(PER, LAST)
            head(LAST, 0)
            head(LAST, 1)

            dve.wait_ge(vecs.sem, vecs.at("o_all", AH - 1))

            def o_copy(t, par, used, copied):
                static = isinstance(t, int)
                rows = S if static and t == TT else P
                if not (static and t < 2):
                    dve.wait_ge(used, 2 * (t - 1))
                dve.sem_inc(end_go_v, 1)
                dve.tensor_copy(o_tile[par][:, :, 0:rows], o_t[:, :, cols(t)] if static else o_t[:, :, bass.DynSlice(t * P, P)])\
                   .then_inc(copied, 1)

            def tile(i, par, nxt=True):
                t = 2 * i + par
                static = isinstance(t, int)
                rows = S if static and t == TT else P
                if nxt:
                    o_copy(t + 1, 1 - par, y_done, o_set)
                dve.wait_ge(res_loaded[par], 16 * (i + 1))
                if not (static and t < 2):
                    dve.wait_ge(h_stored[par], 16 * i)
                for j in range(2):
                    dve.wait_ge(y_done, 2 * t + j + 1)
                    dve.tensor_tensor(h_new[par][0:rows, 512 * j:512 * j + 512], res[par][0:rows, 512 * j:512 * j + 512],
                                      bank[2 * par + j][0:rows], ALU.add).then_inc(tile_v.sem, 1)
                dve.wait_ge(tile_a.sem, tile_a.at("rstd", t))
                if not (static and t < 2):
                    dve.wait_ge(h_turned, 2 * (t - 1))
                dve.tensor_scalar(h_sc[par][0:rows], h_new[par][0:rows], rstd[0:rows, par:par + 1], None, ALU.mult)\
                   .then_inc(tile_v.sem, 1)
            o_copy(0, 0, y_done, o_set)
            tile(0, 0)
            tile(0, 1)
            with dve.Fori(1, TT // 2 - 1) as i:
                tile(i, 0)
                tile(i, 1)
            tile(TT // 2 - 1, 0)
            tile(TT // 2 - 1, 1)
            tile(TT // 2, 0, False)

            dve.wait_ge(keys_in, 16 * 8)
            dve.wait_ge(masks_b.sem, masks_b.at("later1"))
            dve.tensor_tensor(w_f, w_f, gain_kv.unsqueeze(2).broadcast_to([P, KT, BH]), ALU.mult).then_inc(keys_v.sem, 1)
            me.chain(dve.tensor_scalar(gain_kq[:, 2:4, :], gain_kq[:, 2:4, :], DH ** -0.5, None, ALU.mult))
            scale_w(dve, w_kv, gain_kv, 0, w_kv_loaded, w_kv_scaled)
            scale_w(dve, w_qg, gain_b, 0, w_qg_loaded, w_qg_scaled)
            dve.wait_ge(keys_p.sem, keys_p.at("z"))
            z = z16[0:BH]
            for n in range(3):
                me.did(dve.tensor_scalar(z[:, n * W3:(n + 1) * W3], bank[2 + n][0:BH, 0:W3], b_f[0:BH], None, ALU.add))
            me.need(me.base + me.n)
            dve.tensor_scalar(a16[0:BH].bitcast(I32), z.bitcast(I32), 0x7FFFFFFF, None, ALU.bitwise_and).then_inc(keys_v.sem, 1)
            dve.wait_ge(keys_a.sem, 1)
            dve.scalar_tensor_tensor(out=z, in0=z, scalar=0.0, in1=a16[0:BH], op0=ALU.min, op1=ALU.subtract).then_inc(keys_v.sem, 1)
            dve.wait_ge(keys_v.sem, keys_v.at("lf"))
            dve.tensor_tensor_scan(c16[0:BH], one16[0:BH], z[:, 0:T], 0.0, ALU.mult, ALU.add).then_inc(keys_v.sem, 1)
            dve.wait_ge(keys_p.sem, keys_p.at("turned"))
            me.did(dve.tensor_scalar(c_tok, bank[4][:, 0:TT * BH], -1.0, None, ALU.mult))
            me.did(dve.tensor_copy(lf_tok[0:S, TT * BH:(TT + 1) * BH], bank[5][0:S, TT * BH:(TT + 1) * BH]))
            dve.tensor_copy(lf_tok[:, 0:TT * BH], bank[5][:, 0:TT * BH]).then_inc(keys_v.sem, 1)
            dve.wait_ge(keys_p.sem, keys_p.at("suffix"))
            dve.wait_ge(lf_new_in, 16)
            me.chain(dve.tensor_copy(acc, lf_new.rearrange("p (b h) -> p b h", h=BH)))
            within = psum[:, 1024:2048].rearrange("p (b j h) -> p b j h", j=PAGES, h=BH)
            whole = psum[:, 3072:4096].rearrange("p (b j h) -> p b j h", j=PAGES, h=BH)
            for j in reversed(range(PAGES)):
                me.did(dve.tensor_tensor(bias[:, :, :, j], acc, within[:, :, j, :], ALU.add))
                me.chain(dve.scalar_tensor_tensor(out=acc, in0=whole[:, :, j, :], scalar=float(P), in1=acc, op0=ALU.mult, op1=ALU.add))
            dve.sem_inc(keys_v.sem, 1)

            kq5 = raw[:, :, 0:4 * (DH + 1)].rearrange("p t (x d) -> p t x d", x=4)
            g_raw = raw[:, :, 4 * (DH + 1) + P:RAW]

            def norm_k(q, y):
                kq = kq5[:, :, 2 * y:2 * y + 2, 0:DH]
                if y == 0:
                    c2 = c_tok.rearrange("p (t h) -> p t h", h=BH)
                    if not (isinstance(q, int) and q == 0):
                        dve.wait_ge(prep_v.sem, prep_v.at("g", q - 1))
                        dve.sem_inc(end_go_v, 1)
                    me.did(dve.tensor_copy(kq5[:, 0:TT, 0:2, DH], c2[:, :, 2 * q:2 * q + 2] if isinstance(q, int) else
                                           c2[:, :, bass.DynSlice(2 * q, 2)]))
                dve.wait_ge(prep_a.sem, prep_a.at(("rs_k", "rs_q")[y], q))
                rs = rs_kq[:, y * 2 * (TT + 1):(y + 1) * 2 * (TT + 1)].rearrange("p (t x) -> p t x", x=2)
                me.chain(dve.tensor_tensor(kq, kq, rs.unsqueeze(3).broadcast_to([P, TT + 1, 2, DH]), ALU.mult))
                dve.tensor_tensor(kq, kq, gain_kq[:, 2 * y:2 * y + 2, :].unsqueeze(1).broadcast_to([P, TT + 1, 2, DH]), ALU.mult)\
                   .then_inc(prep_v.sem, 1)

            def gate_abs(q):
                dve.wait_ge(pj_taken, SLOTS * q + 18)
                dve.tensor_scalar(g_next.bitcast(I32), g_raw.bitcast(I32), 0x7FFFFFFF, None, ALU.bitwise_and).then_inc(prep_v.sem, 1)

            def gate_in(q):
                dve.wait_ge(prep_a.sem, prep_a.at("ln_g", q))
                dve.scalar_tensor_tensor(out=g_next, in0=g_raw, scalar=0.0, in1=g_next, op0=ALU.min, op1=ALU.subtract).then_inc(prep_v.sem, 1)

            def gate(q):
                dve.wait_ge(prep_a.sem, prep_a.at("sig_g", q))
                dve.tensor_tensor(g_cur, g_next, g_raw, ALU.mult).then_inc(prep_v.sem, 1)

            def masked_max(w, logits):
                x, i = w % 2, w % TT
                dve.wait_ge(fp.sem, logits)
                diag = psum[:, (2 + 2 * x) * 512 + i * P:(2 + 2 * x) * 512 + (i + 1) * P]
                me.chain(dve.tensor_tensor(diag, diag, causal, ALU.add))
                dve.tensor_reduce(top[:, w:w + 1], psum[:, (2 + 2 * x) * 512:(2 + 2 * x) * 512 + (i + 1) * P], AX.X,
                                  ALU.max, negate=True).then_inc(fv.sem, 1)

            def pair(p, nxt, nxt2):
                static = isinstance(p, int)

                def a(name):
                    dve.wait_ge(fa.sem, fa.at(name, p))

                def pe(name, q=None):
                    dve.wait_ge(fp.sem, fp.at(name, p if q is None else q))

                def smp_out(g):
                    dve.wait_ge(dec_done, 2 * p + g + 1)
                    me.chain(dve.tensor_reduce(den, bank[7][:, 16:16 + 72].rearrange("p (n j) -> p n j", j=9), AX.X, ALU.add))
                    me.chain(dve.reciprocal(den, den))
                    me.chain(dve.scalar_tensor_tensor(out=o_two, in0=bank[7][:, P:P + 8], scalar=1.0 / P, in1=den, op0=ALU.mult, op1=ALU.mult))
                    o2 = o_two.rearrange("p (b x) -> p b x", x=2)
                    for x in range(2):
                        rows = slice(x * DH, (x + 1) * DH)
                        lo = T + HALF * g
                        dst = o_t[rows, p, lo:lo + HALF] if static else o_t[rows, bass.DynSlice(p, 1), lo:lo + HALF].rearrange("p a n -> p (a n)")
                        ins = dve.tensor_tensor(dst, o2[rows, :, x], g_smp[rows, HALF * g:HALF * g + HALF], ALU.mult)
                        if x == 0:
                            me.did(ins)
                    ins.then_inc(od_done, 1)

                for w in range(ITEMS):
                    x, i, g = w % 2, w % TT, w // TT
                    if w == TT + HALF:
                        smp_out(0)
                    if w == 1:
                        pe("g_smp")
                        dve.tensor_copy(g_smp, bank[7][:, 0:S]).then_inc(fv.sem, 1)
                    pe(f"pt{w}_0")
                    width = min(i + 1, 4) * P
                    dve.tensor_copy(prob_t[x][:, 0:width], bank[6][:, 0:width]).then_inc(fv.sem, 1)
                    if w + 1 < ITEMS:
                        masked_max(w + 1, fp.at(f"qk{w + 1}", p))
                    pe(f"pv{w}")
                    me.chain(dve.reciprocal(r_total[:, w:w + 1], total[:, w:w + 1]))
                    head_cols = slice(g * DH, (g + 1) * DH)
                    dve.scalar_tensor_tensor(out=og[:, i, head_cols], in0=bank[2 + 2 * x][:, 0:DH], scalar=r_total[:, w:w + 1],
                                             in1=g_cur[:, i, head_cols], op0=ALU.mult, op1=ALU.mult).then_inc(fv.sem, 1)
                    lg = lgt[g].rearrange("p (b x j) -> p b x j", x=2, j=9)
                    if 1 <= i <= HALF:
                        b = i - 1
                        n = HALF * g + b
                        if w == 1:
                            dve.wait_ge(new_loaded, 32 * (p + 1))
                        dve.wait_ge(k_loaded[b], 128 * (2 * p + g + 1))
                        if w > 1:
                            me.need(me_last[0])
                        k = k_ring[:, b]
                        dve.tensor_tensor(prod.rearrange("p (j n) -> p j n", n=P), k, q_all[:, n:n + 1, :].broadcast_to([P, PAGES, P]), ALU.mult).then_inc(fv.sem, 1)
                        dve.wait_ge(fv.sem, fv.at(f"pr{n}", p))
                        me_last[0] = me.did(dve.tensor_reduce(lg[:, b, :, 0:PAGES].rearrange("p x j -> p j x"),
                                                 prod.rearrange("p (j x d) -> p j x d", x=2, d=DH), AX.X, ALU.add))
                    if i == HALF + 1:
                        me.need(me_last[0])
                        lo = slice(HALF * g, HALF * (g + 1))
                        me.did(dve.tensor_tensor(lg[:, :, :, 0:PAGES], lg[:, :, :, 0:PAGES],
                                                 bias[:, lo, 2 * p:2 * p + 2, :] if static else bias[:, lo, bass.DynSlice(2 * p, 2), :], ALU.add))
                        new = prod[0:1, 0:HALF * P]
                        me.chain(dve.tensor_tensor(new.rearrange("p (b n) -> p b n", n=P), k_new[:, lo, :], q_all[0:1, lo, :], ALU.mult))
                        me.chain(dve.tensor_reduce(lg[0:1, :, :, PAGES], new.rearrange("p (b x d) -> p b x d", x=2, d=DH), AX.X, ALU.add))
                        dve.tensor_reduce(top8[g], lg, AX.X, ALU.max).then_inc(fv.sem, 1)
                    if i == TT - 1:
                        dve.wait_ge(top_all, 2 * p + g + 1)
                        if not (static and p == 0):
                            dve.wait_ge(dec_done, 2 * p + g - 1)
                        dve.tensor_tensor(expd[g].rearrange("p (n j) -> p n j", j=9), lgt[g].rearrange("p (n j) -> p n j", j=9),
                                          m_all[g].unsqueeze(2).broadcast_to([P, 8, 9]), ALU.subtract).then_inc(fv.sem, 1)
                    if w == 3 and nxt:
                        scale_w(dve, w_qg, gain_b, p + 1, w_qg_loaded, w_qg_scaled)
                    if w == 7 and nxt:
                        norm_k(p + 1, 0)
                    if w == 10 and nxt2:
                        scale_w(dve, w_kv, gain_kv, p + 2, w_kv_loaded, w_kv_scaled)
                    if w == 13 and nxt:
                        gate_abs(p + 1)
                    if w == 14 and nxt:
                        norm_k(p + 1, 1)
                    if w == 15 and nxt:
                        gate_in(p + 1)
                if nxt:
                    gate(p + 1)
                    masked_max(0, fp.at("qk_next", p))
                smp_out(1)

            me_last = [0]
            me.straight()
            norm_k(0, 0)
            gate_abs(0)
            norm_k(0, 1)
            gate_in(0)
            gate(0)
            scale_w(dve, w_kv, gain_kv, 1, w_kv_loaded, w_kv_scaled)
            masked_max(0, fp.at("qk_next", -1))
            pair(0, True, True)
            me.straight()
            PER = 57
            with dve.Fori(1, PAIRS - 2) as p:
                me.enter(p - 1, PER)
                pair(p, True, True)
                me.leave(PER, PAIRS - 3)
            pair(PAIRS - 2, True, False)
            me.straight()
            pair(PAIRS - 1, False, False)
            me.straight()

            dve.wait_ge(pj_taken, OUT_TAKEN)
            dve.wait_ge(od_done, 2 * PAIRS)

            def tile_b(i, par, nxt=True):
                t = 2 * i + par
                rows = S if isinstance(t, int) and t == TT else P
                if nxt:
                    o_copy(t + 1, 1 - par, yb_done, ob_set)
                dve.wait_ge(resb_loaded[par], 16 * (i + 1))
                for j in range(2):
                    dve.wait_ge(yb_done, 2 * t + j + 1)
                    dve.tensor_tensor(res[par][0:rows, 512 * j:512 * j + 512], res[par][0:rows, 512 * j:512 * j + 512],
                                      bank[2 * par + j][0:rows], ALU.add).then_inc(yb_v.sem, 1)
            o_copy(0, 0, yb_done, ob_set)
            tile_b(0, 0)
            tile_b(0, 1)
            with dve.Fori(1, TT // 2 - 1) as i:
                tile_b(i, 0)
                tile_b(i, 1)
            tile_b(TT // 2 - 1, 0)
            tile_b(TT // 2 - 1, 1)
            tile_b(TT // 2, 0, False)

        @block.tensor
        def _(pe):
            pe.wait_ge(built.sem, built.at("masks"))
            for t in range(TT + 1):
                rows = P if t < TT else S
                pe.wait_ge(x_scaled, t + 1)
                if t >= 2:
                    pe.wait_ge(x_ready, 2 * (t - 1))
                for k in range(KT):
                    ins = pe.transpose(bank[2 + 2 * (t % 2) + k // 4][:, k % 4 * P:k % 4 * P + rows],
                                       x_in[t % 2][0:rows, k * P:(k + 1) * P], ident[0:rows, 0:rows])
                    if k % 4 == 3:
                        ins.then_inc(x_turned, 1)
            pe.wait_ge(x_ready, 2 * (TT + 1))

            def proj(i, par, g):
                h = 2 * i + par
                first = isinstance(h, int) and h == 0
                if g == 0:
                    pe.wait_ge(w_a_loaded[par], 64 * (i + 1))
                if not (first and g < 2):
                    pe.wait_ge(proj_taken.sem, 12 * h + g - 1)
                dst = bank[g % 2]
                if g < 9:
                    for k in range(KT):
                        ins = pe.matmul(dst[:, 0:W3], w_a[:, par, k, g // 3, :], x_t[:, k, g % 3 * W3:(g % 3 + 1) * W3],
                                        start=(k == 0), stop=(k == KT - 1))
                else:
                    for t in range(4 * (g - 9), 4 * (g - 8)) if g < 11 else (TT,):
                        rows = P if t < TT else S
                        for k in range(KT):
                            ins = pe.matmul(dst[0:rows, t % 4 * P:(t % 4 + 1) * P], x_t[:, k, cols(t)],
                                            w_a[:, par, k, 3, :], start=(k == 0), stop=(k == KT - 1))
                ins.then_inc(proj_done.sem, 1)

            def head(i, par, nxt):
                h = 2 * i + par

                def v(name, hh=None):
                    pe.wait_ge(vecs.sem, vecs.at(name, h if hh is None else hh))

                def group(g):
                    if nxt:
                        proj(i + par, 1 - par, g)

                def level(w):
                    l = LEVELS.index(w)
                    v(f"fact{w}")
                    pe.wait_ge(lv_taken_v, 8 * h + l + 1)
                    f = fact[l % 2]
                    for t in range(TT):
                        q = f[:, t * P:(t + 1) * P].rearrange("p (b w) -> p b w", w=2 * w)[:, :, w:2 * w]
                        ins = pe.matmul(bank[2 + l % 2][:, t * C:(t + 1) * C], f[:, t * P:(t + 1) * P], q,
                                        start=True, stop=True)
                    ins.then_inc(lv_done.sem, 1)

                proj(i, par, 9)
                proj(i, par, 10)
                pe.wait_ge(acts.sem, acts.at("k", h))
                v("o_all", h - 1)
                pe.transpose(bank[6][0:S, P:2 * P], k_h[:, T:N], ident).then_inc(smp_done.sem, 1)
                v("q")
                for j in range(2):
                    pe.wait_ge(lv_taken_a, 2 * h + 1 + j)
                    for t in range(4 * j, 4 * j + 4):
                        ins = pe.matmul(bank[2 + j][:, t % 4 * P:(t % 4 + 1) * P], k_h[:, cols(t)], q_h[:, cols(t)],
                                        start=True, stop=True)
                    ins.then_inc(lv_done.sem, 1)
                proj(i, par, 11)
                level(32)
                group(0)
                v("v_diag")
                for j in range(2):
                    pe.wait_ge(uu_taken_v, 6 * h + 5 + j)
                    pe.matmul(bank[4 + j][:, :], k_smp[0:S, :], v_diag[0:S, 4 * j:4 * j + 4, :],
                              start=True, stop=True).then_inc(uu_done.sem, 1)
                level(16)
                group(1)
                v("s_smp")
                for b in range(S):
                    ins = pe.matmul(bank[6][:, b:b + 1], s_smp[:, b, :], q_h[:, T + b:T + b + 1],
                                    start=True, stop=True)
                ins.then_inc(smp_done.sem, 1)
                level(8)
                group(2)
                level(4)
                pe.wait_ge(acts.sem, acts.at("sq_smp", h))
                pe.matmul(bank[6][:, 16:16 + S], ones_mean, sq_smp, start=True, stop=True)\
                  .then_inc(smp_done.sem, 1)
                group(3)
                level(2)
                for j in range(2):
                    pe.wait_ge(uu_taken_v, 6 * h + 7 + j)
                    for t in range(4 * j, 4 * j + 4):
                        ins = pe.transpose(bank[4 + j][:, t % 4 * P:(t % 4 + 1) * P], k_dec[:, cols(t)], ident)
                    ins.then_inc(uu_done.sem, 1)
                group(4)
                level(1)
                group(5)
                for j in range(4):
                    if j < 2:
                        pe.wait_ge(uu_taken_a, 2 * h + 1 + j)
                        if j == 0:
                            pe.wait_ge(uu_taken_a, 2 * h + 2)
                    else:
                        pe.wait_ge(uu_taken_v, 6 * h + 7 + j)
                    for n in range(4):
                        c = 8 * (j // 2) + 2 * n + j % 2
                        rows = slice(c % 2 * C, (c % 2 + 1) * C)
                        ins = pe.matmul(bank[4 + j % 2][:, n * P:(n + 1) * P], k_dec_tok[rows, c // 2, :],
                                        v_tok[par][rows, c // 2, :], start=True, stop=True)
                    ins.then_inc(uu_done.sem, 1)
                group(6)
                group(7)
                v("s_all")
                pe.wait_ge(acts.sem, acts.at("ln_smp", h))
                for t in range(TT):
                    dst = bank[6 + t // 4][:, t % 4 * P:(t % 4 + 1) * P]
                    pe.matmul(dst, v_tok[par][:, t, :], att[:, cols(t)], start=True, stop=False, skip_group_check=True)
                    for c in (2 * t, 2 * t + 1):
                        if c:
                            ins = pe.matmul(dst[:, c % 2 * C:(c % 2 + 1) * C], s_all[:, c - 1, :],
                                            q_dec[:, c * C:(c + 1) * C], start=False, stop=(c % 2 == 1),
                                            skip_group_check=True)
                    if t % 4 == 3:
                        ins.then_inc(ob_done.sem, 1)
                group(8)
                for j in range(2):
                    pe.wait_ge(acts.sem, acts.at(f"sq{j}", h))
                    pe.wait_ge(lv_taken_v, 8 * h + 7 + j)
                    pe.matmul(bank[2 + j][:, :], ones_mean, o_sq[:, 512 * j:512 * j + 512], start=True,
                              stop=True).then_inc(lv_done.sem, 1)

            for g in range(9):
                proj(0, 0, g)
            with pe.Fori(0, LAST) as i:
                head(i, 0, True)
                head(i, 1, True)
            head(LAST, 0, True)
            head(LAST, 1, False)

            pe.wait_ge(w_o_loaded, 16)
            pe.wait_ge(vecs.sem, vecs.at("o_all", AH - 1))

            def y_tile(i, par, copied, done):
                t = 2 * i + par
                static = isinstance(t, int)
                rows = S if static and t == TT else P
                pe.wait_ge(copied, t + 1)
                for j in range(2):
                    for h in range(AH):
                        ins = pe.matmul(bank[2 * par + j][0:rows, :], o_tile[par][:, h, 0:rows], w_o[:, h, 512 * j:512 * j + 512],
                                        start=(h == 0), stop=(h == AH - 1))
                    ins.then_inc(done, 1)

            def turn(i, par):
                t = 2 * i + par
                static = isinstance(t, int)
                rows = S if static and t == TT else P
                pe.wait_ge(tile_v.sem, tile_v.at("scaled", t))
                if not (static and t < 2):
                    pe.wait_ge(tile_a.sem, tile_a.at("h_t1", t) - 2 * len(tile_a.names))
                for k in range(KT):
                    ins = pe.transpose(bank[4 + 2 * par + k // 4][:, k % 4 * P:k % 4 * P + rows],
                                       h_sc[par][0:rows, k * P:(k + 1) * P], ident[0:rows, 0:rows])
                    if k % 4 == 3:
                        ins.then_inc(h_turned, 1)

            y_tile(0, 0, o_set, y_done)
            y_tile(0, 1, o_set, y_done)
            turn(0, 0)
            with pe.Fori(1, TT // 2) as i:
                y_tile(i, 0, o_set, y_done)
                turn(i - 1, 1)
                y_tile(i, 1, o_set, y_done)
                turn(i, 0)
            y_tile(TT // 2, 0, o_set, y_done)
            turn(TT // 2 - 1, 1)
            turn(TT // 2, 0)

            pe.wait_ge(tile_a.sem, tile_a.at("h_t1", TT))
            pe.wait_ge(keys_v.sem, keys_v.at("w_f"))
            for n in range(3):
                for k in range(KT):
                    ins = pe.matmul(bank[2 + n][0:BH, 0:W3], w_f[:, k, :], h_t[:, k, n * W3:(n + 1) * W3],
                                    start=(k == 0), stop=(k == KT - 1))
            ins.then_inc(keys_p.sem, 1)
            def slot(p, c):
                t, rows = c % 9, P if c % 9 < TT else S
                if c in (0, 9):
                    pe.wait_ge((w_kv_scaled, w_qg_scaled)[c // 9], p + 1)
                if c in (18, 22):
                    pe.wait_ge(prep_v.sem, prep_v.at("k" if c == 18 else "q", p))
                if not (isinstance(p, int) and p == 0 and c < 2):
                    pe.wait_ge(pj_taken, SLOTS * p + c - 1)
                if c < 18:
                    w = (w_kv, w_qg)[c // 9]
                    for k in range(KT):
                        ins = pe.matmul(bank[c % 2][0:rows, 0:2 * P], h_t[:, k, cols(t)], w[:, k, :, :],
                                        start=(k == 0), stop=(k == KT - 1))
                else:
                    x, j = divmod(c - 18, 2)
                    for t in range(4 * j, 4 * j + 4):
                        ins = pe.transpose(bank[c % 2][0:DH + 1, t % 4 * P:(t % 4 + 1) * P],
                                           raw[:, t, x * (DH + 1):(x + 1) * (DH + 1)], ident)
                ins.then_inc(pj_done, 1)

            def logits(w):
                hd, i, x = w // TT, w % TT, w % 2
                for j in range(0, i + 1, 4):
                    n = min(4, i + 1 - j)
                    ins = pe.matmul(bank[2 + 2 * x + j // 4][:, 0:n * P], kq_t[0:DH + 1, 2 + hd, cols(i)],
                                    kq_t[0:DH + 1, hd, j * P:(j + n) * P], start=True, stop=True)
                ins.then_inc(fp.sem, 1)

            def pair(p, nxt):
                static = isinstance(p, int)

                def v(name, q=None):
                    pe.wait_ge(fv.sem, fv.at(name, p if q is None else q))

                def a(name):
                    pe.wait_ge(fa.sem, fa.at(name, p))

                def decode(g, b):
                    e = expd[g].rearrange("p (b x j) -> p b x j", x=2, j=9)
                    if b == 0:
                        pe.wait_ge(dec_ready, 2 * p + g + 1)
                        a(f"ptc{TT * g + TT - 1}")
                        if g == 0:
                            pe.wait_ge(v_new_loaded, 16 * (p + 1))
                        pe.matmul(bank[7][:, 16:16 + 72], ones_mean, expd[g], start=True, stop=True, skip_group_check=True)
                    pe.wait_ge(v_loaded[b], 128 * (2 * p + g + 1))
                    dst = bank[7][:, P + 2 * b:P + 2 * b + 2]
                    for j in range(PAGES):
                        pe.matmul(dst, v_ring[:, b, j, :], e[:, b, :, j], start=(j == 0), stop=False, skip_group_check=True)
                    ins = pe.matmul(dst, v_new[:, HALF * g + b, :], e[0:1, b, :, PAGES], start=False, stop=True, skip_group_check=True)
                    if b == HALF - 1:
                        ins.then_inc(dec_done, 1)

                done = 0
                for w in range(ITEMS):
                    hd, i, x = w // TT, w % TT, w % 2
                    if w == 1:
                        pe.wait_ge(prep_v.sem, prep_v.at("g", p))
                        if not (static and p == 0):
                            pe.wait_ge(od_done, 2 * p)
                        pe.sem_inc(pe_go, 1)
                        pe.transpose(bank[7][:, 0:S], g_cur[0:S, TT, :], ident[0:S, 0:S]).then_inc(fp.sem, 1)
                    if w == 0:
                        pe.wait_ge(fa.sem, fa.at("ex_next", p - 1))
                    else:
                        a(f"ex{w}")
                    for j in range(0, i + 1, 4):
                        if j == 0:
                            v(f"ptc{w - 1}") if w else None
                        elif w == 4:
                            v("g_smp")
                        elif w == TT + 4:
                            pe.wait_ge(od_done, 2 * p + 1)
                        else:
                            a(f"ptc{w - 1}")
                        for n in range(j, min(j + 4, i + 1)):
                            ins = pe.transpose(bank[6 + j // 4][:, n % 4 * P:(n % 4 + 1) * P], prob[x][:, n * P:(n + 1) * P], ident)
                        ins.then_inc(fp.sem, 1)
                    if w + 1 < ITEMS:
                        if w >= 1:
                            v(f"nm{w - 1}")
                        elif not (static and p == 0):
                            v(f"nm{ITEMS - 1}", p - 1)
                        if w == 0:
                            pe.wait_ge(pj_taken, SLOTS * p + 24)
                        if w == TT - 1:
                            pe.wait_ge(pj_taken, SLOTS * p + 26)
                        logits(w + 1)
                    if nxt:
                        for _ in range(FILL[w] if w < len(FILL) else 0):
                            slot(p + 1, done)
                            done += 1
                        if w >= ITEMS - 2:
                            slot(p + 1, 18 + 2 * (w - ITEMS + 2))
                            slot(p + 1, 19 + 2 * (w - ITEMS + 2))
                    v(f"ptc{w}")
                    if w == 0:
                        pe.wait_ge(prep_a.sem, prep_a.at("v_cur", p))
                    if i >= 4:
                        a(f"ptc{w}")
                    for n in range(i + 1):
                        ins = pe.matmul(bank[2 + 2 * x][:, 0:DH], prob_t[x][:, n * P:(n + 1) * P],
                                        v_cur[:, n, hd * DH:(hd + 1) * DH], start=(n == 0), stop=(n == i))
                    ins.then_inc(fp.sem, 1)
                    if TT <= w < TT + HALF:
                        decode(0, w - TT)
                decode(1, 0)
                decode(1, 1)
                if nxt:
                    slot(p + 1, 22)
                    slot(p + 1, 23)
                decode(1, 2)
                if nxt:
                    pe.wait_ge(pj_taken, SLOTS * (p + 1) + 24)
                    v(f"nm{ITEMS - 2}")
                    logits(0)
                    slot(p + 1, 24)
                    slot(p + 1, 25)
                decode(1, 3)
                v(f"nm{ITEMS - 1}")
                for j in range(2):
                    pe.wait_ge(pj_taken, SLOTS * (p + 1) + 26 * nxt + j - 1)
                    for t in range(4 * j, 4 * j + 4):
                        ins = pe.transpose(bank[j][:, t % 4 * P:(t % 4 + 1) * P], og[:, t, :], ident)
                    ins.then_inc(pj_done, 1)

            for c in range(9):
                slot(0, c)
            pe.wait_ge(keys_v.sem, keys_v.at("c"))
            for t in range(TT + 1):
                rows = P if t < TT else S
                ins = pe.transpose(bank[5][0:rows, t * BH:(t + 1) * BH], z16[0:BH, cols(t)], ident[0:BH, 0:BH])
                if t < TT:
                    ins = pe.transpose(bank[4][:, t * BH:(t + 1) * BH], c16[0:BH, cols(t)], ident[0:BH, 0:BH])
            ins.then_inc(keys_p.sem, 1)
            for c in range(9, 11):
                slot(0, c)
            pe.wait_ge(lf_in, 16 * S * PAGES)
            pe.wait_ge(masks_b.sem, masks_b.at("later1"))
            for j in range(2):
                pe.matmul(bank[2 + j], later, lf_pages[:, 512 * j:512 * j + 512], start=True, stop=True)
                ins = pe.matmul(bank[6 + j], ones_mean, lf_pages[:, 512 * j:512 * j + 512], start=True, stop=True)
            ins.then_inc(keys_p.sem, 1)
            for c in range(11, 26):
                slot(0, c)
            pe.wait_ge(keys_v.sem, keys_v.at("done"))
            pe.wait_ge(pj_done, 26)
            pe.sem_inc(pj_done, 2)
            pe.wait_ge(pj_taken, 24)
            logits(0)

            pair(0, True)
            with pe.Fori(1, PAIRS - 1) as p:
                pair(p, True)
            pair(PAIRS - 1, False)

            pe.wait_ge(w_ob_loaded, 16)
            pe.wait_ge(pj_taken, OUT_TAKEN)

            y_tile(0, 0, ob_set, yb_done)
            y_tile(0, 1, ob_set, yb_done)
            with pe.Fori(1, TT // 2) as i:
                y_tile(i, 0, ob_set, yb_done)
                y_tile(i, 1, ob_set, yb_done)
            y_tile(TT // 2, 0, ob_set, yb_done)


_OUTS = [("y_prompt", (1, T, D)), ("y_sample", (S, 1, D)), ("state_prompt", (1, 1, AH, P, P)),
         ("state_sample", (1, S, AH, P, P)), ("k_prompt", (1, T, BH, DH)), ("k_sample", (S, 1, BH, DH)),
         ("v_prompt", (1, T, BH, DH)), ("v_sample", (S, 1, BH, DH)), ("logf_prompt", (1, T, BH)),
         ("logf_sample", (S, 1, BH))]


def kernel(**inputs):
    import numpy as np
    import concourse.bacc as bacc
    from concourse.bass_utils import run_bass_kernel_spmd

    nc = bacc.Bacc("TRN2", target_bir_lowering=False, num_devices=1)
    arrays, io = {}, {}
    for name, a in inputs.items():
        a = np.ascontiguousarray(a)
        arrays[f"in_{name}"] = a
        io[name] = nc.dram_tensor(f"in_{name}", a.shape, mybir.dt.from_np(a.dtype), kind="ExternalInput").ap()
    for name, shape in _OUTS:
        io[name] = nc.dram_tensor(f"out_{name}", shape, F32, kind="ExternalOutput").ap()
    build(nc, io)
    r = run_bass_kernel_spmd(nc, [arrays], core_ids=[0])
    return tuple(r.results[0][f"out_{name}"] for name, _ in _OUTS)
```

```python
from contextlib import ExitStack

import concourse.bass as bass
from concourse import mybir

F32 = mybir.dt.float32
BF16 = mybir.dt.bfloat16
I32 = mybir.dt.int32
ALU = mybir.AluOpType
ACT = mybir.ActivationFunctionType
AX = mybir.AxisListType

P = 128
EPS = 1e-6


class Steps:

    def __init__(self, eng, sem):
        self.eng, self.sem, self.start, self.base, self.n = eng, sem, 0, 0, 0

    def did(self, ins):
        ins.then_inc(self.sem, 1)
        self.n += 1
        return self.base + self.n

    def need(self, mark):
        self.eng.wait_ge(self.sem, mark)

    def chain(self, ins):
        self.need(self.did(ins))

    def enter(self, i, per):
        self.start = self.start + self.n
        self.base, self.n = self.start + i * per, 0

    def leave(self, per, times):
        assert self.n == per, (self.n, per)
        self.start, self.n = self.start + per * times, 0
        self.base = self.start

    def straight(self):
        self.start = self.start + self.n
        self.base, self.n = self.start, 0


class Marks:

    def __init__(self, sem, *names, ahead=0):
        self.sem, self.names, self.ahead = sem, names, ahead
        self.index = {n: i + 1 for i, n in enumerate(names)}
        assert len(self.index) == len(names)

    def at(self, name, r=0):
        return r * len(self.names) + self.index[name] + self.ahead


D = 1024
T = 1024
S = 8
N = T + S
KT = D // P
TT = T // P
W3 = N // 3
AH = 8
C = 64
NC = T // C
LEVELS = (32, 16, 8, 4, 2, 1)
BH = 16
DH = 64
PAIRS = BH // 2
PAGES = 8
RAW = 4 * (DH + 1) + 2 * P
HALF = S // 2
ITEMS = 2 * TT
LOW = -3e38
FILL = (1, 1, 1, 2, 1, 1, 1, 1, 2, 2, 2, 2, 1)
TURN = (0, 2, 1, 3)
SLOTS = 28


W_COL = (1, 0, 3, 2)
LAST = AH // 2 - 1


def build(nc, io):
    with ExitStack() as ctx:
        def sem(name):
            return ctx.enter_context(nc.semaphore(name))

        WORDS = 53200
        arena = ctx.enter_context(nc.sbuf_tensor("arena", [P, WORDS], F32))
        psum = ctx.enter_context(nc.psum_tensor("psum", [P, 8 * 512], F32))
        bank = [psum[:, 512 * i:512 * (i + 1)] for i in range(8)]
        used = [0]

        def area(words):
            at = used[0]
            used[0] += words
            assert used[0] <= WORDS, used[0]
            return arena[:, at:at + words]

        ident = area(P)
        ones_mean = area(P)
        spare_at = used[0]
        level_mask = area(len(LEVELS) * C)
        chunk_keep = area(T // 2).bitcast(BF16)
        gain_a = area(KT)
        gain_o = area(1)
        lb_in, one_lb, inv_lb, inv_h = area(AH), area(AH), area(AH), area(1)
        eps = area(1)
        msq, rstd = area(TT + 1), area(TT + 1)
        lb_e, lb_r = area(AH), area(AH)

        x_t = area(KT * N).rearrange("p (k n) -> p k n", n=N)
        w_a_at = used[0]
        w_a = area(2 * KT * 4 * P).rearrange("p (s k y n) -> p s k y n", s=2, y=4, n=P)
        o_t = area(AH * N).rearrange("p (h n) -> p h n", n=N)
        temps = used[0]
        raw_f, raw_q, raw_g = area(N), area(N), area(N)
        t0, t1, t2 = area(N), area(N), area(N)
        k_h, q_h, sg_h, logf, cum, q_dec = area(N), area(N), area(N), area(N), area(T), area(T)
        k_dec = logf[:, 0:T]
        diffs, facts = area(2 * T), area(2 * T)
        diff = [diffs[:, 0:T], diffs[:, T:2 * T]]
        fact = [facts[:, 0:T], facts[:, T:2 * T]]
        o_sq, o_rs = diffs[:, 0:N], facts[:, 0:N]
        att = area(T)
        v_tok = [area((TT + 1) * P).rearrange("p (t v) -> p t v", v=P) for _ in range(2)]
        k_dec_tok = area(T).rearrange("p (t k) -> p t k", k=P)
        s_all = area(NC * P).rearrange("p (c v) -> p c v", v=P)
        s_smp = area(S * P).rearrange("p (b v) -> p b v", v=P)
        v_diag = area(S * P).rearrange("p (b v) -> p b v", v=P)
        k_smp, o_smp, f_smp, dec = area(P), area(S), area(S), area(NC)
        sq_smp, rs_smp = area(S), area(S)
        x_in = [arena[:, temps + t * D:temps + (t + 1) * D] for t in range(TT + 1)]
        x_sq = [diffs[:, 0:D], diffs[:, T:T + D]]

        h_t = x_t
        w_o = arena[:, w_a_at:w_a_at + AH * D].rearrange("p (h n) -> p h n", n=D)
        used[0] = temps
        o_tile = [area(AH * P).rearrange("p (h n) -> p h n", n=P) for _ in range(2)]
        res, h_new, h_sc = [area(D), area(D)], [area(D), area(D)], [area(D), area(D)]
        h_sq = area(D)
        assert used[0] <= temps + 9 * 1024

        used[0] = temps
        raw = area((TT + 1) * RAW).rearrange("p (t c) -> p t c", c=RAW)
        kq_t = area(4 * T).rearrange("p (x n) -> p x n", n=T)
        ssq, rs_kq = area((TT + 1) * 4), area((TT + 1) * 4)
        top, total, r_total = area(16), area(16), area(16)
        expd = [area(HALF * 2 * 9) for _ in range(2)]
        top8, m_all, den, o_two, g_smp = [area(8), area(8)], [area(8), area(8)], area(8), area(8), area(S)
        assert used[0] <= temps + 9 * 1024
        used[0] = temps + 9 * 1024
        w_kv = area(KT * 2 * P).rearrange("p (k y n) -> p k y n", y=2, n=P)
        w_qg = area(KT * 2 * P).rearrange("p (k y n) -> p k y n", y=2, n=P)
        w_o_high = arena[:, temps + 9 * 1024:temps + 9 * 1024 + AH // 2 * D].rearrange("p (h n) -> p h n", n=D)
        bias = area(S * BH * PAGES).rearrange("p (b h j) -> p b h j", h=BH, j=PAGES)
        gain_kv, gain_b = area(KT), area(KT)
        pages = area(S * PAGES).bitcast(I32)
        after = used[0]
        v_cur = area((TT + 1) * P).rearrange("p (t v) -> p t v", v=P)
        g_cur = area((TT + 1) * P).rearrange("p (t v) -> p t v", v=P)
        prob, prob_t = [area(T), area(T)], [area(T), area(T)]
        q_all = area(S * P).rearrange("p (b n) -> p b n", n=P)
        prod = area(PAGES * P)
        og = area(TT * P).rearrange("p (t v) -> p t v", v=P)
        kv_new = area(2 * S * P)
        k_new = kv_new[0:1, 0:S * P].rearrange("p (b n) -> p b n", n=P)
        v_new = kv_new[0:1, S * P:2 * S * P].rearrange("p (b n) -> p b n", n=P)
        g_next = area((TT + 1) * P).rearrange("p (t v) -> p t v", v=P)
        trash = area(DH)
        assert used[0] <= WORDS, used[0]
        used[0] = spare_at
        gain_kq = area(4 * DH).rearrange("p (x d) -> p x d", d=DH)
        lf_tok, c_tok = area((TT + 1) * BH), area(TT * BH)
        causal = area(P)
        lgt = [area(HALF * 2 * 9) for _ in range(2)]
        assert used[0] <= spare_at + len(LEVELS) * C + T // 2
        k_ring = arena[:, w_a_at:w_a_at + 4 * PAGES * P].rearrange("p (s j n) -> p s j n", s=4, n=P)
        v_ring = arena[:, w_a_at + 4 * PAGES * P:w_a_at + 8 * PAGES * P].rearrange("p (s j n) -> p s j n", s=4, n=P)
        used[0] = after
        w_f = area(KT * BH).rearrange("p (k n) -> p k n", n=BH)
        z16, a16, one16, c16, b_f = area(N), area(N), area(T), area(T), area(1)
        lf_pages = area(S * PAGES * BH)
        later, lf_new = area(P), area(S * BH)
        acc = area(S * BH).rearrange("p (b h) -> p b h", h=BH)
        assert used[0] <= WORDS, used[0]
        h_dram = nc.dram_tensor("h_rows", [N, D], F32).ap()
        q_dram = nc.dram_tensor("q_rows", [PAIRS, S, P], F32).ap()

        consts_in = sem("consts_in")
        built = Marks(sem("built"), "ident0", "ones", "masks0", "keep0", "eps", "vdiag0", "ident", "masks1", "keep", "masks")
        consts_v = sem("consts_v")
        x_loaded = [sem(f"x_loaded{t}") for t in range(TT + 1)]
        x_scaled, x_turned, x_ready = sem("x_scaled"), sem("x_turned"), sem("x_ready")
        x_rstd = sem("x_rstd")
        lb_a = sem("lb_a")
        w_a_loaded = [sem("w_a_loaded0"), sem("w_a_loaded1")]
        state_loaded, state_stored, prompt_stored = sem("state_loaded"), sem("state_stored"), sem("prompt_stored")
        s_all_free = sem("s_all_free")
        merge_go, pool_go, sp_go, act_go, dve_go, pe_go = [sem(f"{n}_go") for n in ("merge", "pool", "sp", "act", "dve", "pe")]
        raw_set = sem("raw_set")
        act_steps, dve_steps = sem("act_steps"), sem("dve_steps")
        proj_done = Marks(sem("proj_done"), *range(12))
        lv_done = Marks(sem("lv_done"), "diag0", "diag1", *[f"level{l}" for l in LEVELS], "mean0", "mean1")
        smp_done = Marks(sem("smp_done"), "k_smp", "o_smp", "mean_smp")
        uu_done = Marks(sem("uu_done"), "outer0", "outer1", "turn0", "turn1", "upd0", "upd1", "upd2", "upd3")
        ob_done = Marks(sem("ob_done"), "o0", "o1")
        proj_taken = Marks(sem("proj_taken"), *range(12))
        lv_taken_v, lv_taken_a = sem("lv_taken_v"), sem("lv_taken_a")
        uu_taken_v, uu_taken_a = sem("uu_taken_v"), sem("uu_taken_a")
        acts = Marks(sem("acts"), "ln_g", "k", "sig_q", "exp32", "decays", "exp_cum", "sig_g", "exp16",
                     "exp8", "exp4", "sq_smp", "exp_kd", "exp2", "ln_smp", "exp1",
                     "next_ln_f", "sq0", "sq1", "next_ln_q", "dev", ahead=5)
        vecs = Marks(sem("vecs"), "abs_g", "logf", "k_in", "cum", "q_in", "diff32", "g_in", "q",
                     "fact32", "diff16", "k_smp", "fact16", "diff8", "v_diag", "sg", "diff_kd", "q_dec", "s_smp",
                     "fact8", "diff4", "o_smp", "fact4", "diff2", "k_dec", "fact2", "diff1", "fact1",
                     "att_all", "next_abs_f", "s_all", "next_abs_q", "o_all", ahead=4)
        w_o_loaded, res_loaded, h_stored = sem("w_o_loaded"), [sem("res_loaded0"), sem("res_loaded1")], [sem("h_stored0"), sem("h_stored1")]
        o_set, tile_v = sem("o_set"), Marks(sem("tile_v"), "new0", "new1", "scaled")
        tile_a = Marks(sem("tile_a"), "rstd", "h_t0", "h_t1")
        y_done, h_turned = sem("y_done"), sem("h_turned")
        keys_in, pages_in, lf_in, lf_new_in = sem("keys_in"), sem("pages_in"), sem("lf_in"), sem("lf_new_in")
        lf_stored = sem("lf_stored")
        keys_p = Marks(sem("keys_p"), "z", "turned", "suffix")
        keys_v = Marks(sem("keys_v"), "w_f", "abs", "lf", "c", "tok", "done")
        keys_a = Marks(sem("keys_a"), "ln")
        masks_b = Marks(sem("masks_b"), "ones", "causal0", "later0", "low0", "low1", "causal", "later")
        w_kv_loaded, w_qg_loaded = sem("w_kv_loaded"), sem("w_qg_loaded")
        w_kv_scaled, w_qg_scaled = sem("w_kv_scaled"), sem("w_qg_scaled")
        pj_done, pj_taken = sem("pj_done"), sem("pj_taken")
        k_loaded, v_loaded = [sem(f"k_loaded{i}") for i in range(4)], [sem(f"v_loaded{i}") for i in range(4)]
        kv_stored, q_stored, new_loaded, v_new_loaded, top_all = sem("kv_stored"), sem("q_stored"), sem("new_loaded"), sem("v_new_loaded"), sem("top_all")
        order_p, order_v, order_a = [], [], []
        for w in range(ITEMS):
            order_p += [f"pt{w}_0"] + [f"pt{w}_1"] * (w % TT >= 4) + [f"qk{w + 1}"] * (w + 1 < ITEMS) + [f"pv{w}"] + ["g_smp"] * (w == 3)
            order_v += ["g_smp"] * (w == 4) + [f"ptc{w}"] + [f"mx{w + 1}"] * (w + 1 < ITEMS)
            order_v += [f"pr{w // TT * HALF + w % TT - 1}"] * (1 <= w % TT <= HALF)
            order_v += [f"lg{w // TT}"] * (w % TT == HALF + 1) + [f"df{w // TT}"] * (w % TT == TT - 1)
            order_v += [f"nm{w}"]
            order_a += [f"ptc{w}"] * (w % TT >= 4) + [f"ex{w + 1}"] * (w + 1 < ITEMS)
        fp = Marks(sem("fox_p"), *order_p, "qk_next", ahead=1)
        fv = Marks(sem("fox_v"), *order_v, "mx_next", ahead=1)
        fa = Marks(sem("fox_a"), *order_a, "ex_next", ahead=1)
        prep_v = Marks(sem("prep_v"), "k", "abs_g", "q", "g_in", "g")
        prep_a = Marks(sem("prep_a"), "rs_k", "rs_q", "ln_g", "sig_g", "v_cur")
        dec_ready, v_mult = sem("dec_ready"), sem("v_mult")
        red_ready, dec_done, od_done = sem("red_ready"), sem("dec_done"), sem("od_done")
        w_ob_loaded, resb_loaded, y_stored = sem("w_ob_loaded"), [sem("resb_loaded0"), sem("resb_loaded1")], [sem("y_stored0"), sem("y_stored1")]
        yb_done, ob_set, yb_v = sem("yb_done"), sem("ob_set"), Marks(sem("yb_v"), "y0", "y1")

        block = ctx.enter_context(nc.Block())

        w_in_a = io["w_in_a"].rearrange("l (k p) (y h n) -> p k y (l h) n", p=P, y=4, n=P)
        x_prompt = io["x_prompt"].rearrange("b (t p) d -> (b t) p d", p=P)
        x_sample = io["x_sample"].rearrange("b s d -> (b s) d")
        state_in = io["state_hgrn"].rearrange("l b h k v -> (l h) k b v")
        state_out = io["state_sample"].rearrange("l b h k v -> (l h) k b v")
        prompt_out = io["state_prompt"].rearrange("l b h k v -> (l b h) k v")

        def cols(t):
            return slice(t * P, t * P + (P if t < TT else S))

        def load_w(sp, i, par):
            for y in range(4):
                sp.dma_start(w_a[:, par, :, y, :], w_in_a[:, :, W_COL[y], 2 * i + par, :]).then_inc(w_a_loaded[par], 16)

        w_kv_d = io["w_kv"].rearrange("(k p) (y h n) -> p k y h n", p=P, y=2, n=P)
        w_qg_d = io["w_in_b"].rearrange("l (k p) (y h n) -> p k y (l h) n", p=P, y=2, n=P)
        k_cache = io["cache_k"].rearrange("g s (x h) d -> g s x (h d)", h=2)
        v_cache = io["cache_v"].rearrange("g s (x h) d -> g s x (h d)", h=2)
        lf_cache = io["cache_logf"]
        n_pool = lf_cache.shape[0]

        def o_cols(p, j):
            if isinstance(p, int):
                return o_t[:, p, 512 * j:512 * j + 512]
            return o_t[:, bass.DynSlice(p, 1), 512 * j:512 * j + 512].rearrange("p a n -> p (a n)")

        def scale_w(dve, w, gain, p, loaded, scaled):
            dve.wait_ge(loaded, 32 * (p + 1))
            dve.tensor_tensor(w, w, gain.unsqueeze(2).unsqueeze(3).broadcast_to([P, KT, 2, P]), ALU.mult).then_inc(scaled, 1)

        def load_wb(sp, dst, src, p, loaded):
            for y in range(2):
                sp.dma_start(dst[:, :, y, :], src[:, :, y, p, :]).then_inc(loaded, 16)

        OUT_TAKEN = SLOTS * PAIRS + 2

        def page_id(sp, n):
            at = pages[0:1, n:n + 1] if isinstance(n, int) else pages[0:1, bass.DynSlice(n, 1)]
            return sp.value_load(at, min_val=0, max_val=n_pool - 1)

        def page_ids(n):
            _, ids = nc.values_load_multi_w_load_instructions(
                pages[0:1, n * PAGES:(n + 1) * PAGES], engines=[mybir.EngineType.SP], min_val=0, max_val=n_pool - 1,
                skip_runtime_bounds_check_because="a page table's entries are pages of the pool")
            return ids

        @block.sync
        def _(sp):
            sp.dma_start(gain_a, io["norm_in"][0].rearrange("(k p) -> p k", p=P), allow_slow_non_contiguous=True).then_inc(consts_in, 16)
            sp.dma_start(gain_o, io["g_norm_a"].rearrange("l p -> p l"), allow_slow_non_contiguous=True).then_inc(consts_in, 16)
            sp.dma_start(lb_in, io["lb_logits"].rearrange("l (h p) -> p (l h)", p=P), allow_slow_non_contiguous=True).then_inc(consts_in, 16)
            for t in range(TT + 1):
                rows = P if t < TT else S
                sp.dma_start(x_in[t][0:rows], x_prompt[t] if t < TT else x_sample).then_inc(x_loaded[t], 16)
            load_w(sp, 0, 0)
            load_w(sp, 0, 1)

            def body(i):
                for par in range(2):
                    sp.wait_ge(proj_done.sem, proj_done.at(11, 2 * i + par))
                    load_w(sp, i + 1, par)

            with sp.Fori(0, LAST) as i:
                body(i)

            sp.wait_ge(proj_done.sem, proj_done.at(11, AH - 1))
            sp.dma_start(w_o, io["w_o_a"][0].rearrange("(h p) n -> p h n", p=P)).then_inc(w_o_loaded, 16)
            sp.wait_ge(vecs.sem, vecs.at("o_all", AH - 1))
            sp.dma_start(pages[0:1, :], io["page_table"].rearrange("(o b) j -> o (b j)", o=1)).then_inc(pages_in, 16)

            LF_STEP = S * PAGES // (TT // 2 - 1)

            def res_in(i, par):
                t = 2 * i + par
                sp.wait_ge(tile_v.sem, tile_v.at("new1", t) - 2 * len(tile_v.names)) if not (isinstance(t, int) and t < 2) else None
                sp.sem_inc(sp_go, 1)
                src = x_sample if isinstance(t, int) and t == TT else x_prompt[t]
                sp.dma_start(res[par][0:src.shape[0]], src).then_inc(res_loaded[par], 16)

            res_in(0, 0)
            res_in(0, 1)
            load_wb(sp, w_kv, w_kv_d, 0, w_kv_loaded)
            load_wb(sp, w_qg, w_qg_d, 0, w_qg_loaded)
            with nc.allow_non_contiguous_dma(reason="small constants"):
                sp.dma_start(gain_kv, io["norm_kv"].rearrange("(k p) -> p k", p=P)).then_inc(keys_in, 16)
                sp.dma_start(gain_b, io["norm_in"][1].rearrange("(k p) -> p k", p=P)).then_inc(keys_in, 16)
                sp.dma_start(b_f[0:BH], io["b_fgate"].rearrange("(h o) -> h o", o=1)).then_inc(keys_in, 16)
            for x, g in enumerate((io["k_norm"], io["k_norm"], io["q_norm_b"][0], io["q_norm_b"][0])):
                sp.dma_start(gain_kq[:, x, :], g.partition_broadcast(P)).then_inc(keys_in, 16)
            sp.dma_start(w_f, io["w_fgate"].rearrange("(k p) n -> p k n", p=P)).then_inc(keys_in, 16)
            sp.wait_ge(pages_in, 16)
            with sp.Fori(1, TT // 2) as i:
                res_in(i, 0)
                res_in(i, 1)
                for n in range(LF_STEP):
                    at = (i - 1) * LF_STEP + n
                    page = page_id(sp, at)
                    sp.dma_start(lf_pages[:, bass.DynSlice(at * BH, BH)], lf_cache[page]).then_inc(lf_in, 16)
            res_in(TT // 2, 0)
            for at in range(LF_STEP * (TT // 2 - 1), S * PAGES):
                page = page_id(sp, at)
                sp.dma_start(lf_pages[:, at * BH:(at + 1) * BH], lf_cache[page]).then_inc(lf_in, 16)

            def k_in(p, g):
                for b in range(HALF):
                    for j, page in enumerate(page_ids(HALF * g + b)):
                        sp.dma_start(k_ring[:, b, j, :], k_cache[page, :, p, :]).then_inc(k_loaded[b], 16)

            def v_in(p, g):
                for b in range(HALF):
                    for j, page in enumerate(page_ids(HALF * g + b)):
                        sp.dma_start(v_ring[:, b, j, :], v_cache[page, :, p, :]).then_inc(v_loaded[b], 16)

            sp.wait_ge(y_done, 2 * (TT + 1))
            sp.sem_inc(sp_go, 1)
            k_in(0, 0)
            v_in(0, 0)
            sp.wait_ge(pj_done, TT + 1)
            load_wb(sp, w_kv, w_kv_d, 1, w_kv_loaded)
            sp.wait_ge(pj_done, 2 * (TT + 1))
            load_wb(sp, w_qg, w_qg_d, 1, w_qg_loaded)

            def pair(p, nxt, nxt2):
                sp.wait_ge(fv.sem, fv.at(f"pr{HALF - 1}", p))
                sp.sem_inc(sp_go, 1)
                k_in(p, 1)
                if nxt2:
                    sp.wait_ge(pj_done, SLOTS * (p + 1) + TT + 1)
                    sp.sem_inc(sp_go, 1)
                    load_wb(sp, w_kv, w_kv_d, p + 2, w_kv_loaded)
                sp.wait_ge(dec_done, 2 * p + 1)
                sp.sem_inc(sp_go, 1)
                v_in(p, 1)
                if nxt:
                    sp.wait_ge(fv.sem, fv.at(f"pr{S - 1}", p))
                    sp.sem_inc(sp_go, 1)
                    k_in(p + 1, 0)
                if nxt2:
                    sp.wait_ge(pj_done, SLOTS * (p + 1) + 18)
                    sp.sem_inc(sp_go, 1)
                    load_wb(sp, w_qg, w_qg_d, p + 2, w_qg_loaded)
                if nxt:
                    sp.wait_ge(dec_done, 2 * p + 2)
                    sp.sem_inc(sp_go, 1)
                    v_in(p + 1, 0)

            with sp.Fori(0, PAIRS - 2) as p:
                pair(p, True, True)
            pair(PAIRS - 2, True, False)
            sp.wait_ge(pj_done, SLOTS * PAIRS)
            w_ob = io["w_o_b"][0].rearrange("(h p) n -> p h n", p=P)
            sp.dma_start(w_o_high, w_ob[:, AH // 2:AH]).then_inc(w_ob_loaded, 16)
            pair(PAIRS - 1, False, False)

            sp.wait_ge(fv.sem, fv.at("lg1", PAIRS - 1))
            sp.dma_start(w_o[:, 0:AH // 2], w_ob[:, 0:AH // 2]).then_inc(w_ob_loaded, 16)
            sp.wait_ge(pj_taken, OUT_TAKEN)
            sp.wait_ge(h_stored[0], 16 * (TT // 2 + 1))
            sp.wait_ge(h_stored[1], 16 * TT // 2)

            def resb_in(i, par):
                t = 2 * i + par
                rows = S if isinstance(t, int) and t == TT else P
                if not (isinstance(t, int) and t < 2):
                    sp.wait_ge(y_stored[par], 16 * i)
                sp.sem_inc(sp_go, 1)
                sp.dma_start(res[par][0:rows], h_dram[bass.DynSlice(t * P, rows)] if not isinstance(t, int) else
                             h_dram[t * P:t * P + rows]).then_inc(resb_loaded[par], 16)
            resb_in(0, 0)
            resb_in(0, 1)
            with sp.Fori(1, TT // 2) as i:
                resb_in(i, 0)
                resb_in(i, 1)
            resb_in(TT // 2, 0)

        k_out = io["k_prompt"].rearrange("b (t p) (g x) d -> p (b t) g x d", p=P, x=2)
        v_out = io["v_prompt"].rearrange("b (t p) (g x) d -> p (b t) g (x d)", p=P, x=2)
        ks_out = io["k_sample"].rearrange("b s (g x) d -> (b s) g x d", x=2)
        vs_out = io["v_sample"].rearrange("b s (g x) d -> (b s) g (x d)", x=2)
        y_rows = io["y_prompt"].rearrange("b (t p) d -> (b t) p d", p=P)

        @block.gpsimd
        def _(pool):
            pool.memset(ident, 0.0).then_inc(built.sem, 1)
            pool.memset(ones_mean, 1.0 / P).then_inc(built.sem, 1)
            pool.memset(level_mask, 1.0).then_inc(built.sem, 1)
            pool.memset(chunk_keep, 1.0).then_inc(built.sem, 1)
            pool.memset(eps, EPS).then_inc(built.sem, 1)
            pool.memset(v_diag, 0.0).then_inc(built.sem, 1)
            pool.wait_ge(built.sem, built.at("vdiag0"))
            pool.affine_select(out=ident, in_=ident, compare_op=ALU.not_equal, fill=1.0, base=0,
                               pattern=[[-1, P]], channel_multiplier=1).then_inc(built.sem, 1)
            for l, w in enumerate(LEVELS):
                m = level_mask[:, l * C:(l + 1) * C].rearrange("p (b w) -> p b w", w=w)
                last = pool.affine_select(out=m, in_=m, compare_op=ALU.is_ge, fill=0.0, base=0,
                                          pattern=[[-2 * w, C // w], [0, w]], channel_multiplier=1)
            last.then_inc(built.sem, 1)
            keep = chunk_keep.rearrange("p (c s) -> p c s", s=C)
            pool.affine_select(out=keep, in_=keep, compare_op=ALU.not_equal, fill=0.0, base=0,
                               pattern=[[0, NC], [1, C]], channel_multiplier=0).then_inc(built.sem, 1)
            pool.wait_ge(built.sem, built.at("masks1"))
            for l, w in enumerate(LEVELS):
                m = level_mask[:, l * C:(l + 1) * C].rearrange("p (b w) -> p b w", w=w)
                last = pool.affine_select(out=m, in_=m, compare_op=ALU.is_ge, fill=0.0, base=w - 1,
                                          pattern=[[2 * w, C // w], [0, w]], channel_multiplier=-1)
            last.then_inc(built.sem, 1)

            pool.sem_inc(s_all_free, 1)

            def head(h):
                pool.dma_start(s_smp, state_in[h]).then_inc(state_loaded, 16)
                pool.wait_ge(vecs.sem, vecs.at("s_smp", h))
                pool.sem_inc(pool_go, 1)
                pool.dma_start(state_out[h], s_smp).then_inc(state_stored, 16)
                pool.wait_ge(vecs.sem, vecs.at("s_all", h))
                pool.sem_inc(pool_go, 1)
                pool.dma_start(prompt_out[h], s_all[:, NC - 1, :]).then_inc(prompt_stored, 16)
                pool.wait_ge(smp_done.sem, smp_done.at("o_smp", h))
                pool.wait_ge(state_stored, 16 * (h + 1))
                pool.wait_ge(prompt_stored, 16 * (h + 1))
                pool.sem_inc(s_all_free, 1)
            with pool.Fori(0, AH) as h:
                head(h)
            pool.wait_ge(prompt_stored, 16 * AH)
            pool.wait_ge(vecs.sem, vecs.at("o_all", AH - 1))
            pool.memset(one16, 1.0).then_inc(masks_b.sem, 1)
            pool.memset(causal, 0.0).then_inc(masks_b.sem, 1)
            pool.memset(later, 1.0).then_inc(masks_b.sem, 1)
            pool.wait_ge(masks_b.sem, masks_b.at("later0"))
            pool.memset(lgt[0], LOW).then_inc(masks_b.sem, 1)
            pool.memset(lgt[1], LOW).then_inc(masks_b.sem, 1)
            pool.affine_select(out=causal, in_=causal, compare_op=ALU.is_ge, fill=LOW, base=0,
                               pattern=[[-1, P]], channel_multiplier=1).then_inc(masks_b.sem, 1)
            pool.affine_select(out=later, in_=later, compare_op=ALU.is_gt, fill=0.0, base=0,
                               pattern=[[-1, P]], channel_multiplier=1).then_inc(masks_b.sem, 1)

            def h_out(i, par):
                t = 2 * i + par
                rows = S if isinstance(t, int) and t == TT else P
                pool.wait_ge(tile_v.sem, tile_v.at("new1", t))
                pool.sem_inc(pool_go, 1)
                pool.dma_start(h_dram[t * P:t * P + rows] if isinstance(t, int) else h_dram[bass.DynSlice(t * P, rows)],
                               h_new[par][0:rows]).then_inc(h_stored[par], 16)
            with pool.Fori(0, TT // 2) as i:
                h_out(i, 0)
                h_out(i, 1)
            h_out(TT // 2, 0)
            pool.wait_ge(h_stored[0], 16 * (TT // 2 + 1))
            pool.wait_ge(h_stored[1], 16 * TT // 2)
            pool.wait_ge(tile_a.sem, tile_a.at("h_t1", TT))
            pool.memset(raw, 0.0).then_inc(raw_set, 1)
            pool.memset(ssq, 0.0).then_inc(raw_set, 1)
            pool.wait_ge(raw_set, 2)
            pool.memset(raw[:, :, 0:4 * (DH + 1)].rearrange("p t (x d) -> p t x d", x=4)[:, :, 2:4, DH:DH + 1], 1.0).then_inc(raw_set, 1)

            pool.wait_ge(keys_v.sem, keys_v.at("tok"))
            lf = lf_tok.rearrange("p (t h) -> p t h", h=BH)
            pool.dma_start(io["logf_prompt"].rearrange("b (t p) h -> p (b t) h", p=P), lf[:, 0:TT, :]).then_inc(lf_stored, 16)
            pool.dma_start(io["logf_sample"].rearrange("b s h -> (b s) h"), lf[0:S, TT, :]).then_inc(lf_stored, 16)
            pool.wait_ge(lf_stored, 32)
            pool.dma_start(lf_new, io["logf_sample"].rearrange("b s h -> (b s h)").partition_broadcast(P)).then_inc(lf_new_in, 16)
            pool.wait_ge(lf_new_in, 16)

            def tops(p, g):
                pool.wait_ge(fv.sem, fv.at(f"lg{g}", p))
                pool.sem_inc(pool_go, 1)
                pool.partition_all_reduce(m_all[g], top8[g], P, bass.bass_isa.ReduceOp.max).then_inc(top_all, 1)

            def weigh(p, g):
                e = expd[g].rearrange("p (b x j) -> p b x j", x=2, j=9)
                pool.wait_ge(dec_ready, 2 * p + g + 1)
                for b in range(HALF):
                    pool.wait_ge(v_loaded[b], 128 * (2 * p + g + 1))
                    pool.sem_inc(pool_go, 1)
                    v4 = v_ring[:, b].rearrange("p j (x d) -> p j x d", x=2)
                    weights = e[:, b, :, 0:PAGES].rearrange("p x j -> p j x").unsqueeze(3).broadcast_to([P, PAGES, 2, DH])
                    pool.tensor_tensor(v4, v4, weights, ALU.mult).then_inc(v_mult, 1)

            def pair(p):
                if not isinstance(p, int) or p:
                    tops(p - 1, 0)
                    weigh(p - 1, 0)
                pool.wait_ge(prep_v.sem, prep_v.at("k", p))
                pool.sem_inc(pool_go, 1)
                kk = raw[:, :, 0:2 * (DH + 1)].rearrange("p t (x d) -> p t x d", x=2)[:, :, :, 0:DH]
                qq = raw[:, :, 2 * (DH + 1):4 * (DH + 1)].rearrange("p t (x d) -> p t x d", x=2)[:, :, :, 0:DH]
                vv = raw[:, :, 4 * (DH + 1):4 * (DH + 1) + P]
                for x in range(2):
                    pool.dma_start(k_out[:, :, p, x, :], kk[:, 0:TT, x, :]).then_inc(kv_stored, 16)
                pool.dma_start(v_out[:, :, p, :], vv[:, 0:TT, :]).then_inc(kv_stored, 16)
                pool.dma_start(ks_out[:, p, :, :], kk[0:S, TT]).then_inc(kv_stored, 16)
                pool.dma_start(vs_out[:, p, :], vv[0:S, TT, :]).then_inc(kv_stored, 16)
                if not isinstance(p, int) or p:
                    tops(p - 1, 1)
                pool.wait_ge(kv_stored, 80 * (p + 1))
                pool.sem_inc(pool_go, 1)
                pool.dma_start(k_new, ks_out[:, p].rearrange("b x d -> b (x d)").unsqueeze(0)).then_inc(new_loaded, 16)
                pool.wait_ge(prep_v.sem, prep_v.at("q", p))
                pool.sem_inc(pool_go, 1)
                pool.dma_start(q_dram[p].rearrange("b (x d) -> b x d", x=2), qq[0:S, TT]).then_inc(q_stored, 16)
                pool.wait_ge(q_stored, 16 * (p + 1))
                pool.sem_inc(pool_go, 1)
                pool.dma_start(q_all, q_dram[p].rearrange("b n -> (b n)").partition_broadcast(P)).then_inc(new_loaded, 16)
                if not isinstance(p, int) or p:
                    weigh(p - 1, 1)
                    pool.wait_ge(red_ready, 2 * p)
                    pool.sem_inc(pool_go, 1)
                pool.dma_start(v_new, vs_out[:, p, :].unsqueeze(0)).then_inc(v_new_loaded, 16)

            pair(0)
            with pool.Fori(1, PAIRS) as p:
                pair(p)
            for g in range(2):
                tops(PAIRS - 1, g)
                weigh(PAIRS - 1, g)

            def y_out(i, par):
                t = 2 * i + par
                last = isinstance(t, int) and t == TT
                rows = S if last else P
                pool.wait_ge(yb_v.sem, yb_v.at("y1", t))
                pool.sem_inc(pool_go, 1)
                dst = io["y_sample"].rearrange("b s d -> (b s) d") if last else y_rows[t]
                pool.dma_start(dst, res[par][0:rows]).then_inc(y_stored[par], 16)
            with pool.Fori(0, TT // 2) as i:
                y_out(i, 0)
                y_out(i, 1)
            y_out(TT // 2, 0)
            pool.wait_ge(y_stored[0], 16 * (TT // 2 + 1))
            pool.wait_ge(y_stored[1], 16 * TT // 2)
            pool.wait_ge(kv_stored, 80 * PAIRS)
            pool.wait_ge(q_stored, 16 * PAIRS)
            pool.wait_ge(state_stored, 16 * AH)
            pool.wait_ge(prompt_stored, 16 * AH)
            pool.wait_ge(lf_stored, 32)

        @block.scalar
        def _(act):
            me = Steps(act, act_steps)
            act.preload_act_table_set("natural_log_exp_and_others")
            act.sem_inc(lv_taken_a, 2)
            act.wait_ge(consts_v, 1)
            act.activation(lb_e, lb_e, ACT.Exp).then_inc(lb_a, 1)
            act.wait_ge(built.sem, built.at("eps"))
            for t in range(TT + 1):
                rows = P if t < TT else S
                act.wait_ge(x_loaded[t], 16)
                me.chain(act.activation(x_sq[t % 2][0:rows], x_in[t][0:rows], ACT.Square, accum_out=msq[0:rows, t:t + 1]))
                me.chain(act.activation(rstd[0:rows, t:t + 1], msq[0:rows, t:t + 1], ACT.Ln, bias=eps[0:rows], scale=1.0 / D))
                act.activation(rstd[0:rows, t:t + 1], rstd[0:rows, t:t + 1], ACT.Exp, scale=-0.5).then_inc(x_rstd, 1)

            def evac(i, par, g):
                h = 2 * i + par
                act.wait_ge(proj_done.sem, proj_done.at(g, h))
                src = bank[g % 2]
                if g < 9:
                    if g % 3 == 0 and not (isinstance(h, int) and h == 0):
                        act.wait_ge(vecs.sem, vecs.at(("k_in", "q", "sg")[g // 3], h - 1))
                    dst = (raw_f, raw_q, raw_g)[g // 3][:, g % 3 * W3:(g % 3 + 1) * W3]
                    ins = act.copy(dst, src[:, 0:W3])
                elif g < 11:
                    ins = act.copy(v_tok[par][:, 4 * (g - 9):4 * (g - 8), :], src[:, :])
                else:
                    ins = act.copy(v_tok[par][0:S, TT, :], src[0:S, 0:P])
                ins.then_inc(proj_taken.sem, 1)

            def ln_f(h):
                act.wait_ge(vecs.sem, vecs.at("next_abs_f", h - 1))
                me.chain(act.activation(t0, t0, ACT.Exp, scale=-1.0))
                act.activation(t0, t0, ACT.Ln, bias=inv_h, scale=inv_h).then_inc(acts.sem, 1)

            def ln_q(h):
                act.wait_ge(vecs.sem, vecs.at("next_abs_q", h - 1))
                me.chain(act.activation(t2, t2, ACT.Exp, scale=-1.0))
                act.activation(t2, t2, ACT.Ln, bias=1.0).then_inc(acts.sem, 1)

            def head(i, par, nxt):
                h = 2 * i + par

                def v(name):
                    act.wait_ge(vecs.sem, vecs.at(name, h))

                def e(g):
                    if nxt:
                        evac(i + par, 1 - par, g)

                def level(w):
                    d = diff[LEVELS.index(w) % 2]
                    v(f"diff{w}")
                    act.activation(d, d, ACT.Exp).then_inc(acts.sem, 1)

                v("abs_g")
                me.chain(act.activation(sg_h, sg_h, ACT.Exp, scale=-1.0))
                act.activation(sg_h, sg_h, ACT.Ln, bias=1.0).then_inc(acts.sem, 1)
                v("k_in")
                act.activation(k_h, t1, ACT.Exp, scale=-1.0).then_inc(acts.sem, 1)
                v("q_in")
                act.activation(t2, t2, ACT.Exp).then_inc(acts.sem, 1)
                level(32)
                evac(i, par, 9)
                act.activation(f_smp, logf[:, T:N], ACT.Exp)
                act.activation(dec, cum[:, C - 1::C], ACT.Exp).then_inc(acts.sem, 1)
                act.activation(q_dec, cum, ACT.Exp).then_inc(acts.sem, 1)
                v("g_in")
                act.activation(sg_h, sg_h, ACT.Exp).then_inc(acts.sem, 1)
                level(16)
                evac(i, par, 10)
                level(8)
                evac(i, par, 11)
                e(0)
                level(4)
                e(1)
                v("o_smp")
                act.activation(sq_smp, o_smp, ACT.Square).then_inc(acts.sem, 1)
                v("diff_kd")
                act.activation(t1[:, 0:T], t1[:, 0:T], ACT.Exp).then_inc(acts.sem, 1)
                level(2)
                e(2)
                act.wait_ge(smp_done.sem, smp_done.at("mean_smp", h))
                act.activation(rs_smp, bank[6][:, 16:16 + S], ACT.Ln, bias=eps).then_inc(acts.sem, 1)
                level(1)
                e(3)
                e(4)
                for j in range(2):
                    act.wait_ge(uu_done.sem, uu_done.at(f"turn{j}", h))
                    act.copy(k_dec_tok[:, 4 * j:4 * j + 4, :], bank[4 + j][:, :]).then_inc(uu_taken_a, 1)
                e(5)
                if nxt:
                    ln_f(h + 1)
                else:
                    act.wait_ge(acts.sem, acts.at("exp1", h))
                    act.sem_inc(acts.sem, 1)
                e(6)
                e(7)
                for j in range(2):
                    act.wait_ge(ob_done.sem, ob_done.at(f"o{j}", h))
                    act.activation(o_sq[:, 512 * j:512 * j + 512], bank[6 + j][:, :], ACT.Square).then_inc(acts.sem, 1)
                if nxt:
                    ln_q(h + 1)
                else:
                    act.wait_ge(acts.sem, acts.at("sq1", h))
                    act.sem_inc(acts.sem, 1)
                e(8)
                for j in range(2):
                    act.wait_ge(lv_done.sem, lv_done.at(f"mean{j}", h))
                    act.activation(o_rs[:, 512 * j:512 * j + 512], bank[2 + j][:, :], ACT.Ln, bias=eps).then_inc(lv_taken_a, 1)
                act.wait_ge(lv_taken_a, 2 * h + 4)
                act.activation(o_rs[:, 0:T], o_rs[:, 0:T], ACT.Exp, scale=-0.5)
                act.activation(rs_smp, rs_smp, ACT.Exp, scale=-0.5).then_inc(acts.sem, 1)

            for g in range(9):
                evac(0, 0, g)
            ln_f(0)
            act.wait_ge(acts.sem, 1)
            act.sem_inc(acts.sem, 2)
            ln_q(0)
            act.wait_ge(acts.sem, 4)
            act.sem_inc(acts.sem, 1)
            PER = 2 * 3
            with act.Fori(0, LAST) as i:
                me.enter(i, PER)
                head(i, 0, True)
                head(i, 1, True)
                me.leave(PER, LAST)
            head(LAST, 0, True)
            head(LAST, 1, False)

            me.straight()

            def tile(i, par):
                t = 2 * i + par
                rows = S if isinstance(t, int) and t == TT else P
                act.wait_ge(tile_v.sem, tile_v.at("new1", t))
                me.chain(act.activation(h_sq[0:rows], h_new[par][0:rows], ACT.Square, accum_out=msq[0:rows, par:par + 1]))
                me.chain(act.activation(rstd[0:rows, par:par + 1], msq[0:rows, par:par + 1], ACT.Ln, bias=eps[0:rows], scale=1.0 / D))
                act.activation(rstd[0:rows, par:par + 1], rstd[0:rows, par:par + 1], ACT.Exp, scale=-0.5).then_inc(tile_a.sem, 1)
                for j in range(2):
                    act.wait_ge(h_turned, 2 * t + j + 1)
                    dst = h_t[:, 4 * j:4 * j + 4, t * P:t * P + rows] if isinstance(t, int) else h_t[:, 4 * j:4 * j + 4, bass.DynSlice(t * P, rows)]
                    act.sem_inc(act_go, 1)
                    act.copy(dst, bank[4 + 2 * par + j].rearrange("p (k n) -> p k n", n=P)[:, :, 0:rows]).then_inc(tile_a.sem, 1)
            with act.Fori(0, TT // 2) as i:
                me.enter(i, 4)
                tile(i, 0)
                tile(i, 1)
                me.leave(4, TT // 2)
            tile(TT // 2, 0)

            act.wait_ge(keys_v.sem, keys_v.at("abs"))
            me.chain(act.activation(a16[0:BH], a16[0:BH], ACT.Exp, scale=-1.0))
            act.activation(a16[0:BH], a16[0:BH], ACT.Ln, bias=1.0).then_inc(keys_a.sem, 1)

            act.wait_ge(raw_set, 3)
            me.straight()

            def slot(p, c):
                first = isinstance(p, int) and p == 0
                if c == 0 and not first:
                    act.wait_ge(prep_v.sem, prep_v.at("g", p - 1))
                    act.wait_ge(prep_a.sem, prep_a.at("v_cur", p - 1))
                    act.wait_ge(kv_stored, 80 * p)
                    act.wait_ge(q_stored, 16 * p)
                if c < 18:
                    t, rows, y = c % 9, P if c % 9 < TT else S, c // 9
                    act.wait_ge(pj_done, SLOTS * p + c + 1)
                    kq = raw[0:rows, t, y * 2 * (DH + 1):(y + 1) * 2 * (DH + 1)].rearrange("p (x d) -> p x d", x=2)[:, :, 0:DH]
                    act.copy(kq, bank[c % 2][0:rows, 0:P].rearrange("p (x d) -> p x d", x=2))
                    for x in range(2):
                        me.chain(act.activation(trash[0:rows], bank[c % 2][0:rows, x * DH:(x + 1) * DH], ACT.Square,
                                                accum_out=ssq[0:rows, 2 * ((TT + 1) * y + t) + x:2 * ((TT + 1) * y + t) + x + 1]))
                    act.copy(raw[0:rows, t, 4 * (DH + 1) + y * P:4 * (DH + 1) + (y + 1) * P], bank[c % 2][0:rows, P:2 * P]).then_inc(pj_taken, 1)
                    if t == TT:
                        part = slice(y * 2 * (TT + 1), (y + 1) * 2 * (TT + 1))
                        me.chain(act.activation(rs_kq[:, part], ssq[:, part], ACT.Ln, bias=eps, scale=1.0 / DH))
                        act.activation(rs_kq[:, part], rs_kq[:, part], ACT.Exp, scale=-0.5).then_inc(prep_a.sem, 1)
                else:
                    x, j = TURN[(c - 18) // 2], c % 2
                    if j == 0 and not first:
                        act.wait_ge(fp.sem, fp.at(f"qk{TT - 1 if x in (0, 2) else ITEMS - 1}", p - 1))
                    act.wait_ge(pj_done, SLOTS * p + c + 1)
                    act.copy(kq_t[0:DH + 1, x, 512 * j:512 * j + 512], bank[c % 2][0:DH + 1, :]).then_inc(pj_taken, 1)

            def gate_ln(q):
                act.wait_ge(prep_v.sem, prep_v.at("abs_g", q))
                me.chain(act.activation(g_next, g_next, ACT.Exp, scale=-1.0))
                act.activation(g_next, g_next, ACT.Ln, bias=1.0).then_inc(prep_a.sem, 1)

            def gate_sig(q):
                act.wait_ge(prep_v.sem, prep_v.at("g_in", q))
                act.activation(g_next, g_next, ACT.Exp).then_inc(prep_a.sem, 1)

            def v_copy(q):
                act.copy(v_cur, raw[:, :, 4 * (DH + 1):4 * (DH + 1) + P]).then_inc(prep_a.sem, 1)

            def exp(w, p, name, logits):
                x, i = w % 2, w % TT
                act.wait_ge(fv.sem, logits)
                if w >= 2:
                    act.wait_ge(fp.sem, fp.at(f"pt{w - 2}_{int((w - 2) % TT >= 4)}", p))
                me.did(act.activation(prob[x][:, 0:(i + 1) * P], psum[:, (2 + 2 * x) * 512:(2 + 2 * x) * 512 + (i + 1) * P],
                               ACT.Exp, bias=top[:, w:w + 1], accum_out=total[:, w:w + 1]))
                me.need(me.base + me.n)
                act.sem_inc(fa.sem, 1)

            for c in range(18):
                slot(0, c)
            slot(0, 18)
            slot(0, 19)
            slot(0, 20)
            slot(0, 21)
            gate_ln(0)
            gate_sig(0)
            v_copy(0)
            for c in range(22, 26):
                slot(0, c)
            act.wait_ge(pj_taken, 26)
            act.sem_inc(pj_taken, 2)
            exp(0, 0, "ex_next", fv.at("mx_next", -1))

            def pair(p, nxt):
                done = 0
                for w in range(ITEMS):
                    x, i = w % 2, w % TT
                    if i >= 4:
                        act.wait_ge(fp.sem, fp.at(f"pt{w}_1", p))
                        act.copy(prob_t[x][:, 512:(i + 1) * P], bank[7][:, 0:(i + 1) * P - 512]).then_inc(fa.sem, 1)
                    if w + 1 < ITEMS:
                        exp(w + 1, p, f"ex{w + 1}", fv.at(f"mx{w + 1}", p))
                    if nxt:
                        for _ in range(FILL[w] if w < len(FILL) else 0):
                            slot(p + 1, done)
                            done += 1
                        if w == ITEMS - 3:
                            gate_ln(p + 1)
                        if w == ITEMS - 2:
                            slot(p + 1, 18)
                            slot(p + 1, 19)
                        if w == ITEMS - 1:
                            slot(p + 1, 20)
                            slot(p + 1, 21)
                    if i == TT - 1:
                        g = w // TT
                        act.wait_ge(fv.sem, fv.at(f"df{g}", p))
                        act.activation(expd[g], expd[g], ACT.Exp).then_inc(dec_ready, 1)
                if nxt:
                    gate_sig(p + 1)
                    act.wait_ge(fp.sem, fp.at(f"pv{ITEMS - 1}", p))
                    act.sem_inc(act_go, 1)
                    v_copy(p + 1)
                    exp(0, p + 1, "ex_next", fv.at("mx_next", p))
                    for c in range(22, 26):
                        slot(p + 1, c)
                for j in range(2):
                    act.wait_ge(pj_done, SLOTS * (p + 1) + 26 * nxt + j + 1)
                    act.sem_inc(act_go, 1)
                    act.copy(o_cols(p, j), bank[j]).then_inc(pj_taken, 1)

            PER = 39 + ITEMS
            me.straight()
            with act.Fori(0, PAIRS - 1) as p:
                me.enter(p, PER)
                pair(p, True)
                me.leave(PER, PAIRS - 1)
            pair(PAIRS - 1, False)

        @block.vector
        def _(dve):
            me = Steps(dve, dve_steps)
            dve.sem_inc(uu_taken_v, 6)
            dve.wait_ge(consts_in, 48)
            dve.tensor_tensor(lb_e, lb_in, lb_in, ALU.subtract).then_inc(consts_v, 1)
            dve.wait_ge(lb_a, 1)
            me.chain(dve.reciprocal(lb_r, lb_e))
            me.chain(dve.tensor_tensor(lb_r, lb_e, lb_r, ALU.mult))
            me.chain(dve.tensor_tensor(lb_r, lb_r, lb_r, ALU.subtract))
            me.chain(dve.tensor_scalar(one_lb, lb_r, -1.0, 1.0, ALU.mult, ALU.add))
            me.chain(dve.reciprocal(inv_lb, one_lb))
            dve.wait_ge(built.sem, built.at("masks"))

            def x_out(t):
                rows = P if t < TT else S
                for j in range(2):
                    dve.wait_ge(x_turned, 2 * t + j + 1)
                    src = bank[2 + 2 * (t % 2) + j][:, :].rearrange("p (k n) -> p k n", n=P)[:, :, 0:rows]
                    dve.tensor_tensor(x_t[:, 4 * j:4 * j + 4, cols(t)], src,
                                      gain_a[:, 4 * j:4 * j + 4].unsqueeze(2).broadcast_to([P, 4, rows]),
                                      ALU.mult).then_inc(x_ready, 1)

            for t in range(TT + 1):
                rows = P if t < TT else S
                dve.wait_ge(x_rstd, t + 1)
                dve.tensor_scalar(x_in[t][0:rows], x_in[t][0:rows], rstd[0:rows, t:t + 1], None,
                                  ALU.mult).then_inc(x_scaled, 1)
                if t:
                    x_out(t - 1)
            x_out(TT)
            def col(a, h):
                return a[:, h:h + 1] if isinstance(h, int) else a[:, bass.DynSlice(h, 1)]

            def absolute(out, raw, g, h):
                dve.wait_ge(proj_taken.sem, proj_taken.at(g, h))
                dve.tensor_scalar(out.bitcast(I32), raw.bitcast(I32), 0x7FFFFFFF, None, ALU.bitwise_and).then_inc(vecs.sem, 1)

            def abs_f(h):
                dve.tensor_copy(inv_h, col(inv_lb, h))
                absolute(t0, raw_f, 2, h)

            def head(i, par, nxt=True):
                h = 2 * i + par
                me.straight() if isinstance(i, int) else None

                def a(name):
                    dve.wait_ge(acts.sem, acts.at(name, h))

                def split(w):
                    c = cum.rearrange("p (b w) -> p b w", w=2 * w)
                    d = diff[LEVELS.index(w) % 2].rearrange("p (b w) -> p b w", w=2 * w)
                    mid = c[:, :, w - 1:w].broadcast_to([P, T // (2 * w), w])
                    dve.tensor_tensor(d[:, :, w:2 * w], c[:, :, w:2 * w], mid, ALU.subtract)
                    dve.tensor_tensor(d[:, :, 0:w], mid, c[:, :, 0:w], ALU.subtract).then_inc(vecs.sem, 1)

                def factors(w):
                    a(f"exp{w}")
                    if w == LEVELS[0]:
                        dve.wait_ge(vecs.sem, vecs.at("q", h))
                    d = diff[LEVELS.index(w) % 2].rearrange("p (b w) -> p b w", w=2 * w)
                    f = fact[LEVELS.index(w) % 2].rearrange("p (b w) -> p b w", w=2 * w)
                    q = q_h[:, 0:T].rearrange("p (b w) -> p b w", w=2 * w)
                    k = k_h[:, 0:T].rearrange("p (b w) -> p b w", w=2 * w)
                    dve.tensor_tensor(f[:, :, w:2 * w], d[:, :, w:2 * w], q[:, :, w:2 * w], ALU.mult)
                    dve.tensor_tensor(f[:, :, 0:w], d[:, :, 0:w], k[:, :, 0:w], ALU.mult).then_inc(vecs.sem, 1)

                def merge(w):
                    l = LEVELS.index(w)
                    dve.wait_ge(lv_done.sem, lv_done.at(f"level{w}", h))
                    dve.wait_ge(lv_taken_v, 8 * h + 2 + l)
                    dve.sem_inc(merge_go, 1)
                    out = att.rearrange("p (t b w) -> p t b w", t=TT, w=2 * w)[:, :, :, w:2 * w]
                    mask = level_mask[:, l * C:(l + 1) * C].bitcast(I32).rearrange("p (b w) -> p b w", w=w)
                    dve.copy_predicated(out, mask.unsqueeze(1).broadcast_to([P, TT, C // w, w]),
                                        bank[2 + l % 2][:, :].rearrange("p (t b w) -> p t b w", t=TT, w=w))\
                       .then_inc(lv_taken_v, 1)

                dve.wait_ge(vecs.sem, vecs.at("o_all", h - 1))
                absolute(sg_h, raw_g, 8, h)
                dve.wait_ge(acts.sem, acts.at("next_ln_f", h - 1))
                dve.scalar_tensor_tensor(out=logf, in0=raw_f, scalar=0.0, in1=t0, op0=ALU.min,
                                         op1=ALU.subtract).then_inc(vecs.sem, 1)
                dve.scalar_tensor_tensor(out=t1, in0=raw_f, scalar=0.0, in1=t0, op0=ALU.max,
                                         op1=ALU.add).then_inc(vecs.sem, 1)
                dve.wait_ge(vecs.sem, vecs.at("logf", h))
                dve.tensor_tensor_scan(cum, chunk_keep, logf[:, 0:T], 0.0, ALU.mult, ALU.add)\
                   .then_inc(vecs.sem, 1)
                dve.wait_ge(acts.sem, acts.at("next_ln_q", h - 1))
                dve.scalar_tensor_tensor(out=t2, in0=raw_q, scalar=0.0, in1=t2, op0=ALU.min,
                                         op1=ALU.subtract).then_inc(vecs.sem, 1)
                dve.wait_ge(vecs.sem, vecs.at("cum", h))
                split(32)
                a("ln_g")
                dve.scalar_tensor_tensor(out=sg_h, in0=raw_g, scalar=0.0, in1=sg_h, op0=ALU.min,
                                         op1=ALU.subtract).then_inc(vecs.sem, 1)
                a("sig_q")
                dve.tensor_tensor(q_h, raw_q, t2, ALU.mult).then_inc(vecs.sem, 1)
                factors(32)
                split(16)
                dve.wait_ge(smp_done.sem, smp_done.at("k_smp", h))
                dve.tensor_copy(k_smp[0:S, :], bank[6][0:S, P:2 * P]).then_inc(vecs.sem, 1)
                for j in range(2):
                    dve.wait_ge(lv_done.sem, lv_done.at(f"diag{j}", h))
                    dve.tensor_tensor(att[:, 512 * j:512 * j + 512].rearrange("p (t q) -> p t q", q=P),
                                      bank[2 + j][:, :].rearrange("p (t q) -> p t q", q=P),
                                      ident.unsqueeze(1).broadcast_to([P, 4, P]), ALU.mult).then_inc(lv_taken_v, 1)
                factors(16)
                split(8)
                merge(32)
                dve.wait_ge(proj_taken.sem, proj_taken.at(11, h))
                dve.tensor_tensor(v_diag[0:S], v_tok[par][0:S, TT:TT + 1, :].broadcast_to([S, S, P]),
                                  ident[0:S, 0:S].unsqueeze(2).broadcast_to([S, S, P]), ALU.mult)\
                   .then_inc(vecs.sem, 1)
                a("sig_g")
                dve.scalar_tensor_tensor(out=sg_h, in0=raw_g, scalar=gain_o, in1=sg_h, op0=ALU.mult,
                                         op1=ALU.mult).then_inc(vecs.sem, 1)
                c3 = cum.rearrange("p (c s) -> p c s", s=C)
                dve.tensor_tensor(t1[:, 0:T].rearrange("p (c s) -> p c s", s=C),
                                  c3[:, :, C - 1:C].broadcast_to([P, NC, C]), c3, ALU.subtract)\
                   .then_inc(vecs.sem, 1)
                dve.tensor_tensor(q_dec, q_dec, q_h[:, 0:T], ALU.mult).then_inc(vecs.sem, 1)
                dve.wait_ge(state_loaded, 16 * (h + 1))
                me.chain(dve.tensor_tensor(s_smp, s_smp, f_smp.unsqueeze(2).broadcast_to([P, S, P]), ALU.mult))
                for j in range(2):
                    dve.wait_ge(uu_done.sem, uu_done.at(f"outer{j}", h))
                    dve.tensor_tensor(s_smp[:, 4 * j:4 * j + 4, :], s_smp[:, 4 * j:4 * j + 4, :],
                                      bank[4 + j][:, :].rearrange("p (b v) -> p b v", v=P), ALU.add)\
                       .then_inc(uu_taken_v, 1)
                dve.wait_ge(uu_taken_v, 6 * h + 8)
                dve.sem_inc(vecs.sem, 1)
                factors(8)
                split(4)
                merge(16)
                dve.wait_ge(smp_done.sem, smp_done.at("o_smp", h))
                dve.tensor_copy(o_smp, bank[6][:, 0:S]).then_inc(vecs.sem, 1)
                factors(4)
                split(2)
                merge(8)
                a("exp_kd")
                dve.tensor_tensor(k_dec, k_h[:, 0:T], t1[:, 0:T], ALU.mult).then_inc(vecs.sem, 1)
                factors(2)
                split(1)
                merge(4)
                factors(1)
                merge(2)
                merge(1)
                dve.wait_ge(lv_taken_v, 8 * h + 8)
                dve.sem_inc(vecs.sem, 1)
                abs_f(h + 1) if nxt else dve.sem_inc(vecs.sem, 1)
                dve.wait_ge(s_all_free, h + 1)
                for c in range(NC):
                    half, new = c // 8, bank[4 + c % 2][:, c % 8 // 2 * P:(c % 8 // 2 + 1) * P]
                    if c % 8 == 0:
                        dve.wait_ge(uu_done.sem, uu_done.at(f"upd{2 * half + 1}", h))
                    if c == 0:
                        ins = dve.tensor_copy(s_all[:, 0, :], new)
                    else:
                        ins = dve.scalar_tensor_tensor(out=s_all[:, c, :], in0=s_all[:, c - 1, :],
                                                       scalar=dec[:, c:c + 1], in1=new, op0=ALU.mult, op1=ALU.add)
                    if c % 8 >= 6:
                        ins.then_inc(uu_taken_v, 1)
                        dve.wait_ge(uu_taken_v, 6 * h + 8 + 2 * half + c % 8 - 5)
                    else:
                        me.chain(ins)
                dve.wait_ge(vecs.sem, vecs.at("next_abs_f", h))
                dve.sem_inc(vecs.sem, 1)
                absolute(t2, raw_q, 5, h + 1) if nxt else dve.sem_inc(vecs.sem, 1)
                a("dev")
                for j in range(2):
                    me.did(dve.tensor_tensor(o_rs[:, 512 * j:512 * j + 512], bank[6 + j][:, :],
                                             o_rs[:, 512 * j:512 * j + 512], ALU.mult))
                me.chain(dve.tensor_tensor(o_rs[:, T:N], o_smp, rs_smp, ALU.mult))
                dve.tensor_tensor(o_t[:, h, :], o_rs, sg_h, ALU.mult).then_inc(vecs.sem, 1)

            abs_f(0)
            dve.wait_ge(vecs.sem, 1)
            dve.sem_inc(vecs.sem, 1)
            absolute(t2, raw_q, 5, 0)
            dve.wait_ge(vecs.sem, 3)
            dve.sem_inc(vecs.sem, 1)
            PER = 2 * 16
            with dve.Fori(0, LAST) as i:
                me.enter(i, PER)
                head(i, 0)
                head(i, 1)
                me.leave(PER, LAST)
            head(LAST, 0)
            head(LAST, 1, False)

            dve.wait_ge(vecs.sem, vecs.at("o_all", AH - 1))

            def o_copy(t, par, used, copied):
                static = isinstance(t, int)
                rows = S if static and t == TT else P
                if not (static and t < 2):
                    dve.wait_ge(used, 2 * (t - 1))
                dve.sem_inc(dve_go, 1)
                dve.tensor_copy(o_tile[par][:, :, 0:rows], o_t[:, :, cols(t)] if static else o_t[:, :, bass.DynSlice(t * P, P)])\
                   .then_inc(copied, 1)

            def tile(i, par, nxt=True):
                t = 2 * i + par
                static = isinstance(t, int)
                rows = S if static and t == TT else P
                if nxt:
                    o_copy(t + 1, 1 - par, y_done, o_set)
                dve.wait_ge(res_loaded[par], 16 * (i + 1))
                if not (static and t < 2):
                    dve.wait_ge(h_stored[par], 16 * i)
                for j in range(2):
                    dve.wait_ge(y_done, 2 * t + j + 1)
                    dve.tensor_tensor(h_new[par][0:rows, 512 * j:512 * j + 512], res[par][0:rows, 512 * j:512 * j + 512],
                                      bank[2 * par + j][0:rows], ALU.add).then_inc(tile_v.sem, 1)
                dve.wait_ge(tile_a.sem, tile_a.at("rstd", t))
                if not (static and t < 2):
                    dve.wait_ge(h_turned, 2 * (t - 1))
                dve.tensor_scalar(h_sc[par][0:rows], h_new[par][0:rows], rstd[0:rows, par:par + 1], None, ALU.mult)\
                   .then_inc(tile_v.sem, 1)
            o_copy(0, 0, y_done, o_set)
            tile(0, 0)
            tile(0, 1)
            with dve.Fori(1, TT // 2 - 1) as i:
                tile(i, 0)
                tile(i, 1)
            tile(TT // 2 - 1, 0)
            tile(TT // 2 - 1, 1)
            tile(TT // 2, 0, False)

            dve.wait_ge(keys_in, 16 * 8)
            dve.wait_ge(masks_b.sem, masks_b.at("later"))
            dve.tensor_tensor(w_f, w_f, gain_kv.unsqueeze(2).broadcast_to([P, KT, BH]), ALU.mult).then_inc(keys_v.sem, 1)
            me.chain(dve.tensor_scalar(gain_kq[:, 2:4, :], gain_kq[:, 2:4, :], DH ** -0.5, None, ALU.mult))
            scale_w(dve, w_kv, gain_kv, 0, w_kv_loaded, w_kv_scaled)
            scale_w(dve, w_qg, gain_b, 0, w_qg_loaded, w_qg_scaled)
            dve.wait_ge(keys_p.sem, keys_p.at("z"))
            z = z16[0:BH]
            for n in range(3):
                me.did(dve.tensor_scalar(z[:, n * W3:(n + 1) * W3], bank[2 + n][0:BH, 0:W3], b_f[0:BH], None, ALU.add))
            me.need(me.base + me.n)
            dve.tensor_scalar(a16[0:BH].bitcast(I32), z.bitcast(I32), 0x7FFFFFFF, None, ALU.bitwise_and).then_inc(keys_v.sem, 1)
            dve.wait_ge(keys_a.sem, 1)
            dve.scalar_tensor_tensor(out=z, in0=z, scalar=0.0, in1=a16[0:BH], op0=ALU.min, op1=ALU.subtract).then_inc(keys_v.sem, 1)
            dve.wait_ge(keys_v.sem, keys_v.at("lf"))
            dve.tensor_tensor_scan(c16[0:BH], one16[0:BH], z[:, 0:T], 0.0, ALU.mult, ALU.add).then_inc(keys_v.sem, 1)
            dve.wait_ge(keys_p.sem, keys_p.at("turned"))
            me.did(dve.tensor_scalar(c_tok, bank[4][:, 0:TT * BH], -1.0, None, ALU.mult))
            me.did(dve.tensor_copy(lf_tok[0:S, TT * BH:(TT + 1) * BH], bank[5][0:S, TT * BH:(TT + 1) * BH]))
            dve.tensor_copy(lf_tok[:, 0:TT * BH], bank[5][:, 0:TT * BH]).then_inc(keys_v.sem, 1)
            dve.wait_ge(keys_p.sem, keys_p.at("suffix"))
            dve.wait_ge(lf_new_in, 16)
            me.chain(dve.tensor_copy(acc, lf_new.rearrange("p (b h) -> p b h", h=BH)))
            within = psum[:, 1024:2048].rearrange("p (b j h) -> p b j h", j=PAGES, h=BH)
            whole = psum[:, 3072:4096].rearrange("p (b j h) -> p b j h", j=PAGES, h=BH)
            for j in reversed(range(PAGES)):
                me.did(dve.tensor_tensor(bias[:, :, :, j], acc, within[:, :, j, :], ALU.add))
                me.chain(dve.scalar_tensor_tensor(out=acc, in0=whole[:, :, j, :], scalar=float(P), in1=acc, op0=ALU.mult, op1=ALU.add))
            dve.sem_inc(keys_v.sem, 1)

            kq5 = raw[:, :, 0:4 * (DH + 1)].rearrange("p t (x d) -> p t x d", x=4)
            g_raw = raw[:, :, 4 * (DH + 1) + P:RAW]

            def norm_kq(q, y):
                kq = kq5[:, :, 2 * y:2 * y + 2, 0:DH]
                if y == 0:
                    c2 = c_tok.rearrange("p (t h) -> p t h", h=BH)
                    if not (isinstance(q, int) and q == 0):
                        dve.wait_ge(prep_v.sem, prep_v.at("g", q - 1))
                        dve.sem_inc(dve_go, 1)
                    me.did(dve.tensor_copy(kq5[:, 0:TT, 0:2, DH], c2[:, :, 2 * q:2 * q + 2] if isinstance(q, int) else
                                           c2[:, :, bass.DynSlice(2 * q, 2)]))
                dve.wait_ge(prep_a.sem, prep_a.at(("rs_k", "rs_q")[y], q))
                rs = rs_kq[:, y * 2 * (TT + 1):(y + 1) * 2 * (TT + 1)].rearrange("p (t x) -> p t x", x=2)
                me.chain(dve.tensor_tensor(kq, kq, rs.unsqueeze(3).broadcast_to([P, TT + 1, 2, DH]), ALU.mult))
                dve.tensor_tensor(kq, kq, gain_kq[:, 2 * y:2 * y + 2, :].unsqueeze(1).broadcast_to([P, TT + 1, 2, DH]), ALU.mult)\
                   .then_inc(prep_v.sem, 1)

            def gate_abs(q):
                dve.wait_ge(pj_taken, SLOTS * q + 18)
                dve.tensor_scalar(g_next.bitcast(I32), g_raw.bitcast(I32), 0x7FFFFFFF, None, ALU.bitwise_and).then_inc(prep_v.sem, 1)

            def gate_in(q):
                dve.wait_ge(prep_a.sem, prep_a.at("ln_g", q))
                dve.scalar_tensor_tensor(out=g_next, in0=g_raw, scalar=0.0, in1=g_next, op0=ALU.min, op1=ALU.subtract).then_inc(prep_v.sem, 1)

            def gate(q):
                dve.wait_ge(prep_a.sem, prep_a.at("sig_g", q))
                dve.tensor_tensor(g_cur, g_next, g_raw, ALU.mult).then_inc(prep_v.sem, 1)

            def masked_max(w, logits):
                x, i = w % 2, w % TT
                dve.wait_ge(fp.sem, logits)
                diag = psum[:, (2 + 2 * x) * 512 + i * P:(2 + 2 * x) * 512 + (i + 1) * P]
                me.chain(dve.tensor_tensor(diag, diag, causal, ALU.add))
                dve.tensor_reduce(top[:, w:w + 1], psum[:, (2 + 2 * x) * 512:(2 + 2 * x) * 512 + (i + 1) * P], AX.X,
                                  ALU.max, negate=True).then_inc(fv.sem, 1)

            def sum_pages(p, g, b):
                dve.wait_ge(v_mult, S * p + HALF * g + b + 2)
                dve.sem_inc(dve_go, 1)
                n = PAGES
                while n > 1:
                    n //= 2
                    low = v_ring[:, b:b + 2, 0:n, :]
                    me.did(dve.tensor_tensor(low, low, v_ring[:, b:b + 2, n:2 * n, :], ALU.add))
                    me.need(me.base + me.n)

            def add_new(p, g):
                e = expd[g].rearrange("p (b x j) -> p b x j", x=2, j=9)
                v = v_new[:, HALF * g:HALF * (g + 1), :]
                v4 = v.rearrange("p b (x d) -> p b x d", x=2)
                dve.wait_ge(v_new_loaded, 16 * (p + 1))
                dve.sem_inc(dve_go, 1)
                me.chain(dve.tensor_tensor(v4, v4, e[0:1, :, :, PAGES].unsqueeze(3).broadcast_to([1, HALF, 2, DH]), ALU.mult))
                first = v_ring[0:1, :, 0, :]
                dve.tensor_tensor(first, first, v, ALU.add).then_inc(red_ready, 1)

            def smp_out(p, g):
                dve.wait_ge(dec_done, 2 * p + g + 1)
                me.chain(dve.tensor_reduce(den, bank[7][:, 16:16 + 72].rearrange("p (n j) -> p n j", j=9), AX.X, ALU.add))
                me.chain(dve.reciprocal(den, den))
                me.chain(dve.scalar_tensor_tensor(out=o_two, in0=bank[7][:, P:P + 8], scalar=1.0, in1=den, op0=ALU.mult, op1=ALU.mult))
                o2 = o_two.rearrange("p (b x) -> p b x", x=2)
                for x in range(2):
                    rows = slice(x * DH, (x + 1) * DH)
                    lo = T + HALF * g
                    dst = o_t[rows, p, lo:lo + HALF] if isinstance(p, int) else o_t[rows, bass.DynSlice(p, 1), lo:lo + HALF].rearrange("p a n -> p (a n)")
                    ins = dve.tensor_tensor(dst, o2[rows, :, x], g_smp[rows, HALF * g:HALF * g + HALF], ALU.mult)
                    if x == 0:
                        me.did(ins)
                ins.then_inc(od_done, 1)

            def pair(p, nxt, nxt2):
                static = isinstance(p, int)

                def a(name):
                    dve.wait_ge(fa.sem, fa.at(name, p))

                def pe(name, q=None):
                    dve.wait_ge(fp.sem, fp.at(name, p if q is None else q))

                for w in range(ITEMS):
                    x, i, g = w % 2, w % TT, w // TT
                    if w == 4:
                        if not (static and p == 0):
                            dve.wait_ge(od_done, 2 * p)
                        pe("g_smp")
                        dve.tensor_copy(g_smp, bank[7][:, 0:S]).then_inc(fv.sem, 1)
                    pe(f"pt{w}_0")
                    width = min(i + 1, 4) * P
                    dve.tensor_copy(prob_t[x][:, 0:width], bank[6][:, 0:width]).then_inc(fv.sem, 1)
                    if w + 1 < ITEMS:
                        masked_max(w + 1, fp.at(f"qk{w + 1}", p))
                    lg = lgt[g].rearrange("p (b x j) -> p b x j", x=2, j=9)
                    if 1 <= i <= HALF:
                        b = i - 1
                        n = HALF * g + b
                        if w == 1:
                            dve.wait_ge(new_loaded, 32 * (p + 1))
                        dve.wait_ge(k_loaded[b], 128 * (2 * p + g + 1))
                        if w > 1:
                            me.need(me_last[0])
                        k = k_ring[:, b]
                        dve.tensor_tensor(prod.rearrange("p (j n) -> p j n", n=P), k, q_all[:, n:n + 1, :].broadcast_to([P, PAGES, P]), ALU.mult).then_inc(fv.sem, 1)
                        dve.wait_ge(fv.sem, fv.at(f"pr{n}", p))
                        me_last[0] = me.did(dve.tensor_reduce(lg[:, b, :, 0:PAGES].rearrange("p x j -> p j x"),
                                                 prod.rearrange("p (j x d) -> p j x d", x=2, d=DH), AX.X, ALU.add))
                    if i == HALF + 1:
                        me.need(me_last[0])
                        lo = slice(HALF * g, HALF * (g + 1))
                        me.did(dve.tensor_tensor(lg[:, :, :, 0:PAGES], lg[:, :, :, 0:PAGES],
                                                 bias[:, lo, 2 * p:2 * p + 2, :] if static else bias[:, lo, bass.DynSlice(2 * p, 2), :], ALU.add))
                        new = prod[0:1, 0:HALF * P]
                        me.chain(dve.tensor_tensor(new.rearrange("p (b n) -> p b n", n=P), k_new[:, lo, :], q_all[0:1, lo, :], ALU.mult))
                        me.chain(dve.tensor_reduce(lg[0:1, :, :, PAGES], new.rearrange("p (b x d) -> p b x d", x=2, d=DH), AX.X, ALU.add))
                        dve.tensor_reduce(top8[g], lg, AX.X, ALU.max).then_inc(fv.sem, 1)
                    if i == TT - 1:
                        dve.wait_ge(top_all, 2 * p + g + 1)
                        if not (static and p == 0):
                            dve.wait_ge(dec_done, 2 * p + g - 1)
                        dve.tensor_tensor(expd[g].rearrange("p (n j) -> p n j", j=9), lgt[g].rearrange("p (n j) -> p n j", j=9),
                                          m_all[g].unsqueeze(2).broadcast_to([P, 8, 9]), ALU.subtract).then_inc(fv.sem, 1)
                    if w == 13 and nxt:
                        gate_abs(p + 1)
                    if w == TT + 3:
                        smp_out(p, 0)
                    if w == 3 and not (static and p == 0):
                        smp_out(p - 1, 1)
                    pe(f"pv{w}")
                    me.chain(dve.reciprocal(r_total[:, w:w + 1], total[:, w:w + 1]))
                    head_cols = slice(g * DH, (g + 1) * DH)
                    dve.scalar_tensor_tensor(out=og[:, i, head_cols], in0=bank[2 + 2 * x][:, 0:DH], scalar=r_total[:, w:w + 1],
                                             in1=g_cur[:, i, head_cols], op0=ALU.mult, op1=ALU.mult).then_inc(fv.sem, 1)
                    if w in (1, 2) and not (static and p == 0):
                        sum_pages(p - 1, 1, 2 * w - 2)
                        if w == 2:
                            add_new(p - 1, 1)
                    if w in (TT + 1, TT + 2):
                        sum_pages(p, 0, 2 * (w - TT) - 2)
                    if w == TT + 2:
                        add_new(p, 0)
                    if w == 5 and nxt:
                        scale_w(dve, w_qg, gain_b, p + 1, w_qg_loaded, w_qg_scaled)
                    if w == 7 and nxt:
                        norm_kq(p + 1, 0)
                    if w == 11 and nxt2:
                        scale_w(dve, w_kv, gain_kv, p + 2, w_kv_loaded, w_kv_scaled)
                    if w == 13 and nxt:
                        norm_kq(p + 1, 1)
                    if w == 14 and nxt:
                        gate_in(p + 1)
                if nxt:
                    masked_max(0, fp.at("qk_next", p))
                    gate(p + 1)

            me_last = [0]
            me.straight()
            norm_kq(0, 0)
            gate_abs(0)
            norm_kq(0, 1)
            gate_in(0)
            gate(0)
            scale_w(dve, w_kv, gain_kv, 1, w_kv_loaded, w_kv_scaled)
            masked_max(0, fp.at("qk_next", -1))
            pair(0, True, True)
            me.straight()
            PER = 71
            with dve.Fori(1, PAIRS - 2) as p:
                me.enter(p - 1, PER)
                pair(p, True, True)
                me.leave(PER, PAIRS - 3)
            pair(PAIRS - 2, True, False)
            me.straight()
            pair(PAIRS - 1, False, False)
            me.straight()

            dve.wait_ge(pj_taken, OUT_TAKEN)

            def tile_b(i, par, nxt=True):
                t = 2 * i + par
                rows = S if isinstance(t, int) and t == TT else P
                if nxt:
                    o_copy(t + 1, 1 - par, yb_done, ob_set)
                dve.wait_ge(resb_loaded[par], 16 * (i + 1))
                for j in range(2):
                    dve.wait_ge(yb_done, 2 * t + j + 1)
                    dve.tensor_tensor(res[par][0:rows, 512 * j:512 * j + 512], res[par][0:rows, 512 * j:512 * j + 512],
                                      bank[2 * par + j][0:rows], ALU.add).then_inc(yb_v.sem, 1)
            o_copy(0, 0, yb_done, ob_set)
            tile_b(0, 0)
            for b in range(0, HALF, 2):
                sum_pages(PAIRS - 1, 1, b)
            add_new(PAIRS - 1, 1)
            tile_b(0, 1)
            smp_out(PAIRS - 1, 1)
            with dve.Fori(1, TT // 2 - 1) as i:
                tile_b(i, 0)
                tile_b(i, 1)
            tile_b(TT // 2 - 1, 0)
            dve.wait_ge(od_done, 2 * PAIRS)
            tile_b(TT // 2 - 1, 1)
            tile_b(TT // 2, 0, False)

        @block.tensor
        def _(pe):
            pe.wait_ge(built.sem, built.at("masks"))
            for t in range(TT + 1):
                rows = P if t < TT else S
                pe.wait_ge(x_scaled, t + 1)
                if t >= 2:
                    pe.wait_ge(x_ready, 2 * (t - 1))
                for k in range(KT):
                    ins = pe.transpose(bank[2 + 2 * (t % 2) + k // 4][:, k % 4 * P:k % 4 * P + rows],
                                       x_in[t][0:rows, k * P:(k + 1) * P], ident[0:rows, 0:rows])
                    if k % 4 == 3:
                        ins.then_inc(x_turned, 1)
            pe.wait_ge(x_ready, 2 * (TT + 1))

            def proj(i, par, g):
                h = 2 * i + par
                first = isinstance(h, int) and h == 0
                if g == 0:
                    pe.wait_ge(w_a_loaded[par], 64 * (i + 1))
                if not (first and g < 2):
                    pe.wait_ge(proj_taken.sem, 12 * h + g - 1)
                dst = bank[g % 2]
                if g < 9:
                    for k in range(KT):
                        ins = pe.matmul(dst[:, 0:W3], w_a[:, par, k, g // 3, :], x_t[:, k, g % 3 * W3:(g % 3 + 1) * W3],
                                        start=(k == 0), stop=(k == KT - 1))
                else:
                    for t in range(4 * (g - 9), 4 * (g - 8)) if g < 11 else (TT,):
                        rows = P if t < TT else S
                        for k in range(KT):
                            ins = pe.matmul(dst[0:rows, t % 4 * P:(t % 4 + 1) * P], x_t[:, k, cols(t)],
                                            w_a[:, par, k, 3, :], start=(k == 0), stop=(k == KT - 1))
                ins.then_inc(proj_done.sem, 1)

            def head(i, par, nxt):
                h = 2 * i + par

                def v(name, hh=None):
                    pe.wait_ge(vecs.sem, vecs.at(name, h if hh is None else hh))

                def group(g):
                    if nxt:
                        proj(i + par, 1 - par, g)

                def level(w):
                    l = LEVELS.index(w)
                    v(f"fact{w}")
                    pe.wait_ge(lv_taken_v, 8 * h + l + 1)
                    f = fact[l % 2]
                    for t in range(TT):
                        q = f[:, t * P:(t + 1) * P].rearrange("p (b w) -> p b w", w=2 * w)[:, :, w:2 * w]
                        ins = pe.matmul(bank[2 + l % 2][:, t * C:(t + 1) * C], f[:, t * P:(t + 1) * P], q,
                                        start=True, stop=True)
                    ins.then_inc(lv_done.sem, 1)

                proj(i, par, 9)
                proj(i, par, 10)
                pe.wait_ge(acts.sem, acts.at("k", h))
                v("o_all", h - 1)
                pe.transpose(bank[6][0:S, P:2 * P], k_h[:, T:N], ident).then_inc(smp_done.sem, 1)
                v("q")
                for j in range(2):
                    pe.wait_ge(lv_taken_a, 2 * h + 1 + j)
                    for t in range(4 * j, 4 * j + 4):
                        ins = pe.matmul(bank[2 + j][:, t % 4 * P:(t % 4 + 1) * P], k_h[:, cols(t)], q_h[:, cols(t)],
                                        start=True, stop=True)
                    ins.then_inc(lv_done.sem, 1)
                proj(i, par, 11)
                level(32)
                group(0)
                v("v_diag")
                for j in range(2):
                    pe.wait_ge(uu_taken_v, 6 * h + 5 + j)
                    pe.matmul(bank[4 + j][:, :], k_smp[0:S, :], v_diag[0:S, 4 * j:4 * j + 4, :],
                              start=True, stop=True).then_inc(uu_done.sem, 1)
                level(16)
                group(1)
                v("s_smp")
                for b in range(S):
                    ins = pe.matmul(bank[6][:, b:b + 1], s_smp[:, b, :], q_h[:, T + b:T + b + 1],
                                    start=True, stop=True)
                ins.then_inc(smp_done.sem, 1)
                level(8)
                group(2)
                level(4)
                pe.wait_ge(acts.sem, acts.at("sq_smp", h))
                pe.matmul(bank[6][:, 16:16 + S], ones_mean, sq_smp, start=True, stop=True)\
                  .then_inc(smp_done.sem, 1)
                group(3)
                level(2)
                for j in range(2):
                    pe.wait_ge(uu_taken_v, 6 * h + 7 + j)
                    for t in range(4 * j, 4 * j + 4):
                        ins = pe.transpose(bank[4 + j][:, t % 4 * P:(t % 4 + 1) * P], k_dec[:, cols(t)], ident)
                    ins.then_inc(uu_done.sem, 1)
                group(4)
                level(1)
                group(5)
                for j in range(4):
                    if j < 2:
                        pe.wait_ge(uu_taken_a, 2 * h + 1 + j)
                        if j == 0:
                            pe.wait_ge(uu_taken_a, 2 * h + 2)
                    else:
                        pe.wait_ge(uu_taken_v, 6 * h + 7 + j)
                    for n in range(4):
                        c = 8 * (j // 2) + 2 * n + j % 2
                        rows = slice(c % 2 * C, (c % 2 + 1) * C)
                        ins = pe.matmul(bank[4 + j % 2][:, n * P:(n + 1) * P], k_dec_tok[rows, c // 2, :],
                                        v_tok[par][rows, c // 2, :], start=True, stop=True)
                    ins.then_inc(uu_done.sem, 1)
                    if j == 1:
                        group(6)
                group(7)
                v("s_all")
                pe.wait_ge(acts.sem, acts.at("ln_smp", h))
                for t in range(TT):
                    dst = bank[6 + t // 4][:, t % 4 * P:(t % 4 + 1) * P]
                    pe.matmul(dst, v_tok[par][:, t, :], att[:, cols(t)], start=True, stop=False, skip_group_check=True)
                    for c in (2 * t, 2 * t + 1):
                        if c:
                            ins = pe.matmul(dst[:, c % 2 * C:(c % 2 + 1) * C], s_all[:, c - 1, :],
                                            q_dec[:, c * C:(c + 1) * C], start=False, stop=(c % 2 == 1),
                                            skip_group_check=True)
                    if t % 4 == 3:
                        ins.then_inc(ob_done.sem, 1)
                group(8)
                for j in range(2):
                    pe.wait_ge(acts.sem, acts.at(f"sq{j}", h))
                    pe.wait_ge(lv_taken_v, 8 * h + 7 + j)
                    pe.matmul(bank[2 + j][:, :], ones_mean, o_sq[:, 512 * j:512 * j + 512], start=True,
                              stop=True).then_inc(lv_done.sem, 1)

            for g in range(9):
                proj(0, 0, g)
            with pe.Fori(0, LAST) as i:
                head(i, 0, True)
                head(i, 1, True)
            head(LAST, 0, True)
            head(LAST, 1, False)

            pe.wait_ge(w_o_loaded, 16)
            pe.wait_ge(vecs.sem, vecs.at("o_all", AH - 1))

            def y_tile(i, par, copied, done, high=None):
                t = 2 * i + par
                static = isinstance(t, int)
                rows = S if static and t == TT else P
                pe.wait_ge(copied, t + 1)
                for j in range(2):
                    for h in range(AH):
                        ins = pe.matmul(bank[2 * par + j][0:rows, :], o_tile[par][:, h, 0:rows],
                                        (w_o[:, h] if high is None or h < AH // 2 else high[:, h - AH // 2])[:, 512 * j:512 * j + 512],
                                        start=(h == 0), stop=(h == AH - 1))
                    ins.then_inc(done, 1)

            def turn(i, par):
                t = 2 * i + par
                static = isinstance(t, int)
                rows = S if static and t == TT else P
                pe.wait_ge(tile_v.sem, tile_v.at("scaled", t))
                if not (static and t < 2):
                    pe.wait_ge(tile_a.sem, tile_a.at("h_t1", t) - 2 * len(tile_a.names))
                for k in range(KT):
                    ins = pe.transpose(bank[4 + 2 * par + k // 4][:, k % 4 * P:k % 4 * P + rows],
                                       h_sc[par][0:rows, k * P:(k + 1) * P], ident[0:rows, 0:rows])
                    if k % 4 == 3:
                        ins.then_inc(h_turned, 1)

            y_tile(0, 0, o_set, y_done)
            y_tile(0, 1, o_set, y_done)
            turn(0, 0)
            with pe.Fori(1, TT // 2) as i:
                y_tile(i, 0, o_set, y_done)
                turn(i - 1, 1)
                y_tile(i, 1, o_set, y_done)
                turn(i, 0)
            y_tile(TT // 2, 0, o_set, y_done)
            turn(TT // 2 - 1, 1)
            turn(TT // 2, 0)

            pe.wait_ge(tile_a.sem, tile_a.at("h_t1", TT))
            pe.wait_ge(keys_v.sem, keys_v.at("w_f"))
            for n in range(3):
                for k in range(KT):
                    ins = pe.matmul(bank[2 + n][0:BH, 0:W3], w_f[:, k, :], h_t[:, k, n * W3:(n + 1) * W3],
                                    start=(k == 0), stop=(k == KT - 1))
            ins.then_inc(keys_p.sem, 1)
            def slot(p, c):
                t, rows = c % 9, P if c % 9 < TT else S
                if c in (0, 9):
                    pe.wait_ge((w_kv_scaled, w_qg_scaled)[c // 9], p + 1)
                if c in (18, 20):
                    pe.wait_ge(prep_v.sem, prep_v.at("k" if c == 18 else "q", p))
                if not (isinstance(p, int) and p == 0 and c < 2):
                    pe.wait_ge(pj_taken, SLOTS * p + c - 1)
                if c < 18:
                    w = (w_kv, w_qg)[c // 9]
                    for k in range(KT):
                        ins = pe.matmul(bank[c % 2][0:rows, 0:2 * P], h_t[:, k, cols(t)], w[:, k, :, :],
                                        start=(k == 0), stop=(k == KT - 1))
                else:
                    x, j = TURN[(c - 18) // 2], c % 2
                    for t in range(4 * j, 4 * j + 4):
                        ins = pe.transpose(bank[c % 2][0:DH + 1, t % 4 * P:(t % 4 + 1) * P],
                                           raw[:, t, x * (DH + 1):(x + 1) * (DH + 1)], ident)
                ins.then_inc(pj_done, 1)

            def logits(w):
                hd, i, x = w // TT, w % TT, w % 2
                for j in range(0, i + 1, 4):
                    n = min(4, i + 1 - j)
                    ins = pe.matmul(bank[2 + 2 * x + j // 4][:, 0:n * P], kq_t[0:DH + 1, 2 + hd, cols(i)],
                                    kq_t[0:DH + 1, hd, j * P:(j + n) * P], start=True, stop=True)
                ins.then_inc(fp.sem, 1)

            def decode(p, g):
                pe.wait_ge(red_ready, 2 * p + g + 1)
                pe.wait_ge(fa.sem, fa.at(f"ptc{TT * g + TT - 1}", p))
                pe.matmul(bank[7][:, 16:16 + 72], ones_mean, expd[g], start=True, stop=True, skip_group_check=True)
                for b in range(HALF):
                    ins = pe.matmul(bank[7][:, P + 2 * b:P + 2 * b + 2], v_ring[:, b, 0, :], ones_mean[:, 0:2], start=True,
                                    stop=True, skip_group_check=True)
                ins.then_inc(dec_done, 1)

            def pair(p, nxt):
                static = isinstance(p, int)

                def v(name, q=None):
                    pe.wait_ge(fv.sem, fv.at(name, p if q is None else q))

                def a(name):
                    pe.wait_ge(fa.sem, fa.at(name, p))

                done = 0
                for w in range(ITEMS):
                    hd, i, x = w // TT, w % TT, w % 2
                    if w == 0:
                        pe.wait_ge(fa.sem, fa.at("ex_next", p - 1))
                    else:
                        a(f"ex{w}")
                    for j in range(0, i + 1, 4):
                        if j == 0:
                            v(f"ptc{w - 1}") if w else None
                        elif w == 4:
                            v("g_smp")
                        elif w == TT + 4:
                            pe.wait_ge(od_done, 2 * p + 1)
                        else:
                            a(f"ptc{w - 1}")
                        for n in range(j, min(j + 4, i + 1)):
                            ins = pe.transpose(bank[6 + j // 4][:, n % 4 * P:(n % 4 + 1) * P], prob[x][:, n * P:(n + 1) * P], ident)
                        ins.then_inc(fp.sem, 1)
                    if w + 1 < ITEMS:
                        if w >= 1:
                            v(f"nm{w - 1}")
                        elif not (static and p == 0):
                            v(f"nm{ITEMS - 1}", p - 1)
                        if w == 0:
                            pe.wait_ge(pj_taken, SLOTS * p + 22)
                        if w == TT - 1:
                            pe.wait_ge(pj_taken, SLOTS * p + 26)
                        logits(w + 1)
                    if nxt:
                        for _ in range(FILL[w] if w < len(FILL) else 0):
                            slot(p + 1, done)
                            done += 1
                        if w >= ITEMS - 2:
                            slot(p + 1, 18 + 2 * (w - ITEMS + 2))
                            slot(p + 1, 19 + 2 * (w - ITEMS + 2))
                    if w == 3 and not (static and p == 0):
                        decode(p - 1, 1)
                    if w == TT + 3:
                        decode(p, 0)
                    v(f"ptc{w}")
                    if w == 0:
                        pe.wait_ge(prep_a.sem, prep_a.at("v_cur", p))
                    if i >= 4:
                        a(f"ptc{w}")
                    for n in range(i + 1):
                        ins = pe.matmul(bank[2 + 2 * x][:, 0:DH], prob_t[x][:, n * P:(n + 1) * P],
                                        v_cur[:, n, hd * DH:(hd + 1) * DH], start=(n == 0), stop=(n == i))
                    ins.then_inc(fp.sem, 1)
                    if w == 3:
                        pe.wait_ge(prep_v.sem, prep_v.at("g", p))
                        if not (static and p == 0):
                            pe.wait_ge(od_done, 2 * p)
                        pe.sem_inc(pe_go, 1)
                        pe.transpose(bank[7][:, 0:S], g_cur[0:S, TT, :], ident[0:S, 0:S]).then_inc(fp.sem, 1)
                if nxt:
                    pe.wait_ge(pj_taken, SLOTS * (p + 1) + 22)
                    v(f"nm{ITEMS - 2}")
                    logits(0)
                    for c in range(22, 26):
                        slot(p + 1, c)
                v(f"nm{ITEMS - 1}")
                for j in range(2):
                    pe.wait_ge(pj_taken, SLOTS * (p + 1) + 26 * nxt + j - 1)
                    for t in range(4 * j, 4 * j + 4):
                        ins = pe.transpose(bank[j][:, t % 4 * P:(t % 4 + 1) * P], og[:, t, :], ident)
                    ins.then_inc(pj_done, 1)

            for c in range(9):
                slot(0, c)
            pe.wait_ge(keys_v.sem, keys_v.at("c"))
            for t in range(TT + 1):
                rows = P if t < TT else S
                ins = pe.transpose(bank[5][0:rows, t * BH:(t + 1) * BH], z16[0:BH, cols(t)], ident[0:BH, 0:BH])
                if t < TT:
                    ins = pe.transpose(bank[4][:, t * BH:(t + 1) * BH], c16[0:BH, cols(t)], ident[0:BH, 0:BH])
            ins.then_inc(keys_p.sem, 1)
            for c in range(9, 11):
                slot(0, c)
            pe.wait_ge(lf_in, 16 * S * PAGES)
            pe.wait_ge(masks_b.sem, masks_b.at("later"))
            for j in range(2):
                pe.matmul(bank[2 + j], later, lf_pages[:, 512 * j:512 * j + 512], start=True, stop=True)
                ins = pe.matmul(bank[6 + j], ones_mean, lf_pages[:, 512 * j:512 * j + 512], start=True, stop=True)
            ins.then_inc(keys_p.sem, 1)
            for c in range(11, 26):
                slot(0, c)
            pe.wait_ge(keys_v.sem, keys_v.at("done"))
            pe.wait_ge(pj_done, 26)
            pe.sem_inc(pj_done, 2)
            pe.wait_ge(pj_taken, 22)
            logits(0)

            pair(0, True)
            with pe.Fori(1, PAIRS - 1) as p:
                pair(p, True)
            pair(PAIRS - 1, False)

            pe.wait_ge(w_ob_loaded, 32)
            pe.wait_ge(pj_taken, OUT_TAKEN)

            y_tile(0, 0, ob_set, yb_done, w_o_high)
            y_tile(0, 1, ob_set, yb_done, w_o_high)
            decode(PAIRS - 1, 1)
            with pe.Fori(1, TT // 2) as i:
                y_tile(i, 0, ob_set, yb_done, w_o_high)
                y_tile(i, 1, ob_set, yb_done, w_o_high)
            y_tile(TT // 2, 0, ob_set, yb_done, w_o_high)


_OUTS = [("y_prompt", (1, T, D)), ("y_sample", (S, 1, D)), ("state_prompt", (1, 1, AH, P, P)),
         ("state_sample", (1, S, AH, P, P)), ("k_prompt", (1, T, BH, DH)), ("k_sample", (S, 1, BH, DH)),
         ("v_prompt", (1, T, BH, DH)), ("v_sample", (S, 1, BH, DH)), ("logf_prompt", (1, T, BH)),
         ("logf_sample", (S, 1, BH))]


def kernel(**inputs):
    import numpy as np
    import concourse.bacc as bacc
    from concourse.bass_utils import run_bass_kernel_spmd

    nc = bacc.Bacc("TRN2", target_bir_lowering=False, num_devices=1)
    arrays, io = {}, {}
    for name, a in inputs.items():
        a = np.ascontiguousarray(a)
        arrays[f"in_{name}"] = a
        io[name] = nc.dram_tensor(f"in_{name}", a.shape, mybir.dt.from_np(a.dtype), kind="ExternalInput").ap()
    for name, shape in _OUTS:
        io[name] = nc.dram_tensor(f"out_{name}", shape, F32, kind="ExternalOutput").ap()
    build(nc, io)
    r = run_bass_kernel_spmd(nc, [arrays], core_ids=[0])
    return tuple(r.results[0][f"out_{name}"] for name, _ in _OUTS)
```
